# Optimizing a Trainium2 kernel written in Bass

```python
import math
import jax, jax.numpy as jnp
from jax import lax
import numpy as np

D_MODEL = 1024
BATCH = 1
SEQ = 256
DEPTH = 2
DEC_BATCH = 8
DEC_SEQ = 8
PAST_LEN = 2048
PAGE_SIZE = 128

N_BRANCH = 4
BRANCH_W = D_MODEL // 2
CONV_W = 4
CHUNK = 64
D_FF = 2816
EPS = 1e-6
ROPE_BASE = 10000.0

MB_HEADDIM = 64
MB_HEADS = BRANCH_W // MB_HEADDIM
MB_GROUPS = 2
MB_STATE = 64
MB_CONV_DIM = BRANCH_W + 2 * MB_GROUPS * MB_STATE

HG_DK = 128
HG_HEADS = BRANCH_W // HG_DK
HG_DV = BRANCH_W // HG_HEADS

RET_HEADS = 4
RET_DK = 64
RET_DV = BRANCH_W // RET_HEADS

GDN_HEADS = 4
GDN_DK = 128
GDN_DV = BRANCH_W // GDN_HEADS
GDN_CONV_DIM = 2 * GDN_HEADS * GDN_DK + GDN_HEADS * GDN_DV

IN_SPLITS = (
    BRANCH_W, MB_CONV_DIM, MB_HEADS,
    HG_HEADS * HG_DK, HG_HEADS * HG_DK, BRANCH_W, BRANCH_W,
    RET_HEADS * RET_DK, RET_HEADS * RET_DK, BRANCH_W, BRANCH_W,
    GDN_CONV_DIM, BRANCH_W, GDN_HEADS, GDN_HEADS,
    N_BRANCH * D_MODEL,
)
D_IN = sum(IN_SPLITS)
IN_OFFSETS = tuple(int(v) for v in np.cumsum(IN_SPLITS)[:-1])

kernel_name = 'hybrid_ssd_hgrn2_retnet_gdn_step'

def rmsnorm(x, g):
    xf = x.astype(jnp.float32)
    y = xf * lax.rsqrt(jnp.mean(xf * xf, axis=-1, keepdims=True) + EPS)
    if g is not None:
        y = y * g.astype(jnp.float32)
    return y.astype(x.dtype)

def l2norm(x):
    xf = x.astype(jnp.float32)
    return xf * lax.rsqrt(jnp.sum(xf * xf, axis=-1, keepdims=True) + EPS)

def swiglu(x, w_in, w_out):
    gate, up = jnp.split(x @ w_in, 2, axis=-1)
    return (jax.nn.silu(gate) * up) @ w_out

def rotary(x, pos):
    half = x.shape[-1] // 2
    inv_freq = 1.0 / (ROPE_BASE ** jnp.linspace(0.0, 1.0, half, dtype=jnp.float32))
    ang = pos.astype(jnp.float32)[:, None] * inv_freq[None, :]
    cos = jnp.cos(ang)[None, :, None, :]
    sin = jnp.sin(ang)[None, :, None, :]
    xf = x.astype(jnp.float32)
    x1, x2 = xf[..., :half], xf[..., half:]
    return jnp.concatenate([x1 * cos - x2 * sin, x1 * sin + x2 * cos], axis=-1)

def causal_conv(x, buf, w):
    seq = x.shape[1]
    xp = jnp.concatenate([buf.astype(x.dtype), x], axis=1)
    y = xp[:, 0:seq] * w[0]
    for j in range(1, CONV_W):
        y = y + xp[:, j:j + seq] * w[j]
    return y, xp[:, seq:]

def _to_chunks(a, c):
    b, l = a.shape[0], a.shape[1]
    return jnp.moveaxis(a.reshape((b, l // c, c) + a.shape[2:]), 1, 0)

def _from_chunks(a):
    n, b, c = a.shape[0], a.shape[1], a.shape[2]
    return jnp.moveaxis(a, 0, 1).reshape((b, n * c) + a.shape[3:])

def chunked_scalar_decay(q, k, v, log_a, s0):
    f32 = jnp.float32
    c = math.gcd(q.shape[1], CHUNK)
    incl = jnp.tril(jnp.ones((c, c), dtype=bool))[None, :, :, None]

    def step(s, blk):
        qc, kc, vc, lac = blk
        cum = jnp.cumsum(lac, axis=1)
        dec = jnp.exp(jnp.where(incl, cum[:, :, None] - cum[:, None], -jnp.inf))
        scores = jnp.einsum('bihd,bjhd->bijh', qc, kc) * dec
        o = (jnp.einsum('bijh,bjhv->bihv', scores, vc)
             + jnp.einsum('bihd,bhdv->bihv', qc * jnp.exp(cum)[..., None], s))
        k_end = kc * jnp.exp(cum[:, -1:] - cum)[..., None]
        s = s * jnp.exp(cum[:, -1])[..., None, None] + jnp.einsum('bjhd,bjhv->bhdv', k_end, vc)
        return s, o

    xs = tuple(_to_chunks(a.astype(f32), c) for a in (q, k, v, log_a))
    s, o = lax.scan(step, s0.astype(f32), xs)
    return _from_chunks(o), s

def chunked_vector_decay(q, k, v, log_f, s0):
    f32 = jnp.float32
    c = math.gcd(q.shape[1], CHUNK)
    incl = jnp.tril(jnp.ones((c, c), dtype=bool))[None, :, :, None, None]

    def step(s, blk):
        qc, kc, vc, lfc = blk
        cum = jnp.cumsum(lfc, axis=1)
        dec = jnp.exp(jnp.where(incl, cum[:, :, None] - cum[:, None], -jnp.inf))
        scores = jnp.einsum('bihd,bjhd,bijhd->bijh', qc, kc, dec)
        o = (jnp.einsum('bijh,bjhv->bihv', scores, vc)
             + jnp.einsum('bihd,bhdv->bihv', qc * jnp.exp(cum), s))
        k_end = kc * jnp.exp(cum[:, -1:] - cum)
        s = s * jnp.exp(cum[:, -1])[..., None] + jnp.einsum('bjhd,bjhv->bhdv', k_end, vc)
        return s, o

    xs = tuple(_to_chunks(a.astype(f32), c) for a in (q, k, v, log_f))
    s, o = lax.scan(step, s0.astype(f32), xs)
    return _from_chunks(o), s

def chunked_gated_delta(q, k, v, log_g, beta, s0):
    f32 = jnp.float32
    c = math.gcd(q.shape[1], CHUNK)
    incl = jnp.tril(jnp.ones((c, c), dtype=bool))[None, None]
    strict = jnp.tril(jnp.ones((c, c), dtype=bool), -1)[None, None]
    dv = v.shape[-1]

    def step(s, blk):
        qc, kc, vc, lgc, bc = blk
        cum = jnp.cumsum(lgc, axis=1)
        cum_h = jnp.swapaxes(cum, 1, 2)
        dec = jnp.exp(jnp.where(incl, cum_h[..., :, None] - cum_h[..., None, :], -jnp.inf))
        b_h = jnp.swapaxes(bc, 1, 2)
        a_mat = jnp.where(strict, b_h[..., :, None] * dec * jnp.einsum('bihd,bjhd->bhij', kc, kc), 0.0)
        rhs = jnp.concatenate([vc, kc * jnp.exp(cum)[..., None]], axis=-1) * bc[..., None]
        sol = lax.linalg.triangular_solve(a_mat + jnp.eye(c, dtype=f32), jnp.swapaxes(rhs, 1, 2),
                                          left_side=True, lower=True, unit_diagonal=True)
        w_new = sol[..., :dv] - jnp.einsum('bhcd,bhdv->bhcv', sol[..., dv:], s)
        scores = jnp.einsum('bihd,bjhd->bhij', qc, kc) * dec
        o = (jnp.einsum('bhij,bhjv->bihv', scores, w_new)
             + jnp.einsum('bihd,bhdv->bihv', qc * jnp.exp(cum)[..., None], s))
        k_end = kc * jnp.exp(cum[:, -1:] - cum)[..., None]
        s = s * jnp.exp(cum[:, -1])[..., None, None] + jnp.einsum('bjhd,bhjv->bhdv', k_end, w_new)
        return s, o

    xs = tuple(_to_chunks(a.astype(f32), c) for a in (q, k, v, log_g, beta))
    s, o = lax.scan(step, s0.astype(f32), xs)
    return _from_chunks(o), s

def hybrid_layer(x, pos, states, lw):
    (s_ssm, s_ssm_conv, s_hg, s_ret, s_gdn, s_gdn_conv) = states
    (norm_g, ffn_w_in, ffn_w_out, w_in, w_branch, w_out,
     mb_conv_w, mb_conv_b, mb_a_log, mb_dt_bias, mb_d, mb_norm,
     hg_lb, hg_norm, gdn_conv_w, gdn_a_log, gdn_dt_bias, gdn_norm) = lw
    f32 = jnp.float32
    bsz, seq = x.shape[0], x.shape[1]

    h = x + 0.5 * rmsnorm(swiglu(rmsnorm(x, norm_g[0]), ffn_w_in[0], ffn_w_out[0]), norm_g[1])

    u = rmsnorm(h, norm_g[2])
    (mb_z, mb_xbc, mb_dt, hg_q, hg_f, hg_i, hg_g, ret_q, ret_k, ret_v, ret_g,
     gdn_qkv, gdn_z, gdn_a, gdn_b, gates) = jnp.split(u @ w_in, IN_OFFSETS, axis=-1)

    xbc, new_ssm_conv = causal_conv(mb_xbc, s_ssm_conv, mb_conv_w)
    xbc = jax.nn.silu(xbc + mb_conv_b)
    xs, bm, cm = jnp.split(xbc, (BRANCH_W, BRANCH_W + MB_GROUPS * MB_STATE), axis=-1)
    xs = xs.reshape(bsz, seq, MB_HEADS, MB_HEADDIM)
    bm = jnp.repeat(bm.reshape(bsz, seq, MB_GROUPS, MB_STATE), MB_HEADS // MB_GROUPS, axis=2)
    cm = jnp.repeat(cm.reshape(bsz, seq, MB_GROUPS, MB_STATE), MB_HEADS // MB_GROUPS, axis=2)
    dt = jax.nn.softplus(mb_dt.astype(f32) + mb_dt_bias.astype(f32))
    log_a = -jnp.exp(mb_a_log.astype(f32)) * dt
    y_mb, new_ssm = chunked_scalar_decay(cm, bm * dt[..., None], xs, log_a, s_ssm)
    y_mb = y_mb + mb_d.astype(f32)[:, None] * xs
    y_mb = rmsnorm(y_mb.reshape(bsz, seq, BRANCH_W) * jax.nn.silu(mb_z.astype(f32)), mb_norm)

    lb = hg_lb.astype(f32)
    f_gate = lb + (1.0 - lb) * jax.nn.sigmoid(hg_f.astype(f32))
    shp = (bsz, seq, HG_HEADS, HG_DK)
    y_hg, new_hg = chunked_vector_decay(jax.nn.silu(hg_q).reshape(shp), (1.0 - f_gate).reshape(shp),
                                        hg_i.reshape(bsz, seq, HG_HEADS, HG_DV),
                                        jnp.log(f_gate).reshape(shp), s_hg)
    y_hg = rmsnorm(y_hg, hg_norm).reshape(bsz, seq, BRANCH_W) * jax.nn.silu(hg_g.astype(f32))

    q_r = rotary(ret_q.reshape(bsz, seq, RET_HEADS, RET_DK), pos)
    k_r = rotary(ret_k.reshape(bsz, seq, RET_HEADS, RET_DK), pos) * (RET_DK ** -0.5)
    log_gamma = jnp.log(1.0 - jnp.exp2(-5.0 - jnp.arange(RET_HEADS, dtype=f32)))
    y_r, new_ret = chunked_scalar_decay(q_r, k_r, ret_v.reshape(bsz, seq, RET_HEADS, RET_DV),
                                        jnp.broadcast_to(log_gamma, (bsz, seq, RET_HEADS)), s_ret)
    y_r = rmsnorm(y_r, None).reshape(bsz, seq, BRANCH_W) * jax.nn.silu(ret_g.astype(f32))

    qkv, new_gdn_conv = causal_conv(gdn_qkv, s_gdn_conv, gdn_conv_w)
    qkv = jax.nn.silu(qkv)
    q_d, k_d, v_d = jnp.split(qkv, (GDN_HEADS * GDN_DK, 2 * GDN_HEADS * GDN_DK), axis=-1)
    q_d = l2norm(q_d.reshape(bsz, seq, GDN_HEADS, GDN_DK)) * (GDN_DK ** -0.5)
    k_d = l2norm(k_d.reshape(bsz, seq, GDN_HEADS, GDN_DK))
    beta = jax.nn.sigmoid(gdn_b.astype(f32))
    log_g = -jnp.exp(gdn_a_log.astype(f32)) * jax.nn.softplus(gdn_a.astype(f32) + gdn_dt_bias.astype(f32))
    y_d, new_gdn = chunked_gated_delta(q_d, k_d, v_d.reshape(bsz, seq, GDN_HEADS, GDN_DV), log_g, beta, s_gdn)
    y_d = rmsnorm(y_d, gdn_norm).reshape(bsz, seq, BRANCH_W) * jax.nn.silu(gdn_z.astype(f32))

    gate = jax.nn.sigmoid(gates.astype(f32)).reshape(bsz, seq, N_BRANCH, D_MODEL)
    merged = jnp.zeros((bsz, seq, D_MODEL), f32)
    for n, yb in enumerate((y_mb, y_hg, y_r, y_d)):
        merged = merged + gate[:, :, n] * (yb.astype(x.dtype) @ w_branch[n])
    mixed = merged.astype(x.dtype) @ w_out
    h = h + rmsnorm(mixed, norm_g[3])

    h = h + 0.5 * rmsnorm(swiglu(rmsnorm(h, norm_g[4]), ffn_w_in[1], ffn_w_out[1]), norm_g[5])

    sd = x.dtype
    new_states = (new_ssm.astype(sd), new_ssm_conv.astype(sd), new_hg.astype(sd),
                  new_ret.astype(sd), new_gdn.astype(sd), new_gdn_conv.astype(sd))
    return h, new_states

def setup_inputs(seed: int = 0) -> dict:
    key = jax.random.key(seed)
    ks = jax.random.split(key, 26)
    f32 = jnp.float32

    def nrm(k, shape, scale):
        return jax.random.normal(k, shape, f32) * scale

    def dt_bias_init(k, shape):
        dt0 = jnp.exp(jax.random.uniform(k, shape, f32, math.log(1e-3), math.log(1e-1)))
        return dt0 + jnp.log(-jnp.expm1(-dt0))

    return {
        'x_prompt': nrm(ks[0], (BATCH, SEQ, D_MODEL), 1.0),
        'x_sample': nrm(ks[1], (DEC_BATCH, DEC_SEQ, D_MODEL), 1.0),
        'state_ssm': nrm(ks[2], (DEPTH, DEC_BATCH, MB_HEADS, MB_STATE, MB_HEADDIM), 0.5),
        'state_ssm_conv': nrm(ks[3], (DEPTH, DEC_BATCH, CONV_W - 1, MB_CONV_DIM), 1.0),
        'state_hgrn': nrm(ks[4], (DEPTH, DEC_BATCH, HG_HEADS, HG_DK, HG_DV), 0.5),
        'state_ret': nrm(ks[5], (DEPTH, DEC_BATCH, RET_HEADS, RET_DK, RET_DV), 0.5),
        'state_gdn': nrm(ks[6], (DEPTH, DEC_BATCH, GDN_HEADS, GDN_DK, GDN_DV), 0.1),
        'state_gdn_conv': nrm(ks[7], (DEPTH, DEC_BATCH, CONV_W - 1, GDN_CONV_DIM), 1.0),
        'norm_g': 1.0 + nrm(ks[8], (DEPTH, 6, D_MODEL), 0.02),
        'ffn_w_in': nrm(ks[9], (DEPTH, 2, D_MODEL, 2 * D_FF), D_MODEL ** -0.5),
        'ffn_w_out': nrm(ks[10], (DEPTH, 2, D_FF, D_MODEL), D_FF ** -0.5),
        'w_in': nrm(ks[11], (DEPTH, D_MODEL, D_IN), D_MODEL ** -0.5),
        'w_branch': nrm(ks[12], (DEPTH, N_BRANCH, BRANCH_W, D_MODEL), BRANCH_W ** -0.5),
        'w_out': nrm(ks[13], (DEPTH, D_MODEL, D_MODEL), D_MODEL ** -0.5),
        'mb_conv_w': nrm(ks[14], (DEPTH, CONV_W, MB_CONV_DIM), CONV_W ** -0.5),
        'mb_conv_b': nrm(ks[15], (DEPTH, MB_CONV_DIM), 0.02),
        'mb_a_log': jnp.log(jax.random.uniform(ks[16], (DEPTH, MB_HEADS), f32, 1.0, 16.0)),
        'mb_dt_bias': dt_bias_init(ks[17], (DEPTH, MB_HEADS)),
        'mb_d': 1.0 + nrm(ks[18], (DEPTH, MB_HEADS), 0.1),
        'mb_norm': 1.0 + nrm(ks[19], (DEPTH, BRANCH_W), 0.02),
        'hg_lb_logits': nrm(ks[20], (DEPTH, HG_HEADS * HG_DK), 1.0),
        'hg_norm': 1.0 + nrm(ks[21], (DEPTH, HG_DV), 0.02),
        'gdn_conv_w': nrm(ks[22], (DEPTH, CONV_W, GDN_CONV_DIM), CONV_W ** -0.5),
        'gdn_a_log': jnp.log(jax.random.uniform(ks[23], (DEPTH, GDN_HEADS), f32, 1.0, 16.0)),
        'gdn_dt_bias': dt_bias_init(ks[24], (DEPTH, GDN_HEADS)),
        'gdn_norm': 1.0 + nrm(ks[25], (DEPTH, GDN_DV), 0.02),
    }

def reference(x_prompt, x_sample, state_ssm, state_ssm_conv, state_hgrn, state_ret, state_gdn,
              state_gdn_conv, norm_g, ffn_w_in, ffn_w_out, w_in, w_branch, w_out,
              mb_conv_w, mb_conv_b, mb_a_log, mb_dt_bias, mb_d, mb_norm,
              hg_lb_logits, hg_norm, gdn_conv_w, gdn_a_log, gdn_dt_bias, gdn_norm):
    f32 = jnp.float32
    lb_all = jnp.cumsum(jax.nn.softmax(hg_lb_logits.astype(f32), axis=0), axis=0)
    lb_all = lb_all - lb_all[0:1]

    pos_p = jnp.arange(x_prompt.shape[1])
    pos_s = PAST_LEN + jnp.arange(x_sample.shape[1])
    bp = x_prompt.shape[0]
    zero_states = (
        jnp.zeros((bp, MB_HEADS, MB_STATE, MB_HEADDIM), f32),
        jnp.zeros((bp, CONV_W - 1, MB_CONV_DIM), x_prompt.dtype),
        jnp.zeros((bp, HG_HEADS, HG_DK, HG_DV), f32),
        jnp.zeros((bp, RET_HEADS, RET_DK, RET_DV), f32),
        jnp.zeros((bp, GDN_HEADS, GDN_DK, GDN_DV), f32),
        jnp.zeros((bp, CONV_W - 1, GDN_CONV_DIM), x_prompt.dtype),
    )

    hp, hs = x_prompt, x_sample
    st_prompt, st_sample = [], []
    for l in range(DEPTH):
        lw = (norm_g[l], ffn_w_in[l], ffn_w_out[l], w_in[l], w_branch[l], w_out[l],
              mb_conv_w[l], mb_conv_b[l], mb_a_log[l], mb_dt_bias[l], mb_d[l], mb_norm[l],
              lb_all[l], hg_norm[l], gdn_conv_w[l], gdn_a_log[l], gdn_dt_bias[l], gdn_norm[l])
        hp, sp = hybrid_layer(hp, pos_p, zero_states, lw)
        past = (state_ssm[l], state_ssm_conv[l], state_hgrn[l], state_ret[l], state_gdn[l], state_gdn_conv[l])
        hs, ss = hybrid_layer(hs, pos_s, past, lw)
        st_prompt.append(sp)
        st_sample.append(ss)

    def stack(sts, i):
        return jnp.stack([s[i] for s in sts], axis=0)

    return (hp, hs,
            stack(st_prompt, 0), stack(st_prompt, 1), stack(st_prompt, 2),
            stack(st_prompt, 3), stack(st_prompt, 4), stack(st_prompt, 5),
            stack(st_sample, 0), stack(st_sample, 1), stack(st_sample, 2),
            stack(st_sample, 3), stack(st_sample, 4), stack(st_sample, 5))


_drawn_inputs = setup_inputs


def setup_inputs(seed=0):
    import zlib

    import numpy as np

    out = dict(_drawn_inputs(seed))
    spreads = {}
    factors = {}
    for name, (base, spread) in spreads.items():
        noise = np.random.default_rng([zlib.crc32(name.encode()), seed]).standard_normal(out[name].shape)
        drawn = base * np.exp(spread * noise) if base else spread * noise
        out[name] = __import__('jax').numpy.asarray(drawn.astype(out[name].dtype))
    for name, factor in factors.items():
        out[name] = (out[name] * factor).astype(out[name].dtype)
    return out
```

```python
from contextlib import ExitStack, contextmanager

import numpy as np

import concourse.bass as bass
from concourse import mybir

ALU = mybir.AluOpType
ACT = mybir.ActivationFunctionType
F32 = mybir.dt.float32
F32R = mybir.dt.float32r
AX_X = mybir.AxisListType.X

P = 128
D_MODEL, DEPTH = 1024, 2
SEQ, DEC_BATCH, DEC_SEQ, PAST_LEN = 256, 8, 8, 2048
T = SEQ + DEC_BATCH * DEC_SEQ
D_FF = 2816
KD = D_MODEL // P
KF = D_FF // P
KB = 4
C = 8
NC = T // C
NCP = SEQ // C
EPS = 1e-6
XW = SEQ + 3 + DEC_BATCH * (DEC_SEQ + 3)

Z, HQ, HF, HI, HG, RQ, RK, RV, RG, GZ = 0, 4, 8, 12, 16, 20, 22, 24, 28, 32
NPLAIN, NCONV = 36, 18
NSLOT = 4
SLOT = KD * P
DOWN_K = (8, 8, 6)
ROWS = 96

V_G, V_CW, V_CB, V_D, V_MN, V_LB, V_HN, V_GN, V_RB, V_RA, V_ON = 0, 48, 120, 126, 130, 134, 142, 143, 144, 145, 146
NV = 147

CONST, _at = {}, 0
for _name, _cols in (("ones", P), ("ident", P), ("tri", P), ("neg", P), ("pos", P), ("tri_s", 64), ("neg_s", 64),
                     ("pos_s", 64), ("same_s", 64), ("rot", P), ("cos", T), ("sin", T), ("b8", P), ("b16", P),
                     ("b32", P), ("b64", P), ("b128", P), ("lgam", 4), ("pick", 8), ("eps", 1)):
    CONST[_name] = (_at, _cols)
    _at += _cols
NCONST = _at
MB, RET, GDN = 0, 8, 12
TILES3 = ((0, 128), (128, 128), (256, 64))
NS = DEC_BATCH


START = ("dma_conv_out", "dma_hout0", "dma_hout1", "dma_tok", "h_ready", "hg_kv", "hg_o", "hg_oi", "o_copied",
         "state_new", "vec_free", *(f"{n}{i}" for n in ("bank_free", "lo_ready") for i in range(NSLOT)))


def unit_of(name):
    return 16 if name.startswith("dma_") else 1


class Count:

    def __init__(self, sem, unit, name):
        self.sem, self.unit, self.name, self.terms = sem, unit, name, []
        self.n = unit if name in START else 0

    def at(self):
        e = self.n
        for reg, per in self.terms:
            if per:
                e = reg * per + e
        return e

    def one(self):
        self.n += self.unit
        return self.sem, self.unit

    def now(self):
        return self.sem, self.at()

    def next(self):
        self.n += self.unit
        return self.sem, self.at()

    def skip(self, k=1):
        self.n += k * self.unit


class Book:

    def __init__(self, eng, name, sems, per_body, seen):
        self.eng, self.name, self.sems, self.per_body, self.seen = eng, name, sems, per_body, seen
        self.counts = {}

    def __getitem__(self, name):
        if name not in self.counts:
            self.counts[name] = Count(self.sems[name], unit_of(name), name)
            self.counts[name].terms = [(r, self.per_body.get((self.name, tag, name), 0)) for r, tag in self.around]
        return self.counts[name]

    around = ()

    @contextmanager
    def passing(self, section):
        uses = {k: n for k, n in section.uses.items() if self.name == "pe" or not k.startswith("dma_")}
        start = {k: self[k].n for k in uses}
        yield
        for k, n in uses.items():
            self.counts[k].n = start[k] + n * self.counts[k].unit

    @contextmanager
    def loop(self, trips, tag):
        first = {k: unit_of(k) if k in START else 0 for k in self.sems}
        start = {**first, **{k: c.n for k, c in self.counts.items()}}
        outer = self.around
        with self.eng.Fori(0, trips) as i:
            self.around = (*outer, (i, tag))
            for k, c in self.counts.items():
                c.terms.append((i, self.per_body.get((self.name, tag, k), 0)))
            yield i
            for k, c in self.counts.items():
                per = c.n - start[k]
                self.seen[(self.name, tag, k)] = per
                c.terms.pop()
                c.n = start[k] + per * trips
        self.around = outer


def build(nc, a, o, per_body, seen):
    with ExitStack() as ctx:
        _build(nc, a, o, per_body, seen, ctx)


def _build(nc, a, o, per_body, seen, ctx):
    sems = {}

    def sem(*names):
        for n in names:
            sems[n] = ctx.enter_context(nc.semaphore(n))

    def sb(name, shape, dt=F32, stack=ctx):
        return stack.enter_context(nc.sbuf_tensor(name, shape, dt))

    h = sb("h", [P, KD, T])
    u_hi, u_lo = sb("u_hi", [P, KD, T], F32R), sb("u_lo", [P, KD, T], F32R)
    raw = [sb(f"w_raw{i}", [P, SLOT]) for i in range(NSLOT)]
    w_hi = [sb(f"w_hi{i}", [P, SLOT], F32R) for i in range(NSLOT)]
    w_lo = [sb(f"w_lo{i}", [P, SLOT], F32R) for i in range(NSLOT)]
    vec = sb("vec", [P, NV])
    const = sb("const", [P, NCONST])
    c_ = {k: const[:, at:at + n] for k, (at, n) in CONST.items()}
    ones, eps_c = c_["ones"], c_["eps"]
    fade = sb("fade", [P, 4, NC])
    lb = sb("lb", [P, 32])
    la_tok, beta_tok, dt_tok = sb("la_tok", [P, 3, 16]), sb("beta_tok", [P, 3, 4]), sb("dt_tok", [P, 3, 8])
    cum_tok, ecum_tok = sb("cum_tok", [P, 3, 16]), sb("ecum_tok", [P, 3, 16])
    to_end, to_end_dt, beta_cum = sb("to_end", [P, 3, 16]), sb("to_end_dt", [P, 3, 8]), sb("beta_cum", [P, 3, 4])
    rows = sb("rows", [ROWS, T])
    with ExitStack() as part:
        hid_hi = sb("hid_hi", [P, KF, T], F32R, part)
        hid_lo = sb("hid_lo", [P, KF, T], F32R, part)
    part = ExitStack()
    proj = sb("proj", [P, NPLAIN, T], F32, ctx)
    with ExitStack() as part:
        m_hi = sb("m_hi", [P, KD, T], F32R, part)
        m_lo = sb("m_lo", [P, KD, T], F32R, part)
    xp = sb("xp", [P, NCONV, XW], F32, ctx)
    with ExitStack() as part:
        y = sb("y", [P, KD, T], F32, part)
        tmp = sb("tmp", [P, KD, T], F32, part)
        gate_s = [sb(f"gate_s{i}", [P, T], F32, part) for i in range(2)]
        hid_t = [sb(f"hid_t{i}", [P, T], F32, part) for i in range(2)]
        ssq = sb("ssq", [P, T], F32, part)
        rms = sb("rms", [P, T], F32, part)
        rinv = sb("rinv", [P, T], F32, part)


    with ExitStack() as part:
        hc = sb("hg_cum", [P, 160, C], F32, part)
        he = [sb(f"hg_e{i}", [P, 160 * C], F32, part) for i in range(2)]
        hx = [sb(f"hg_x{i}", [P, 160 * C], F32, part) for i in range(2)]
        ho = sb("hg_o", [P, 160, C], F32, part)
        ht = sb("hg_t", [P, 160 * C], F32, part)
    with ExitStack() as part:
        sb("_cum", [P, 160 * C], F32, part)
        kv = [sb(f"hg_kv{i}", [C, 1024], F32, part) for i in range(4)]
        sb("_pad", [P, 4 * 160 * C - 4 * 1024], F32, part)
        sb("_o", [P, 160 * C], F32, part)
        hoi = sb("hg_oi", [P, 4, T], F32, part)
        hs = [sb(f"hg_s{i}", [P, 512], F32, part) for i in range(2)]
        hs_in = [sb(f"hg_in{i}", [P, 512], F32, part) for i in range(2)]
        hs_out = [sb(f"hg_out{i}", [P, 512], F32, part) for i in range(2)]
    with ExitStack() as part:
        rx, re, ru, rt, rl, rb = (sb(f"row_{n}", [ROWS, T], F32, part) for n in "xeutlb")
        cacc = [sb(f"conv_acc{i}", [P, XW], F32, part) for i in range(2)]
        cin = sb("conv_in", [P, NCONV, NS, 3], F32, part)
        cout = sb("conv_out", [P, NCONV, NS + 1, 3], F32, part)
        lsq = [sb(f"l2_sq{i}", [P, T], F32, part) for i in range(4)]
        lrt = [sb(f"l2_rt{i}", [P, T], F32, part) for i in range(4)]
    with ExitStack() as part:
        dm, em, dm2, ecb, pm, qd, kend, vtok, kb, vb, wn, nsk = (
            sb(f"sc_{n}", [P, 512], F32, part) for n in ("d", "e", "d2", "ecb", "p", "qd", "kend", "v", "kb", "vb", "wn", "nsk"))
        state = {MB: sb("st_mb", [P, 4, 64], F32, part), RET: sb("st_ret", [P, 2, 128], F32, part),
                 GDN: sb("st_gdn", [P, 4, 128], F32, part)}
        st_s = sb("st_s", [P, NS, 512], F32, part)
    work = proj[:, HQ:HQ + 12, :].rearrange("p k t -> p (k t)")
    W = [work[:, 512 * i:512 * i + 512] for i in range(7)]
    f_sq, f_rt, f_o = (work[:, 1280 * i:1280 * i + 1280] for i in range(3))

    f_ok = f_o.rearrange("p (k t) -> p k t", k=4)
    ho_k = ho[:, :, :].rearrange("p (k c) t -> p k (c t)", k=4)
    vm = [work[0:64, 1024 * i:1024 * i + 1024] for i in range(2)]

    def by_chunk(x):
        return x.rearrange("p k (c t) -> p (k c) t", t=C)

    hq, hf, hi_v = (by_chunk(proj[:, at:at + 4, :]) for at in (HQ, HF, HI))
    fade_v = fade[:, :, :].rearrange("p h c -> p (h c)")
    GROUPS = (("mb", 0), ("mb", 1), ("ret", 0), ("gdn", 0))

    def acc_sample(acc):
        return acc[:, SEQ + 3:XW].rearrange("p (s t) -> p s t", s=NS)[:, :, 0:C]

    def over(x, shape):
        return x.to_broadcast(shape)

    def tri_of(t):
        return c_["tri"] if t < 2 else c_["tri_s"][0:64, :]

    psum = [ctx.enter_context(nc.psum_tensor(f"bank{i}", [P, 512], F32)) for i in range(4)]
    mix = ctx.enter_context(nc.psum_tensor("mix", [P, 4, 512], F32))
    tok_scratch = nc.dram_tensor("tok_scratch", [T, 1024], F32, kind="Internal").ap()

    sem("dma_in", "dma_vec", "dma_out", "v_step", "a_step", "p_step", "t_step")
    sem(*[f"{n}{i}" for n in ("dma_w", "hi_ready", "lo_ready", "bank_free") for i in range(NSLOT)])
    sem("tiles_done")
    sem("gate_ready", "hid_ready", "squares", "sums", "norm_sum", "root", "u_ready", "y_ready", "h_ready", "merged", "vec_free", "projected")
    sem("row_x", "row_e", "row_u", "row_ln", "rows_ready", "tok_t", "tok_copied", "tok_sums", "tok_exp", "tok_ready")
    sem("dma_conv", "dma_conv_out", "conv_filled", "conv_saved", "conv_sum", "conv_done")
    sem("l2_sq", "l2_sum", "l2_root", "l2_done", "bound_d", "bound_e", "hg_sig", "hg_f", "hg_ln", "silus")
    sem("pair_d", "pair_e", "pair_x", "pair_a", "pair_t", "hg_end_d", "hg_end_e", "hg_ready")
    sem("kv_t", "kv_copied", "dma_tok", "hg_kv", "hg_o", "hg_oi", "hg_s", "dma_hgp", "hg_finished")
    sem(*[f"dma_kv{i}" for i in range(4)], *[f"dma_{n}{i}" for n in ("hin", "hout") for i in range(2)])
    sem("f_sq", "f_sum", "f_root", "f_pre", "mixer_done", "rot_ps", "rot_used", "rotated")
    sem("cum_bc", "cum_used", "ecb_ready", "dec_d", "dec_e", "scores", "v_copied", "p_ready", "q_ready", "k_ready",
        "o_done", "o_copied", "state_mm", "state_new", "dma_state", "dma_state_out", "gdn_mm", "gdn_ev", "vm_ready", "vm_used",
        "w_ready", "gdn_v", "o_part")

    block = ctx.enter_context(nc.Block())

    def book(eng, name):
        return Book(eng, name, sems, per_body, seen)

    sections = {}

    class Section:
        def __init__(self, name, f, trips, sources, banks):
            self.name, self.f, self.trips, self.sources, self.banks = name, f, trips, sources, banks
            self.n, self.base, self.lead = len(sources), sum(x.trips * x.n for x in sections.values()), 2
            self.tag = f"{name}{f}"
            sections[self.tag] = self
            self.loads, s = [], 0
            for j, (src, nk, split) in enumerate(sources):
                self.loads.append((src, nk, split, j % NSLOT, s % NSLOT if split else None))
                s += split
            self.uses = {f"bank_free{q}": trips * sum(x == q for x in banks) for q in range(4)}
            self.uses |= {f"dma_w{r}": trips * sum(x[3] == r for x in self.loads) for r in range(NSLOT)}

    def row(x, cols):
        return x[:, 0:cols]

    for f in range(2):
        Section("up", f, KF // 2, [(lambda l, i, m=m, g=g, f=f: a["w_up"][l, f, 2 * i + m, g], KD, True)
                                   for m in range(2) for g in range(2)], (0, 1, 2, 3))
        Section("down", f, 2, [(lambda l, i, m=m, q=q, f=f: a["w_down"][l, f, 4 * i + m][:, sum(DOWN_K[:q]) * P:sum(DOWN_K[:q + 1]) * P],
                                DOWN_K[q], True) for m in range(4) for q in range(3)], (0, 1, 2, 3))
        if f:
            break
        Section("proj", 0, NPLAIN // 4, [(lambda l, i, m=m: a["w_proj"][l, 4 * i + m], KD, True) for m in range(4)],
                (0, 1, 2, 3))
        Section("conv", 0, 4, [(lambda l, i, m=m: a["w_proj"][l, 4 * i + (NPLAIN + m)], KD, True) for m in range(4)],
                (0, 1, 2, 3))
        Section("tail", 0, 1, [(lambda l, i, m=m: a["w_proj"][l, NPLAIN + 16 + m], KD, True) for m in range(2)]
                + [(lambda l, i: a["w_rows"][l], KD * ROWS // P, True)], (0, 1, 2))
        Section("merge", 0, KD, [t for n in range(4) for t in (
            (lambda l, i, n=n: a["w_gate"][l, i, n], KD, True),
            (lambda l, i, n=n: a["w_branch"][l, i, n], KB, False))], (0, 1, 2, 3) * 2)
        sections["merge0"].lead = 4
        Section("out", 0, KD // 4, [(lambda l, i, m=m: a["w_out"][l, 4 * i + m], KD, True) for m in range(4)],
                (0, 1, 2, 3))
    ORDER = list(sections.values())
    TILES = sum(x.trips * x.n for x in ORDER)
    AHEAD = NSLOT

    def done(l, sec, i, j):
        return l * TILES + (i * sec.n + (AHEAD + sec.base + j + 1))

    def slot_empty(l, sec, i, j):
        return done(l, sec, i, j - (3 if sec.name == "merge" else NSLOT))

    @block.sync
    def _(sp):
        b = book(sp, "sp")

        def mixer_dmas(l):
            sp.wait_ge(*b["projected"].next())
            sp.dma_start(cin[:, :, :, :], a["st_conv"][l]).then_inc(*b["dma_conv"].one())
            sp.wait_ge(*b["conv_saved"].next())
            sp.dma_start(o["st_conv"][l], cout[:, :, :, :]).then_inc(*b["dma_conv_out"].one())
            b["dma_tok"].skip(3)
            with b.loop(NCP // 4, "hg_prompt") as i:
                sp.wait_ge(*b["dma_tok"].now())
                for q in range(4):
                    sp.wait_ge(*b["hg_kv"].now())
                    b["hg_kv"].skip()
                    sp.dma_start(kv[q][:, :], tok_scratch[bass.ds(i * (4 * C) + q * C, C), :]).then_inc(
                        *b[f"dma_kv{q}"].one())
            b["hg_s"].skip(NCP)
            with b.loop(NS // 4, "hg_sample") as i:
                for q in range(4):
                    sp.wait_ge(*b["hg_kv"].now())
                    b["hg_kv"].skip()
                    sp.dma_start(kv[q][:, :], tok_scratch[bass.ds(i * (4 * C) + (SEQ + q * C), C), :]).then_inc(
                        *b[f"dma_kv{q}"].one())
                    sp.wait_ge(*b["hg_s"].now())
                    b["hg_s"].skip()
                    sp.dma_start(hs_in[q % 2][:, :], a["st_hg"][l, 4 * i + q]).then_inc(*b[f"dma_hin{q % 2}"].one())
            sp.wait_ge(*b["hg_finished"].next())
            sp.dma_start(st_s[:, :, 0:256], a["st_mb"][l].rearrange("p (s n) -> p s n", s=NS)).then_inc(*b["dma_state"].one())
            sp.dma_start(st_s[:, :, 256:512], a["st_ret"][l].rearrange("p (s n) -> p s n", s=NS)).then_inc(*b["dma_state"].one())
            n_state = {"mb": 3, "ret": 6, "gdn": 9}
            b["state_new"].skip(6)
            sp.wait_ge(*b["state_new"].now())
            sp.dma_start(o["mb_p"][l], state[MB][:, :, :].rearrange("p h n -> p (h n)")).then_inc(*b["dma_state_out"].one())
            sp.dma_start(o["mb_s"][l].rearrange("p (s n) -> p s n", s=NS), st_s[:, :, 0:256]).then_inc(*b["dma_state_out"].one())
            b["state_new"].skip(3)
            sp.wait_ge(*b["state_new"].now())
            sp.dma_start(o["ret_p"][l], state[RET][:, :, :].rearrange("p h n -> p (h n)")).then_inc(*b["dma_state_out"].one())
            sp.dma_start(o["ret_s"][l].rearrange("p (s n) -> p s n", s=NS), st_s[:, :, 256:512]).then_inc(*b["dma_state_out"].one())
            sp.wait_ge(*b["dma_state_out"].now())
            sp.dma_start(st_s[:, :, :], a["st_gdn"][l].rearrange("p (s n) -> p s n", s=NS)).then_inc(*b["dma_state"].one())
            b["state_new"].skip(3)
            sp.wait_ge(*b["state_new"].now())
            sp.dma_start(o["gdn_p"][l], state[GDN][:, :, :].rearrange("p h n -> p (h n)")).then_inc(*b["dma_state_out"].one())
            sp.dma_start(o["gdn_s"][l].rearrange("p (s n) -> p s n", s=NS), st_s[:, :, :]).then_inc(*b["dma_state_out"].one())

        sp.dma_start(h[:, :, :], a["x"]).then_inc(*b["dma_in"].one())
        sp.dma_start(const[:, :], a["const"]).then_inc(*b["dma_in"].one())
        with b.loop(DEPTH, "layer") as l:
            sp.wait_ge(*b["vec_free"].now())
            b["vec_free"].skip()
            sp.dma_start(vec[:, :], a["vec"][l]).then_inc(*b["dma_vec"].one())
            for sec in ORDER:
                if sec.name == "merge":
                    mixer_dmas(l)
                with b.loop(sec.trips, sec.tag) as i:
                    for j, (src, nk, split, r, _) in enumerate(sec.loads):
                        sp.wait_ge(*b[f"lo_ready{r}"].now())
                        if split:
                            b[f"lo_ready{r}"].skip()
                        if sec.name in ("merge", "out"):
                            sp.wait_ge(sems["tiles_done"], done(l, sec, i, j - NSLOT))
                        sp.dma_start(raw[r][:, 0:nk * P], src(l, i)).then_inc(*b[f"dma_w{r}"].one())
        sp.wait_ge(sems["h_ready"], 1 + 3 * DEPTH)
        sp.dma_start(o["x"], h[:, :, :]).then_inc(*b["dma_out"].one())
        for name in ("dma_out", "dma_conv_out", "dma_state_out"):
            sp.wait_ge(*b[name].now())
        sp.wait_ge(sems["dma_hgp"], 16 * DEPTH)
        for q in range(2):
            sp.wait_ge(sems[f"dma_hout{q}"], 16 * (1 + DEPTH * NS // 2))

    @block.gpsimd
    def _(pool):
        b = book(pool, "pool")
        def padded(x):
            return xp[:, :, 3 + SEQ:XW].rearrange("p m (s t) -> p m s t", s=NS)

        def passed():
            nc.gpsimd.sem_inc(sems["p_step"], 1)

        def conv_ends(l):
            pool.wait_ge(*b["projected"].next())
            passed()
            nc.gpsimd.memset(xp[:, :, 0:3], 0.0)
            pool.wait_ge(*b["dma_conv"].next())
            passed()
            nc.gpsimd.tensor_copy(padded(xp)[:, :, :, 0:3], cin[:, :, :, :]).then_inc(*b["conv_filled"].one())
            pool.wait_ge(*b["dma_conv_out"].now())
            b["dma_conv_out"].skip()
            passed()
            nc.gpsimd.tensor_copy(cout[:, :, 0, :], xp[:, :, SEQ:SEQ + 3])
            nc.gpsimd.tensor_copy(cout[:, :, 1:, :], padded(xp)[:, :, :, C:C + 3]).then_inc(*b["conv_saved"].one())



        with b.loop(DEPTH, "layer") as l:
            for sec in ORDER:
                if sec.name == "merge":
                    conv_ends(l)

                with b.loop(sec.trips, sec.tag) as i:
                    for j, (_, nk, split, r, s) in enumerate(sec.loads):
                        if not split:
                            continue
                        n = nk * P
                        pool.wait_ge(*b[f"hi_ready{s}"].next())
                        pool.wait_ge(sems["tiles_done"], slot_empty(l, sec, i, j))
                        nc.gpsimd.tensor_tensor(w_lo[s][:, 0:n], raw[r][:, 0:n], w_hi[s][:, 0:n].bitcast(F32),
                                                ALU.subtract).then_inc(*b[f"lo_ready{r}"].one())



    @block.scalar
    def _(act):
        b = book(act, "act")
        step = b["a_step"]

        def hi(l, sec, i, j):
            _, nk, split, r, s = sec.loads[j]
            if not split:
                b[f"dma_w{r}"].skip()
                return
            act.wait_ge(*b[f"dma_w{r}"].next())
            act.wait_ge(sems["tiles_done"], slot_empty(l, sec, i, j))
            nc.scalar.activation(w_hi[s][:, 0:nk * P], raw[r][:, 0:nk * P], ACT.Copy).then_inc(
                *b[f"hi_ready{s}"].one())

        def first(l, sec):
            for j in range(sec.lead):
                hi(l, sec, 0, j)

        def dense(l, sec, evacuate):
            with b.passing(sec):
                if sec.trips > 1:
                    with b.loop(sec.trips - 1, sec.tag) as i:
                        for j in range(sec.n):
                            a = j + sec.lead
                            hi(l, sec, i + a // sec.n if a >= sec.n else i, a % sec.n)
                            evacuate(i, j)
                for j in range(sec.n):
                    if j + sec.lead < sec.n:
                        hi(l, sec, sec.trips - 1, j + sec.lead)
                    evacuate(sec.trips - 1, j)

        def tile_done(l, sec, i, j):
            act.wait_ge(sems["tiles_done"], done(l, sec, i, j))

        def squares(src):
            nc.scalar.activation(tmp[:, :, :], src[:, :, :], ACT.Square).then_inc(*b["squares"].one())

        def root():
            act.wait_ge(*b["norm_sum"].next())
            nc.scalar.activation(rms[:, :], mix[:, 0, 0:T], ACT.Sqrt, scale=1.0 / D_MODEL,
                                 bias=eps_c).then_inc(*b["root"].one())

        def gating(l, sec, func):
            def evacuate(i, j):
                q = sec.banks[j]
                if q % 2 == 0:
                    tile_done(l, sec, i, j)
                    act.wait_ge(*b[f"bank_free{q + 1}"].now())
                    b[f"bank_free{q + 1}"].skip()
                    nc.scalar.activation(gate_s[q // 2][:, :], psum[q][:, 0:T], func).then_inc(
                        *b[f"bank_free{q}"].one())
            return evacuate

        def copying(l, sec, to):
            def evacuate(i, j):
                out = to(i, j)
                if out is None:
                    return
                q, dst = out
                tile_done(l, sec, i, j)
                nc.scalar.activation(dst, psum[q][:, 0:T], ACT.Copy).then_inc(*b[f"bank_free{q}"].one())
            return evacuate

        def padded(l, sec, first_tile):
            def evacuate(i, j):
                if sec.name == "tail" and j == 2:
                    tile_done(l, sec, i, j)
                    nc.scalar.activation(rows[:, :], psum[j][0:ROWS, 0:T], ACT.Copy).then_inc(
                        *b[f"bank_free{j}"].one())
                    return
                m = sec.n * i + (first_tile + j)
                tile_done(l, sec, i, j)
                nc.scalar.activation(xp[:, m, 3:3 + SEQ], psum[j][:, 0:SEQ], ACT.Copy)
                nc.scalar.activation(
                    xp[:, m, 3 + SEQ:XW].rearrange("p (s t) -> p s t", s=DEC_BATCH)[:, :, 3:],
                    psum[j][:, SEQ:T].rearrange("p (s t) -> p s t", s=DEC_BATCH), ACT.Copy).then_inc(
                    *b[f"bank_free{j}"].one())
            return evacuate

        def wait_copies():
            for q in range(4):
                act.wait_ge(*b[f"bank_free{q}"].now())

        def rows_and_tokens(l):
            nc.scalar.activation(rt[:, :], rows[:, :], ACT.Sigmoid).then_inc(*step.one())
            act.wait_ge(*step.now())
            act.wait_ge(*b["row_x"].next())
            nc.scalar.activation(re[:, :], rx[:, :], ACT.Abs).then_inc(*step.one())
            act.wait_ge(*step.now())
            nc.scalar.activation(re[:, :], re[:, :], ACT.Exp, scale=-1.0).then_inc(*step.one())
            nc.scalar.activation(lb[0:ROWS, 30:31], vec[0:ROWS, V_RA:V_RA + 1], ACT.Exp).then_inc(*b["row_e"].one())
            act.wait_ge(*b["bound_d"].next())
            nc.scalar.activation(lb[:, 4:12], lb[:, 4:12], ACT.Exp).then_inc(*b["bound_e"].one())
            act.wait_ge(*b["row_u"].next())
            nc.scalar.activation(rl[:, :], ru[:, :], ACT.Ln).then_inc(*b["row_ln"].one())
            for t, (t0, n) in enumerate(TILES3):
                act.wait_ge(*b["tok_t"].next())
                nc.scalar.activation(la_tok[0:n, t, 0:8], psum[t][0:n, 0:8], ACT.Copy)
                nc.scalar.activation(la_tok[0:n, t, 12:16], psum[t][0:n, 32:36], ACT.Copy)
                nc.scalar.activation(beta_tok[0:n, t, :], psum[t][0:n, 64:68], ACT.Copy)
                nc.scalar.activation(dt_tok[0:n, t, :], psum[t][0:n, 128:136], ACT.Copy)
                nc.scalar.activation(la_tok[0:n, t, 8:12], c_["lgam"][0:n, :], ACT.Copy).then_inc(*b["tok_copied"].one())
            act.wait_ge(*b["tok_exp"].next())
            for t, (t0, n) in enumerate(TILES3):
                nc.scalar.activation(to_end[0:n, t, :], to_end[0:n, t, :], ACT.Exp).then_inc(*step.one())
                nc.scalar.activation(ecum_tok[0:n, t, :], cum_tok[0:n, t, :], ACT.Exp).then_inc(*b["tok_ready"].one())

        def convolutions(l):
            act.wait_ge(*b["conv_saved"].next())
            for m in range(NCONV):
                act.wait_ge(*b["conv_sum"].next())
                acc = cacc[m % 2]
                bias = {"bias": vec[:, V_CB + m:V_CB + m + 1]} if m < 6 else {}
                nc.scalar.activation(xp[:, m, 0:SEQ], acc[:, 0:SEQ], ACT.Silu, **bias)
                nc.scalar.activation(xp[:, m, SEQ:T].rearrange("p (s t) -> p s t", s=NS),
                                     acc_sample(acc), ACT.Silu, **bias).then_inc(*b["conv_done"].one())

        def unit_norms(l):
            act.wait_ge(*b["conv_done"].now())
            for half in range(2):
                for e in range(4):
                    if half:
                        act.wait_ge(*b["l2_sum"].now())
                    nc.scalar.activation(lsq[e][:, :], xp[:, 6 + 4 * half + e, 0:T], ACT.Square).then_inc(*b["l2_sq"].one())
                for e in range(4):
                    act.wait_ge(*b["l2_sum"].next())
                    if half and e == 0:
                        b["l2_done"].skip(4)
                        act.wait_ge(*b["l2_done"].now())
                    nc.scalar.activation(lrt[e][:, :], mix[:, e, 0:T], ACT.Sqrt, bias=eps_c).then_inc(*b["l2_root"].one())
            b["l2_done"].skip(4)

        def silus(l):
            for at in (Z, HG, RG, GZ):
                nc.scalar.activation(proj[:, at:at + 4, :], proj[:, at:at + 4, :], ACT.Silu).then_inc(*b["silus"].one())

        def hgrn(l):
            nc.scalar.activation(proj[:, HQ:HQ + 4, :], proj[:, HQ:HQ + 4, :], ACT.Silu).then_inc(*step.one())
            nc.scalar.activation(proj[:, HF:HF + 4, :], proj[:, HF:HF + 4, :], ACT.Sigmoid).then_inc(*b["hg_sig"].one())
            act.wait_ge(*b["hg_f"].next())
            nc.scalar.activation(hc[:, :, :].rearrange("p k t -> p (k t)"), proj[:, HF:HF + 4, :].rearrange("p k t -> p (k t)"),
                                 ACT.Ln).then_inc(*b["hg_ln"].one())
            for d in range(1, C):
                act.wait_ge(*b["pair_d"].next())
                n = 160 * (C - d)
                nc.scalar.activation(he[d % 2][:, 0:n], he[d % 2][:, 0:n], ACT.Exp).then_inc(*b["pair_e"].one())
            act.wait_ge(*b["hg_end_d"].next())
            nc.scalar.activation(he[1][:, :], he[1][:, :], ACT.Exp).then_inc(*step.one())
            nc.scalar.activation(he[0][:, :], hc[:, :, :].rearrange("p k t -> p (k t)"), ACT.Exp).then_inc(*b["hg_end_e"].one())
            for t, (t0, n) in enumerate(TILES3):
                act.wait_ge(*b["kv_t"].next())
                act.wait_ge(*b["dma_tok"].now())
                nc.scalar.activation(ht[0:n, 0:512], psum[0][0:n, :], ACT.Copy)
                nc.scalar.activation(ht[0:n, 512:1024], psum[1][0:n, :], ACT.Copy).then_inc(*b["kv_copied"].one())
                act.wait_ge(*b["kv_copied"].now())
                act.dma_start(tok_scratch[t0:t0 + n, :], ht[0:n, 0:1024]).then_inc(*b["dma_tok"].one())
            act.wait_ge(*b["dma_tok"].now())
            for part, trips, c0 in (("prompt", NCP // 4, 0), ("sample", NS // 4, NCP)):
                if part == "sample":
                    act.wait_ge(sems["hg_s"], l * NC + (1 + NCP))
                    act.dma_start(o["hg_p"][l], hs[0][:, :]).then_inc(*b["dma_hgp"].one())
                with b.loop(trips, f"hg_{part}") as i:
                    for q in range(4):
                        act.wait_ge(*b["hg_o"].next())
                        nc.scalar.activation(hoi[:, :, bass.ds(i * (4 * C) + (c0 + q) * C, C)],
                                             psum[2 + q % 2][:, 0:32].rearrange("p (h t) -> p h t", h=4),
                                             ACT.Copy).then_inc(*b["hg_oi"].one())
                        if part == "sample":
                            act.wait_ge(sems["hg_s"], l * NC + (i * 4 + (1 + NCP + q + 1)))
                            act.dma_start(o["hg_s"][l, 4 * i + q], hs_out[q % 2][:, :]).then_inc(*b[f"dma_hout{q % 2}"].one())
            f_norm(1.0 / P, 4, ho_k, he_v=True)

        def f_norm(scale, banks, src, he_v=False):
            act.wait_ge(*b["f_pre"].next())
            sq, rtv = (hx[0][:, :], hx[1][:, :]) if he_v else (f_sq, f_rt)
            nc.scalar.activation(sq.rearrange("p (k t) -> p k t", k=4), src, ACT.Square).then_inc(*b["f_sq"].one())
            act.wait_ge(*b["f_sum"].next())
            if banks == 4:
                nc.scalar.activation(rtv.rearrange("p (k t) -> p k t", k=4), mix[:, :, 0:T], ACT.Sqrt, scale=scale,
                                     bias=eps_c).then_inc(*b["f_root"].one())
            else:
                nc.scalar.activation(rtv[:, 0:T], mix[:, 0, 0:T], ACT.Sqrt, scale=scale, bias=eps_c).then_inc(
                    *b["f_root"].one())

        def scalar_decay(l):
            act.wait_ge(*b["hg_finished"].next())
            for kind, g in GROUPS:
                if kind == "gdn":
                    act.wait_ge(*b["f_root"].now())
                for t, (t0, n) in enumerate(TILES3):
                    act.wait_ge(*b["cum_bc"].next())
                    nc.scalar.activation(ecb[:, 0:4 * n], psum[0][:, 0:4 * n], ACT.Exp).then_inc(*b["ecb_ready"].one())
                    act.wait_ge(*b["dec_d"].next())
                    nc.scalar.activation(em[0:n, 0:4 * n], dm[0:n, 0:4 * n], ACT.Exp).then_inc(*b["dec_e"].one())
                    if kind == "gdn":
                        nc.scalar.activation(dm2[0:n, 0:4 * n], dm2[0:n, 0:4 * n], ACT.Exp, scale=-1.0).then_inc(
                            *b["dec_e"].one())
                    act.wait_ge(*b["scores"].next())
                    w = 256 if kind == "mb" else 512
                    nc.scalar.activation(vtok[0:n, 0:w], psum[3][0:n, 0:w], ACT.Copy).then_inc(*b["v_copied"].one())
                    if kind == "gdn":
                        def copy(dst, src, **kw):
                            act.wait_ge(*b["gdn_mm"].next())
                            nc.scalar.activation(dst, src, ACT.Copy, **kw).then_inc(*b["gdn_ev"].one())
                        m = 4 * n
                        copy(W[2][0:n, 0:m], psum[1][0:n, 0:m])
                        b["gdn_mm"].skip()
                        copy(W[5][0:n, 0:m], psum[2][0:n, 0:m])
                        b["gdn_mm"].skip()
                        copy(W[4][0:n, 0:m], psum[2][0:n, 0:m])
                        copy(W[2][0:n, 0:m], psum[1][0:n, 0:m])
                        if t < 2:
                            copy(W[5][0:n, 0:m], psum[2][0:n, 0:m])
                            for m2 in (16, 32, 64, 128):
                                copy(W[6][0:n, 0:m], psum[1][0:n, 0:m])
                                b["gdn_mm"].skip()
                                if m2 < 128:
                                    copy(W[5][0:n, 0:m], psum[1][0:n, 0:m])
                        if t:
                            copy(nsk[:, 0:m], psum[1][:, 0:m], scale=-1.0)
                        if t < 2:
                            copy(wn[0:n, :], psum[2][0:n, :])
                        else:
                            copy(W[6][:, 0:m], psum[2][:, 0:m])
                            copy(wn[0:n, :], psum[1][0:n, :])
                    act.wait_ge(*b["o_done"].next())
                    if kind == "mb":
                        nc.scalar.activation(f_o.rearrange("p (k t) -> p k t", k=4)[:, 2 * g:2 * g + 2, t0:t0 + n],
                                             mix[:, 0, 0:2 * n].rearrange("p (k t) -> p k t", k=2), ACT.Copy).then_inc(
                            *b["o_copied"].one())
                    elif kind == "gdn":
                        nc.scalar.activation(xp[:, 0:4, t0:t0 + n], mix[:, 0, 0:4 * n].rearrange("p (k t) -> p k t", k=4),
                                             ACT.Copy).then_inc(*b["o_copied"].one())
                    else:
                        for r in range(2):
                            nc.scalar.activation(xp[:, r:4:2, t0:t0 + n],
                                                 mix[:, r, 0:2 * n].rearrange("p (k t) -> p k t", k=2),
                                                 ACT.Copy).then_inc(*b["o_copied"].one())
                if (kind, g) != ("mb", 0):
                    if kind == "mb":
                        f_norm(1.0 / 512, 1, f_ok)
                    else:
                        f_norm(1.0 / P, 4, xp[:, 0:4, 0:T])

        nc.scalar.sem_inc(sems["hg_oi"], 1)
        act.wait_ge(b["dma_in"].sem, 32)
        with b.loop(DEPTH, "layer") as l:
            for f in range(2):
                up, down = sections[f"up{f}"], sections[f"down{f}"]
                first(l, up)
                if f == 0:
                    act.wait_ge(*b["h_ready"].now())
                squares(h)
                root()
                dense(l, up, gating(l, up, ACT.Silu))
                first(l, down)
                dense(l, down, copying(l, down, lambda i, j: (j // 3, y[:, 4 * i + j // 3, :]) if j % 3 == 2 else None))
                wait_copies()
                if f == 0:
                    first(l, sections["proj0"])
                squares(y)
                root()
                b["h_ready"].skip()
                if f == 1:
                    continue
                act.wait_ge(*b["h_ready"].now())
                squares(h)
                root()
                sec = sections["proj0"]
                dense(l, sec, copying(l, sec, lambda i, j: (j, proj[:, 4 * i + j, :])))
                sec = sections["conv0"]
                first(l, sec)
                dense(l, sec, padded(l, sec, 0))
                sec = sections["tail0"]
                first(l, sec)
                dense(l, sec, padded(l, sec, 16))
                wait_copies()
                nc.scalar.sem_inc(sems["projected"], 1)
                rows_and_tokens(l)
                convolutions(l)
                unit_norms(l)
                silus(l)
                hgrn(l)
                scalar_decay(l)
                sec = sections["merge0"]
                first(l, sec)
                dense(l, sec, gating(l, sec, ACT.Sigmoid))
                sec = sections["out0"]
                first(l, sec)
                dense(l, sec, copying(l, sec, lambda i, j: (j, y[:, 4 * i + j, :])))
                wait_copies()
                squares(y)
                root()
                b["h_ready"].skip()
                act.wait_ge(*b["h_ready"].now())

    @block.vector
    def _(dve):
        b = book(dve, "dve")
        step = b["v_step"]

        def inverse_root():
            dve.wait_ge(*b["squares"].next())
            nc.vector.tensor_reduce(ssq[:, :], tmp[:, :, :].rearrange("p k t -> p t k"), AX_X,
                                    ALU.add).then_inc(*b["sums"].one())
            dve.wait_ge(*b["root"].next())
            nc.vector.reciprocal(rinv[:, :], rms[:, :]).then_inc(*step.one())

        def norm_in(g):
            inverse_root()
            dve.wait_ge(*step.now())
            for k in range(KD):
                nc.vector.scalar_tensor_tensor(out=tmp[:, k, :], in0=h[:, k, :], scalar=vec[:, g * KD + k:g * KD + k + 1],
                                               in1=rinv[:, :], op0=ALU.mult, op1=ALU.mult).then_inc(*step.one())
            for k in range(KD):
                if k == 0:
                    dve.wait_ge(*step.now())
                nc.vector.tensor_copy(u_hi[:, k, :], tmp[:, k, :]).then_inc(*step.one())
                dve.wait_ge(*step.now())
                nc.vector.tensor_tensor(u_lo[:, k, :], tmp[:, k, :], u_hi[:, k, :].bitcast(F32),
                                        ALU.subtract).then_inc(*b["u_ready"].one())

        def norm_out(g, half):
            inverse_root()
            if half:
                dve.wait_ge(*step.now())
                nc.vector.tensor_scalar(rinv[:, :], rinv[:, :], 0.5, None, ALU.mult).then_inc(*step.one())
            dve.wait_ge(*step.now())
            for k in range(KD):
                nc.vector.scalar_tensor_tensor(out=tmp[:, k, :], in0=y[:, k, :], scalar=vec[:, g * KD + k:g * KD + k + 1],
                                               in1=rinv[:, :], op0=ALU.mult, op1=ALU.mult).then_inc(*step.one())
            dve.wait_ge(*step.now())
            nc.vector.tensor_tensor(h[:, :, :], h[:, :, :], tmp[:, :, :], ALU.add).then_inc(*b["h_ready"].one())
            dve.wait_ge(*b["h_ready"].now())

        def gated(l, sec, i, j):
            q = sec.banks[j]
            dve.wait_ge(*b[f"bank_free{q - 1}"].next())
            dve.wait_ge(sems["tiles_done"], done(l, sec, i, j))
            nc.vector.tensor_tensor(hid_t[q // 2][:, :], gate_s[q // 2][:, :], psum[q][:, 0:T],
                                    ALU.mult).then_inc(*b[f"bank_free{q}"].one())
            dve.wait_ge(*b[f"bank_free{q}"].now())
            return hid_t[q // 2][:, :]

        def hidden(l, f):
            sec = sections[f"up{f}"]
            with b.passing(sec), b.loop(sec.trips, sec.tag) as i:
                for m in range(2):
                    t = gated(l, sec, i, 2 * m + 1)
                    nc.vector.tensor_copy(hid_hi[:, 2 * i + m, :], t).then_inc(*step.one())
                    dve.wait_ge(*step.now())
                    nc.vector.tensor_tensor(hid_lo[:, 2 * i + m, :], t, hid_hi[:, 2 * i + m, :].bitcast(F32),
                                            ALU.subtract).then_inc(*b["hid_ready"].one())
            with b.passing(sections[f"down{f}"]):
                pass


        def rows_and_tokens(l):
            V = nc.vector
            V.tensor_scalar(rx[:, :], rows[:, :], vec[0:ROWS, V_RB:V_RB + 1], None, ALU.add).then_inc(*b["row_x"].one())
            V.tensor_tensor(lb[:, 0:4], vec[:, V_LB:V_LB + 4], vec[:, V_LB + 4:V_LB + 8], ALU.max).then_inc(*step.one())
            dve.wait_ge(*step.now())
            for x in range(2):
                V.tensor_tensor(lb[:, 4 + 4 * x:8 + 4 * x], vec[:, V_LB + 4 * x:V_LB + 4 * x + 4], lb[:, 0:4],
                                ALU.subtract).then_inc(*(step if x == 0 else b["bound_d"]).one())
            dve.wait_ge(*b["row_e"].next())
            V.tensor_scalar(ru[:, :], re[:, :], 1.0, None, ALU.add).then_inc(*b["row_u"].one())
            fix, inv = cacc[0][0:ROWS, 0:T], cacc[1][0:ROWS, 0:T]
            dve.wait_ge(*b["row_u"].now())
            V.tensor_scalar(fix, ru[:, :], -1.0, None, ALU.add).then_inc(*step.one())
            V.reciprocal(inv, ru[:, :]).then_inc(*step.one())
            V.tensor_scalar(rx[:, :], rx[:, :], 0.0, None, ALU.max).then_inc(*step.one())
            dve.wait_ge(*step.now())
            V.tensor_tensor(fix, fix, re[:, :], ALU.subtract).then_inc(*step.one())
            dve.wait_ge(*step.now())
            V.tensor_tensor(fix, fix, inv, ALU.mult).then_inc(*step.one())
            dve.wait_ge(*b["row_ln"].next())
            V.tensor_tensor(rl[:, :], rl[:, :], rx[:, :], ALU.add).then_inc(*step.one())
            dve.wait_ge(*step.now())
            V.tensor_tensor(rl[:, :], rl[:, :], fix, ALU.subtract).then_inc(*step.one())
            dve.wait_ge(*step.now())
            V.tensor_scalar(rb[0:64, :], rl[0:64, :], lb[0:64, 30:31], -1.0, ALU.mult, ALU.mult)
            V.tensor_copy(rb[64:ROWS, :], rt[64:ROWS, :]).then_inc(*b["rows_ready"].one())
            dve.wait_ge(*b["bound_e"].next())
            V.tensor_tensor(lb[:, 12:16], lb[:, 4:8], lb[:, 8:12], ALU.add).then_inc(*step.one())
            dve.wait_ge(*step.now())
            V.reciprocal(lb[:, 12:16], lb[:, 12:16]).then_inc(*step.one())
            dve.wait_ge(*step.now())
            V.tensor_tensor(lb[:, 16:20], lb[:, 4:8], lb[:, 12:16], ALU.mult)
            V.tensor_tensor(lb[:, 20:24], lb[:, 8:12], lb[:, 12:16], ALU.mult).then_inc(*step.one())
            dve.wait_ge(*step.now())
            V.tensor_tensor(lb[:, 24:28], lb[:, 16:20], lb[:, 20:24], ALU.add).then_inc(*step.one())
            dve.wait_ge(*step.now())
            V.tensor_tensor(lb[:, 24:28], lb[:, 24:28], lb[:, 16:20], ALU.subtract).then_inc(*step.one())
            dve.wait_ge(*step.now())
            V.tensor_scalar(lb[:, 24:28], lb[:, 24:28], vec[:, V_ON:V_ON + 1], None, ALU.mult).then_inc(*step.one())
            dve.wait_ge(*step.now())
            V.tensor_scalar(lb[:, 20:24], lb[:, 24:28], -1.0, 1.0, ALU.mult, ALU.add).then_inc(*step.one())
            for t, (t0, n) in enumerate(TILES3):
                dve.wait_ge(*b["tok_sums"].next())
                V.tensor_copy(cum_tok[0:n, t, :], psum[t][0:n, 0:16]).then_inc(*step.one())
            dve.wait_ge(*step.now())
            for t, (t0, n) in enumerate(TILES3):
                V.tensor_tensor(to_end[0:n, t, :], psum[t][0:n, 16:32], cum_tok[0:n, t, :], ALU.subtract).then_inc(
                    *(step if t < 2 else b["tok_exp"]).one())
            for t, (t0, n) in enumerate(TILES3):
                dve.wait_ge(*b["tok_ready"].next())
                V.tensor_tensor(to_end_dt[0:n, t, :], to_end[0:n, t, 0:8], dt_tok[0:n, t, :], ALU.mult)
                V.tensor_tensor(beta_cum[0:n, t, :], ecum_tok[0:n, t, 12:16], beta_tok[0:n, t, :], ALU.mult).then_inc(*step.one())

        def convolutions(l):
            dve.wait_ge(*b["conv_filled"].next())
            n = XW - 3
            for m in range(0, NCONV, 2):
                for j in range(4):
                    for e in range(2):
                        tap = vec[:, V_CW + 4 * (m + e) + j:V_CW + 4 * (m + e) + j + 1]
                        src, acc = xp[:, m + e, j:j + n], cacc[e][:, 0:n]
                        if j == 0:
                            if m:
                                dve.wait_ge(*b["conv_done"].next())
                            nc.vector.tensor_scalar(acc, src, tap, None, ALU.mult).then_inc(*step.one())
                            continue
                        own, at = step.now()
                        dve.wait_ge(own, at - ((j, e) != (3, 1)))
                        nc.vector.scalar_tensor_tensor(out=acc, in0=src, scalar=tap, in1=acc, op0=ALU.mult,
                                                       op1=ALU.add).then_inc(*(step if j < 3 else b["conv_sum"]).one())
            b["conv_done"].skip(2)

        def unit_norms(l):
            for half in range(2):
                for e in range(4):
                    dve.wait_ge(*b["l2_root"].next())
                    nc.vector.reciprocal(lrt[e][:, :], lrt[e][:, :]).then_inc(*step.one())
                    x = xp[:, 6 + 4 * half + e, 0:T]
                    dve.wait_ge(*step.now())
                    if half:
                        nc.vector.tensor_tensor(x, x, lrt[e][:, :], ALU.mult).then_inc(*b["l2_done"].one())
                    else:
                        nc.vector.scalar_tensor_tensor(out=x, in0=x, scalar=P ** -0.5, in1=lrt[e][:, :], op0=ALU.mult,
                                                       op1=ALU.mult).then_inc(*b["l2_done"].one())

        def hgrn(l):
            V = nc.vector
            dve.wait_ge(*b["hg_sig"].next())
            for k in range(4):
                V.tensor_scalar(proj[:, HF + k, :], proj[:, HF + k, :], lb[:, 20 + k:21 + k], lb[:, 24 + k:25 + k],
                                ALU.mult, ALU.add).then_inc(*(step if k < 3 else b["hg_f"]).one())
            dve.wait_ge(*b["hg_ln"].next())
            V.tensor_scalar(hf, hf, -1.0, 1.0, ALU.mult, ALU.add).then_inc(*step.one())
            for t in range(1, C):
                if t > 1:
                    dve.wait_ge(*step.now())
                V.tensor_tensor(hc[:, :, t], hc[:, :, t], hc[:, :, t - 1], ALU.add).then_inc(*step.one())
            dve.wait_ge(*step.now())

            def pairs(x, d):
                return x[:, 0:160 * (C - d)].rearrange("p (c t) -> p c t", t=C - d)

            def difference(d):
                V.tensor_tensor(pairs(he[d % 2], d), hc[:, :, d:C], hc[:, :, 0:C - d], ALU.subtract).then_inc(
                    *b["pair_d"].one())

            def consume(d):
                n = C - d
                dve.wait_ge(*b["pair_a"].next())
                score = mix[:, :, 0:40 * n].rearrange("p k (c t) -> p k c t", t=n)
                value = proj[:, HI:HI + 4, :].rearrange("p k (c t) -> p k c t", t=C)[:, :, :, 0:n]
                if d == 0:
                    V.tensor_tensor(ho[:, :, :].rearrange("p (k c) t -> p k c t", k=4), score, value, ALU.mult).then_inc(
                        *b["pair_t"].one())
                    return
                dve.wait_ge(*step.now())
                V.tensor_tensor(ht[:, 0:160 * n].rearrange("p (k c t) -> p k c t", k=4, t=n), score, value,
                                ALU.mult).then_inc(*b["pair_t"].one())
                dve.wait_ge(*b["pair_t"].now())
                V.tensor_tensor(ho[:, :, d:C], ho[:, :, d:C], pairs(ht, d), ALU.add).then_inc(*step.one())

            V.tensor_tensor(hx[0][:, :].rearrange("p (c t) -> p c t", t=C), hq, hf, ALU.mult).then_inc(*b["pair_x"].one())
            dve.wait_ge(*b["dma_conv_out"].next())
            difference(1)
            for d in range(1, C):
                if d < C - 1:
                    dve.wait_ge(*b["pair_x"].now())
                    difference(d + 1)
                V.tensor_tensor(pairs(hx[d % 2], d), hq[:, :, d:C], hf[:, :, 0:C - d], ALU.mult).then_inc(*step.one())
                dve.wait_ge(*b["pair_e"].next())
                dve.wait_ge(*step.now())
                V.tensor_tensor(pairs(hx[d % 2], d), pairs(hx[d % 2], d), pairs(he[d % 2], d), ALU.mult).then_inc(
                    *b["pair_x"].one())
                consume(d - 1)
            dve.wait_ge(*b["pair_x"].now())
            V.tensor_tensor(pairs(he[1], 0), over(hc[:, :, C - 1:C], [P, 160, C]), hc[:, :, :], ALU.subtract).then_inc(
                *b["hg_end_d"].one())
            consume(C - 1)
            V.memset(hs[0][:, :], 0.0).then_inc(*step.one())
            dve.wait_ge(*b["hg_end_e"].next())
            V.tensor_tensor(hq, hq, pairs(he[0], 0), ALU.mult)
            V.tensor_tensor(hf, hf, pairs(he[1], 0), ALU.mult)
            V.tensor_copy(fade_v, pairs(he[0], 0)[:, :, C - 1]).then_inc(*b["hg_ready"].one())
            with b.loop(NCP // 4, "hg_prompt") as i:
                for q in range(4):
                    dve.wait_ge(*b["hg_kv"].next())
                    dve.wait_ge(*b["hg_o"].now())
                    b["hg_o"].skip()
                    dve.wait_ge(*b["hg_s"].now())
                    for k in range(4):
                        up = V.scalar_tensor_tensor(
                            out=hs[(q + 1) % 2][:, k * P:(k + 1) * P], in0=hs[q % 2][:, k * P:(k + 1) * P],
                            scalar=fade[:, k, bass.ds(i * 4 + q, 1)], in1=mix[:, q, k * P:(k + 1) * P],
                            op0=ALU.mult, op1=ALU.add)
                    up.then_inc(*b["hg_s"].one())
            with b.loop(NS // 4, "hg_sample") as i:
                for q in range(4):
                    dve.wait_ge(*b["hg_kv"].next())
                    dve.wait_ge(*b["hg_o"].next())
                    dve.wait_ge(*b[f"dma_hin{q % 2}"].next())
                    dve.wait_ge(*b[f"dma_hout{q % 2}"].now())
                    b[f"dma_hout{q % 2}"].skip()
                    for k in range(4):
                        up = V.scalar_tensor_tensor(
                            out=hs_out[q % 2][:, k * P:(k + 1) * P], in0=hs_in[q % 2][:, k * P:(k + 1) * P],
                            scalar=fade[:, k, bass.ds(i * 4 + (NCP + q), 1)], in1=mix[:, q, k * P:(k + 1) * P],
                            op0=ALU.mult, op1=ALU.add)
                    up.then_inc(*b["hg_s"].one())
            b["hg_oi"].skip(NC)
            dve.wait_ge(*b["hg_oi"].now())
            V.tensor_tensor(ho[:, :, :].rearrange("p c t -> p (c t)"), ho[:, :, :].rearrange("p c t -> p (c t)"),
                            hoi[:, :, :].rearrange("p k t -> p (k t)"), ALU.add).then_inc(*b["f_pre"].one())
            dve.wait_ge(*b["f_root"].next())
            V.reciprocal(hx[1][:, :], hx[1][:, :]).then_inc(*step.one())
            b["silus"].skip(4)
            dve.wait_ge(*b["silus"].now())
            dve.wait_ge(*step.now())
            V.scalar_tensor_tensor(out=ho_k, in0=ho_k, scalar=vec[:, V_HN:V_HN + 1],
                                   in1=hx[1][:, :].rearrange("p (k t) -> p k t", k=4), op0=ALU.mult, op1=ALU.mult).then_inc(*step.one())
            dve.wait_ge(*step.now())
            V.tensor_tensor(proj[:, HG:HG + 4, :], proj[:, HG:HG + 4, :], ho_k, ALU.mult).then_inc(*step.one())
            dve.wait_ge(*b["dma_hgp"].next())
            for q in range(2):
                dve.wait_ge(*b[f"dma_hout{q}"].now())
            dve.wait_ge(*step.now())
            V.sem_inc(sems["hg_finished"], 1)

        def rotate(l):
            dve.wait_ge(*b["rot_ps"].next())
            turned = f_sq.rearrange("p (k t) -> p k t", k=4)
            x = proj[:, RQ:RQ + 4, :]
            nc.vector.tensor_tensor(turned, mix[:, :, 0:T], over(c_["sin"].unsqueeze(1), [P, 4, T]), ALU.mult)
            nc.vector.tensor_tensor(x, x, over(c_["cos"].unsqueeze(1), [P, 4, T]), ALU.mult).then_inc(*step.one())
            dve.wait_ge(*step.now())
            nc.vector.tensor_tensor(x, x, turned, ALU.add).then_inc(*step.one())
            dve.wait_ge(*step.now())
            nc.vector.tensor_scalar(proj[:, RK:RK + 2, :], proj[:, RK:RK + 2, :], 64 ** -0.5, None, ALU.mult).then_inc(
                *b["rotated"].one())

        def by_head(x, n):
            return x.rearrange("p (k i) -> p k i", i=n)

        def odd_even(x, n, r):
            return x.rearrange("p (k r i) -> p r k i", r=2, i=n)[:, r]

        def delta_rule(t, t0, n):
            V, m = nc.vector, 4 * n
            heads = lambda i: by_head(W[i][0:n, 0:m], n)
            eye = over(c_["ident"][0:n, 0:n].unsqueeze(1), [n, 4, n])
            dve.wait_ge(*b["dec_e"].next())
            for k in range(4):
                V.scalar_tensor_tensor(out=W[0][0:n, k * n:(k + 1) * n], in0=psum[2][0:n, k * n:(k + 1) * n],
                                       scalar=beta_tok[0:n, t, k:k + 1], in1=dm2[0:n, k * n:(k + 1) * n], op0=ALU.mult,
                                       op1=ALU.mult).then_inc(*(step if t < 2 or k < 3 else b["gdn_v"]).one())
            if t < 2:
                dve.wait_ge(*step.now())
                V.tensor_tensor(heads(1), heads(0), over(c_["b8"].unsqueeze(1), [n, 4, n]), ALU.mult).then_inc(
                    *b["gdn_v"].one())
            dve.wait_ge(*b["gdn_ev"].next())
            V.tensor_tensor(heads(3), eye, heads(2), ALU.subtract).then_inc(*step.one())
            b["gdn_mm"].skip()
            dve.wait_ge(*b["gdn_mm"].next())
            V.tensor_copy(W[4][0:n, 0:m], psum[1][0:n, 0:m]).then_inc(*b["gdn_v"].one())
            dve.wait_ge(*b["gdn_ev"].next())
            V.tensor_tensor(heads(6), eye, heads(5), ALU.add).then_inc(*step.one())
            b["gdn_mm"].skip()
            dve.wait_ge(*b["gdn_mm"].next())
            V.tensor_tensor(heads(1), eye, by_head(psum[1][0:n, 0:m], n), ALU.add).then_inc(*b["gdn_v"].one())
            b["gdn_mm"].skip(2)
            b["gdn_ev"].skip(2)
            if t < 2:
                b["gdn_mm"].skip()
                b["gdn_ev"].skip()
                for m2 in (16, 32, 64, 128):
                    dve.wait_ge(*b["gdn_mm"].now())
                    V.tensor_tensor(heads(1), heads(0), over(c_[f"b{m2}"].unsqueeze(1), [n, 4, n]), ALU.mult).then_inc(
                        *b["gdn_v"].one())
                    b["gdn_mm"].skip()
                    b["gdn_ev"].skip()
                    dve.wait_ge(*b["gdn_mm"].next())
                    V.tensor_tensor(W[2][0:n, 0:m], W[2][0:n, 0:m], psum[2][0:n, 0:m], ALU.subtract).then_inc(
                        *b["gdn_v"].one())
                    if m2 < 128:
                        b["gdn_mm"].skip()
                        b["gdn_ev"].skip()
            b["gdn_mm"].skip(1 + (t > 0) + (t == 2))
            b["gdn_ev"].skip(1 + (t > 0) + (t == 2))

        def new_state(kind, g, t, n):
            V = nc.vector
            at = {"mb": 0, "ret": 256, "gdn": 0}[kind]
            width = 64 if kind == "mb" else P
            own = {"mb": MB, "ret": RET, "gdn": GDN}[kind]

            def place(k):
                if kind == "mb":
                    return slice(64 * g, 64 * g + 64), k
                if kind == "ret":
                    return slice(64 * (k % 2), 64 * (k % 2) + 64), k // 2
                return slice(0, P), k

            if t < 2:
                dve.wait_ge(*b["state_mm"].next())
                for k in range(4):
                    pr, pos = place(k)
                    dst, src = state[own][pr, pos, :], mix[pr, 3, pos * width:(pos + 1) * width]
                    if t == 0:
                        up = V.tensor_copy(dst, src)
                    else:
                        up = V.scalar_tensor_tensor(out=dst, in0=dst, scalar=ecb[pr, k * n + n - 1:k * n + n], in1=src,
                                                    op0=ALU.mult, op1=ALU.add)
                    up.then_inc(*(step if k < 3 else b["state_new"]).one())
                return

            def masked(k):
                src = wn if kind == "gdn" else vtok
                V.tensor_tensor(vm[k % 2][:, 0:NS * width].rearrange("p (s d) -> p s d", s=NS),
                                over(src[0:n, k * width:(k + 1) * width].unsqueeze(1), [n, NS, width]),
                                over(c_["pick"][0:n, :].unsqueeze(2), [n, NS, width]), ALU.mult).then_inc(
                    *b["vm_ready"].one())

            dve.wait_ge(*b["o_done"].now())
            masked(0)
            masked(1)
            for k in range(4):
                pr, pos = place(k)
                dst = st_s[pr, :, at + pos * width:at + (pos + 1) * width]
                rows_ = pr.stop - pr.start
                V.tensor_tensor(dst, dst, over(ecb[pr, k * n:(k + 1) * n].rearrange("p (s t) -> p s t", t=C)[:, :, C - 1:C],
                                               [rows_, NS, width]), ALU.mult).then_inc(*step.one())
                dve.wait_ge(*b["state_mm"].next())
                dve.wait_ge(*step.now())
                bank = 2 if k % 2 == 0 else 0
                kvs = mix[pr, bank:bank + NS * width // 512, :].rearrange("p b f -> p (b f)").rearrange("p (s d) -> p s d", s=NS)
                V.tensor_tensor(dst, dst, kvs, ALU.add).then_inc(*(step if k < 3 else b["state_new"]).one())
                if k < 2:
                    masked(k + 2)

        def scalar_decay(l):
            V = nc.vector
            rotate(l)
            for kind, g in GROUPS:
                col = {"mb": 4 * g, "ret": RET, "gdn": GDN}[kind]
                if (kind, g) == ("mb", 0):
                    b["dma_state"].skip(2)
                if kind == "gdn":
                    b["dma_state"].skip()
                for t, (t0, n) in enumerate(TILES3):
                    m = 4 * n
                    dve.wait_ge(*b["ecb_ready"].next())
                    neg, pos = (c_["neg"], c_["pos"]) if t < 2 else (c_["neg_s"][0:n, :], c_["pos_s"][0:n, :])
                    for k in range(4):
                        cum = cum_tok[0:n, t, col + k:col + k + 1]
                        src, sl = psum[0][0:n, k * n:(k + 1) * n], slice(k * n, (k + 1) * n)
                        last = V.scalar_tensor_tensor(out=dm[0:n, sl], in0=src, scalar=cum, in1=neg, op0=ALU.subtract,
                                                      op1=ALU.add)
                        if kind == "gdn":
                            last = V.scalar_tensor_tensor(out=dm2[0:n, sl], in0=src, scalar=cum, in1=pos,
                                                          op0=ALU.subtract, op1=ALU.add)
                    last.then_inc(*b["dec_d"].one())
                    dve.wait_ge(*b["scores"].next())
                    dve.wait_ge(*b["dec_e"].next())
                    if kind == "mb":
                        for k in range(4):
                            V.scalar_tensor_tensor(out=pm[0:n, k * n:(k + 1) * n], in0=psum[1][0:n, 0:n],
                                                   scalar=dt_tok[0:n, t, col + k:col + k + 1],
                                                   in1=em[0:n, k * n:(k + 1) * n], op0=ALU.mult, op1=ALU.mult).then_inc(
                                *(step if k < 3 else b["p_ready"]).one())
                    elif kind == "ret":
                        for r in range(2):
                            V.tensor_tensor(odd_even(pm[0:n, 0:m], n, r), by_head(psum[1 + r][0:n, 0:2 * n], n),
                                            odd_even(em[0:n, 0:m], n, r), ALU.mult).then_inc(
                                *(step if r == 0 else b["p_ready"]).one())
                    else:
                        V.tensor_tensor(pm[0:n, 0:m], psum[1][0:n, 0:m], em[0:n, 0:m], ALU.mult).then_inc(*b["p_ready"].one())
                    if t:
                        if kind == "mb":
                            pr = slice(64 * g, 64 * g + 64)
                            V.tensor_tensor(by_head(qd[pr, 0:m], n), over(xp[pr, 5, t0:t0 + n].unsqueeze(1), [64, 4, n]),
                                            by_head(ecb[pr, 0:m], n), ALU.mult).then_inc(*b["q_ready"].one())
                        elif kind == "ret":
                            for r in range(2):
                                pr = slice(64 * r, 64 * r + 64)
                                V.tensor_tensor(odd_even(qd[pr, 0:m], n, r), proj[pr, RQ:RQ + 2, t0:t0 + n],
                                                odd_even(ecb[pr, 0:m], n, r), ALU.mult).then_inc(
                                    *(step if r == 0 else b["q_ready"]).one())
                        else:
                            V.tensor_tensor(by_head(qd[:, 0:m], n), xp[:, 6:10, t0:t0 + n], by_head(ecb[:, 0:m], n),
                                            ALU.mult).then_inc(*b["q_ready"].one())
                    if kind == "mb":
                        V.tensor_tensor(by_head(kend[0:n, 0:256], 64), over(mix[0:n, 2, 64 * g:64 * g + 64].unsqueeze(1), [n, 4, 64]),
                                        over(to_end_dt[0:n, t, col:col + 4].unsqueeze(2), [n, 4, 64]), ALU.mult).then_inc(
                            *b["k_ready"].one())
                    elif kind == "ret":
                        V.tensor_tensor(by_head(kend[0:n, 0:256], 64), by_head(mix[0:n, 2, 0:256], 64),
                                        over(to_end[0:n, t, RET:RET + 4].unsqueeze(2), [n, 4, 64]), ALU.mult).then_inc(
                            *b["k_ready"].one())
                    else:
                        keys = by_head(mix[0:n, 2, :], P)
                        V.tensor_tensor(by_head(kend[0:n, :], P), keys, over(to_end[0:n, t, GDN:GDN + 4].unsqueeze(2), [n, 4, P]),
                                        ALU.mult)
                        V.tensor_tensor(by_head(kb[0:n, :], P), keys, over(beta_cum[0:n, t, :].unsqueeze(2), [n, 4, P]),
                                        ALU.mult).then_inc(*b["k_ready"].one())
                        dve.wait_ge(*b["v_copied"].now())
                    b["v_copied"].skip()
                    if kind == "gdn":
                        dve.wait_ge(*b["v_copied"].now())
                        V.tensor_tensor(by_head(vb[0:n, :], P), by_head(vtok[0:n, :], P),
                                        over(beta_tok[0:n, t, :].unsqueeze(2), [n, 4, P]), ALU.mult).then_inc(*step.one())
                        delta_rule(t, t0, n)
                    b["o_done"].skip()
                    if t == 2:
                        dve.wait_ge(*b["v_copied"].now())
                        dve.wait_ge(*b["dma_state"].now())
                    new_state(kind, g, t, n)
                    b["o_copied"].skip(2 if kind == "ret" else 1)
                if (kind, g) == ("mb", 0):
                    continue
                dve.wait_ge(*b["o_copied"].now())
                if kind == "mb":
                    for k in range(4):
                        V.scalar_tensor_tensor(out=f_ok[:, k], in0=xp[:, k, 0:T], scalar=vec[:, V_D + k:V_D + k + 1],
                                               in1=f_ok[:, k], op0=ALU.mult, op1=ALU.add).then_inc(*step.one())
                    dve.wait_ge(*step.now())
                    V.tensor_tensor(f_ok, f_ok, proj[:, Z:Z + 4, :], ALU.mult).then_inc(*b["f_pre"].one())
                    dve.wait_ge(*b["f_root"].next())
                    V.reciprocal(f_rt[:, 0:T], f_rt[:, 0:T]).then_inc(*step.one())
                    dve.wait_ge(*step.now())
                    for k in range(4):
                        V.scalar_tensor_tensor(out=proj[:, Z + k, :], in0=f_ok[:, k], scalar=vec[:, V_MN + k:V_MN + k + 1],
                                               in1=f_rt[:, 0:T], op0=ALU.mult, op1=ALU.mult).then_inc(*step.one())
                    continue
                dve.wait_ge(*b["state_new"].now())
                V.sem_inc(sems["f_pre"], 1)
                b["f_pre"].skip()
                dve.wait_ge(*b["f_root"].next())
                V.reciprocal(f_rt, f_rt).then_inc(*step.one())
                dve.wait_ge(*step.now())
                out, gate = xp[:, 0:4, 0:T], RG if kind == "ret" else GZ
                root = f_rt.rearrange("p (k t) -> p k t", k=4)
                if kind == "ret":
                    V.tensor_tensor(root, out, root, ALU.mult).then_inc(*step.one())
                else:
                    V.scalar_tensor_tensor(out=root, in0=out, scalar=vec[:, V_GN:V_GN + 1], in1=root, op0=ALU.mult,
                                           op1=ALU.mult).then_inc(*step.one())
                    b["dma_state_out"].skip(6)
                    dve.wait_ge(*b["dma_state_out"].now())
                dve.wait_ge(*step.now())
                V.tensor_tensor(proj[:, gate:gate + 4, :], proj[:, gate:gate + 4, :], root, ALU.mult).then_inc(
                    *(step if kind == "ret" else b["y_ready"]).one())

        nc.vector.sem_inc(sems["hg_s"], 1)
        b["hg_s"].skip()
        b["hg_oi"].skip()
        b["hg_kv"].skip(3)
        dve.wait_ge(b["dma_in"].sem, 32)
        with b.loop(DEPTH, "layer") as l:
            dve.wait_ge(*b["dma_vec"].next())
            norm_in(0)
            hidden(l, 0)
            norm_out(1, True)
            norm_in(2)
            for sec in ("proj0", "conv0", "tail0"):
                with b.passing(sections[sec]):
                    pass
            dve.wait_ge(*b["projected"].next())
            rows_and_tokens(l)
            convolutions(l)
            unit_norms(l)
            hgrn(l)
            scalar_decay(l)
            sec = sections["merge0"]
            with b.passing(sec), b.loop(KD, sec.tag) as i:
                for n in range(4):
                    t = gated(l, sec, i, 2 * n + 1)
                    if n == 1:
                        nc.vector.tensor_tensor(tmp[:, 0, :], hid_t[0][:, :], t, ALU.add).then_inc(*step.one())
                    elif n > 1:
                        nc.vector.tensor_tensor(tmp[:, 0, :], tmp[:, 0, :], t, ALU.add).then_inc(*step.one())
                    if n:
                        dve.wait_ge(*step.now())
                nc.vector.tensor_copy(m_hi[:, i, :], tmp[:, 0, :]).then_inc(*step.one())
                dve.wait_ge(*step.now())
                nc.vector.tensor_tensor(m_lo[:, i, :], tmp[:, 0, :], m_hi[:, i, :].bitcast(F32),
                                        ALU.subtract).then_inc(*b["merged"].one())
            with b.passing(sections["out0"]):
                pass
            norm_out(3, False)
            norm_in(4)
            hidden(l, 1)
            norm_out(5, True)
            nc.vector.sem_inc(sems["vec_free"], 1)

    @block.tensor
    def _(pe):
        b = book(pe, "pe")

        def split_product(j, sec, x_hi, x_lo, k0=0, first=True, last=True):
            _, nk, _, r, s = sec.loads[j]
            nk = KD if (sec.name, j) == ("tail", 2) else nk
            bank = sec.banks[j if sec.name != "down" else j // 3]
            if first:
                pe.wait_ge(*b[f"bank_free{bank}"].now())
                b[f"bank_free{bank}"].skip()
            pe.wait_ge(*b[f"lo_ready{r}"].next())
            rows_out = ROWS if (sec.name, j) == ("tail", 2) else P
            out = psum[bank][0:rows_out, 0:T]
            for k in range(nk):
                lhs_hi, lhs_lo = (w[s][:, k * rows_out:(k + 1) * rows_out] for w in (w_hi, w_lo))
                nc.tensor.matmul(out, lhs_hi, x_hi(k0 + k), start=(first and k == 0), stop=False)
                nc.tensor.matmul(out, lhs_hi, x_lo(k0 + k), start=False, stop=False)
                mm = nc.tensor.matmul(out, lhs_lo, x_hi(k0 + k), start=False, stop=(last and k == nk - 1))
            mm.then_inc(sems["tiles_done"], 1)

        u = (lambda k: u_hi[:, k, :]), (lambda k: u_lo[:, k, :])
        hid = (lambda k: hid_hi[:, k, :]), (lambda k: hid_lo[:, k, :])
        mrg = (lambda k: m_hi[:, k, :]), (lambda k: m_lo[:, k, :])

        def feature_sum():
            pe.wait_ge(*b["sums"].next())
            nc.tensor.matmul(mix[:, 0, 0:T], ones, ssq[:, :], start=True, stop=True).then_inc(
                *b["norm_sum"].one())

        def products(tag, x, ready):
            sec = sections[tag]
            with b.passing(sec), b.loop(sec.trips, sec.tag):
                pe.wait_ge(*b[ready].now())
                for j in range(sec.n):
                    split_product(j, sec, *x)

        def wait_u():
            b["u_ready"].skip(KD)

        def mlp(l, f):
            feature_sum()
            wait_u()
            products(f"up{f}", u, "u_ready")
            b["hid_ready"].skip(KF)
            sec = sections[f"down{f}"]
            with b.passing(sec), b.loop(sec.trips, sec.tag):
                pe.wait_ge(*b["hid_ready"].now())
                for j in range(sec.n):
                    q = j % 3
                    split_product(j, sec, *hid, k0=sum(DOWN_K[:q]), first=q == 0, last=q == 2)
            feature_sum()


        def passed(narrow=True):
            if narrow:
                nc.tensor.sem_inc(sems["t_step"], 1)

        def row_transposes(l):
            pe.wait_ge(*b["rows_ready"].next())
            for t, (t0, n) in enumerate(TILES3):
                nc.tensor.transpose(psum[t][0:n, 0:ROWS], rb[:, t0:t0 + n], c_["ident"][0:ROWS, 0:ROWS])
                nc.tensor.transpose(psum[t][0:n, 128:136], rl[0:8, t0:t0 + n], c_["ident"][0:8, 0:8]).then_inc(
                    *b["tok_t"].one())
            for t, (t0, n) in enumerate(TILES3):
                pe.wait_ge(*b["tok_copied"].next())
                passed(t == 2)
                whole = ones[0:n, 0:n] if t < 2 else c_["same_s"][0:n, :]
                nc.tensor.matmul(psum[t][0:n, 0:16], tri_of(t), la_tok[0:n, t, :], start=True, stop=True)
                nc.tensor.matmul(psum[t][0:n, 16:32], whole, la_tok[0:n, t, :], start=True, stop=True).then_inc(
                    *b["tok_sums"].one())

        def unit_norms(l):
            for half in range(2):
                for e in range(4):
                    pe.wait_ge(*b["l2_sq"].next())
                    if half:
                        pe.wait_ge(*b["l2_root"].now())
                    nc.tensor.matmul(mix[:, e, 0:T], ones, lsq[e][:, :], start=True, stop=True).then_inc(*b["l2_sum"].one())
                b["l2_root"].skip(4)

        def head_sums(src):
            pe.wait_ge(*b["f_sq"].next())
            for k in range(4):
                mm = nc.tensor.matmul(mix[:, k, 0:T], ones, src[:, k * T:(k + 1) * T], start=True, stop=True)
            mm.then_inc(*b["f_sum"].one())

        def hgrn(l):
            for d in range(C):
                n = 40 * (C - d)
                pe.wait_ge(*b["pair_x"].next())
                if d:
                    pe.wait_ge(*b["pair_t"].next())
                for k in range(4):
                    mm = nc.tensor.matmul(mix[:, k, 0:n], ones, hx[d % 2][:, k * n:(k + 1) * n], start=True, stop=True)
                mm.then_inc(*b["pair_a"].one())
            b["pair_t"].skip()
            pe.wait_ge(*b["hg_ready"].next())
            for t, (t0, n) in enumerate(TILES3):
                if t:
                    pe.wait_ge(*b["kv_copied"].next())
                    passed(t == 2)
                for bank, at in ((0, HF), (1, HI)):
                    for k in range(4):
                        mm = nc.tensor.transpose(psum[bank][0:n, k * P:(k + 1) * P], proj[:, at + k, t0:t0 + n], c_["ident"])
                mm.then_inc(*b["kv_t"].one())
            b["kv_copied"].skip()

            def keys_values(q):
                pe.wait_ge(*b[f"dma_kv{q}"].next())
                for k in range(4):
                    mm = nc.tensor.matmul(mix[:, q, k * P:(k + 1) * P], kv[q][:, k * P:(k + 1) * P],
                                          kv[q][:, 512 + k * P:512 + (k + 1) * P], start=True, stop=True)
                mm.then_inc(*b["hg_kv"].one())

            def outputs(q, s_in, at):
                pe.wait_ge(*b["hg_oi"].now())
                b["hg_oi"].skip()
                for k in range(4):
                    mm = nc.tensor.matmul(psum[2 + q % 2][:, k * C:(k + 1) * C], s_in[:, k * P:(k + 1) * P],
                                          proj[:, HQ + k, bass.ds(at, C)], start=True, stop=True)
                mm.then_inc(*b["hg_o"].one())

            with b.loop(NCP // 4, "hg_prompt") as i:
                for q in range(4):
                    keys_values(q)
                    pe.wait_ge(*b["hg_s"].now())
                    b["hg_s"].skip()
                    outputs(q, hs[q % 2], i * (4 * C) + q * C)
            with b.loop(NS // 4, "hg_sample") as i:
                for q in range(4):
                    sem_, at = b["hg_s"].now()
                    pe.wait_ge(sem_, at - 3)
                    b["hg_s"].skip()
                    keys_values(q)
                    pe.wait_ge(*b[f"dma_hin{q % 2}"].next())
                    outputs(q, hs_in[q % 2], i * (4 * C) + (SEQ + q * C))
            pe.wait_ge(*b["f_pre"].next())
            head_sums(hx[0])
            b["f_root"].skip()

        def delta_rule(t, n):
            m = 4 * n

            def heads(bank, lhs, rhs):
                passed(n == 64)
                for k in range(4):
                    mm = nc.tensor.matmul(psum[bank][0:n, k * n:(k + 1) * n], lhs[0:n, k * n:(k + 1) * n],
                                          rhs[0:n, k * n:(k + 1) * n], start=True, stop=True)
                mm.then_inc(*b["gdn_mm"].one())

            def transposes(bank, src):
                passed(n == 64)
                for k in range(4):
                    mm = nc.tensor.transpose(psum[bank][0:n, k * n:(k + 1) * n], src[0:n, k * n:(k + 1) * n],
                                             c_["ident"][0:n, 0:n])
                mm.then_inc(*b["gdn_mm"].one())

            def evacuated():
                pe.wait_ge(*b["gdn_ev"].next())

            def from_vector():
                pe.wait_ge(*b["gdn_v"].next())

            X = W[1] if t < 2 else W[0]
            from_vector()
            pe.wait_ge(*b["p_ready"].now())
            transposes(1, X)
            evacuated()
            heads(1, W[2], X)
            heads(2, X, W[2])
            from_vector()
            evacuated()
            heads(1, W[5], W[4])
            from_vector()
            heads(2, W[6], W[1])
            evacuated()
            heads(1, W[4], W[3])
            evacuated()
            if t < 2:
                transposes(2, W[2])
                for m2 in (16, 32, 64, 128):
                    from_vector()
                    evacuated()
                    heads(1, W[1], W[2])
                    evacuated()
                    heads(2, W[5], W[6])
                    from_vector()
                    if m2 < 128:
                        transposes(1, W[2])
            if t:
                for k in range(4):
                    mm = nc.tensor.matmul(psum[1][:, k * n:(k + 1) * n], kb[0:n, k * P:(k + 1) * P],
                                          W[2][0:n, k * n:(k + 1) * n], start=True, stop=True)
                mm.then_inc(*b["gdn_mm"].one())
                evacuated()
            if t < 2:
                for k in range(4):
                    out = psum[2][0:n, k * P:(k + 1) * P]
                    mm = nc.tensor.matmul(out, W[2][0:n, k * n:(k + 1) * n], vb[0:n, k * P:(k + 1) * P], start=True,
                                          stop=t == 0)
                    if t:
                        mm = nc.tensor.matmul(out, nsk[:, k * n:(k + 1) * n], state[GDN][:, k, :], start=False, stop=True)
                mm.then_inc(*b["gdn_mm"].one())
            else:
                for k in range(4):
                    nc.tensor.matmul(psum[2][:, k * n:(k + 1) * n], vb[0:n, k * P:(k + 1) * P],
                                     W[2][0:n, k * n:(k + 1) * n], start=True, stop=False)
                    for s in range(NS):
                        at = k * n + C * s
                        mm = nc.tensor.matmul(psum[2][:, at:at + C], st_s[:, s, k * P:(k + 1) * P], nsk[:, at:at + C],
                                              start=False, stop=s == NS - 1)
                mm.then_inc(*b["gdn_mm"].one())
                evacuated()
                passed()
                for k in range(4):
                    mm = nc.tensor.transpose(psum[1][0:n, k * P:(k + 1) * P], W[6][:, k * n:(k + 1) * n], c_["ident"])
                mm.then_inc(*b["gdn_mm"].one())
            evacuated()

        def outputs(kind, g, t, n):
            vals = wn if kind == "gdn" else vtok
            width = 64 if kind == "mb" else P

            def place(k):
                if kind == "mb":
                    return mix[64 * (k % 2):64 * (k % 2) + 64, 0, (k // 2) * n:(k // 2 + 1) * n]
                if kind == "ret":
                    return mix[:, k % 2, (k // 2) * n:(k // 2 + 1) * n]
                return mix[:, 0, k * n:(k + 1) * n]

            def state_of(k, s):
                at = {"mb": k, "ret": k // 2, "gdn": k}[kind]
                pr = {"mb": slice(64 * g, 64 * g + 64), "ret": slice(64 * (k % 2), 64 * (k % 2) + 64),
                      "gdn": slice(0, P)}[kind]
                if s is None:
                    own = {"mb": MB, "ret": RET, "gdn": GDN}[kind]
                    return state[own][pr, at, :], pr
                c0 = {"mb": 0, "ret": 256, "gdn": 0}[kind]
                return st_s[pr, s, c0 + at * width:c0 + (at + 1) * width], pr

            def inside(k, start):
                return nc.tensor.matmul(place(k), vals[0:n, k * width:(k + 1) * width], pm[0:n, k * n:(k + 1) * n],
                                        start=start, stop=t == 0)

            def before(k):
                if t == 1:
                    st, pr = state_of(k, None)
                    return nc.tensor.matmul(place(k), st, qd[pr, k * n:(k + 1) * n], start=False, stop=True)
                for s in range(NS):
                    st, pr = state_of(k, s)
                    mm = nc.tensor.matmul(place(k)[:, C * s:C * s + C], st, qd[pr, k * n + C * s:k * n + C * s + C],
                                          start=False, stop=s == NS - 1)
                return mm

            if t == 2 and kind != "gdn":
                for k in range(4):
                    inside(k, True).then_inc(*b["o_part"].one())
                    pe.wait_ge(*b["o_part"].now())
                    passed()
                    mm = before(k)
            else:
                for k in range(4):
                    mm = inside(k, True)
                    if t:
                        mm = before(k)
            mm.then_inc(*b["o_done"].one())

        def states(kind, g, t, n):
            vals = wn if kind == "gdn" else vtok
            width = 64 if kind == "mb" else P
            key = P if kind == "gdn" else 64
            pe.wait_ge(*b["k_ready"].now())
            passed()
            for k in range(4):
                pr = {"mb": slice(64 * g, 64 * g + 64), "ret": slice(64 * (k % 2), 64 * (k % 2) + 64),
                      "gdn": slice(0, P)}[kind]
                at = {"mb": k, "ret": k // 2, "gdn": k}[kind]
                keys = kend[0:n, k * key:(k + 1) * key]
                if t < 2:
                    mm = nc.tensor.matmul(mix[pr, 3, at * width:(at + 1) * width], keys, vals[0:n, k * width:(k + 1) * width],
                                          start=True, stop=True)
                    continue
                pe.wait_ge(*b["vm_ready"].next())
                if k == 1:
                    pe.wait_ge(*b["o_copied"].now())
                passed()
                bank = 2 if k % 2 == 0 else 0
                for half in range(NS * width // 512):
                    mm = nc.tensor.matmul(mix[pr, bank + half, :], keys, vm[k % 2][:, 512 * half:512 * half + 512],
                                          start=True, stop=True)
                mm.then_inc(*b["state_mm"].one())
            if t < 2:
                mm.then_inc(*b["state_mm"].one())

        def scalar_decay(l):
            pe.wait_ge(*b["hg_finished"].next())
            for k in range(4):
                mm = nc.tensor.matmul(mix[:, k, 0:T], c_["rot"], proj[:, RQ + k, :], start=True, stop=True)
            mm.then_inc(*b["rot_ps"].one())
            b["rotated"].skip()
            for kind, g in GROUPS:
                col = {"mb": 4 * g, "ret": RET, "gdn": GDN}[kind]
                if (kind, g) == ("mb", 0):
                    b["dma_state"].skip(2)
                if kind == "gdn":
                    b["dma_state"].skip()
                pr = slice(64 * g, 64 * g + 64)
                for t, (t0, n) in enumerate(TILES3):
                    pe.wait_ge(*b["state_new"].now())
                    pe.wait_ge(*b["o_copied"].now())
                    passed(t == 2)
                    for k in range(4):
                        mm = nc.tensor.matmul(psum[0][:, k * n:(k + 1) * n],
                                              la_tok[0:n, t, col + k:col + k + 1].to_broadcast([n, P]), tri_of(t)[0:n, 0:n],
                                              start=True, stop=True)
                    mm.then_inc(*b["cum_bc"].one())
                    pe.wait_ge(*b["rotated"].now())
                    passed(t == 2)
                    if kind == "mb":
                        nc.tensor.matmul(psum[1][0:n, 0:n], xp[pr, 4, t0:t0 + n], xp[pr, 5, t0:t0 + n], start=True, stop=True)
                        turns = [(psum[3], e, xp[:, 2 * g + e, t0:t0 + n]) for e in range(2)]
                        turns.append((mix[:, 2], 0, xp[:, 4, t0:t0 + n]))
                    elif kind == "ret":
                        for k in range(4):
                            r = slice(64 * (k % 2), 64 * (k % 2) + 64)
                            nc.tensor.matmul(psum[1 + k % 2][0:n, (k // 2) * n:(k // 2 + 1) * n], proj[r, RK + k // 2, t0:t0 + n],
                                             proj[r, RQ + k // 2, t0:t0 + n], start=True, stop=True)
                        turns = [(psum[3], e, proj[:, RV + e, t0:t0 + n]) for e in range(4)]
                        turns += [(mix[:, 2], e, proj[:, RK + e, t0:t0 + n]) for e in range(2)]
                    else:
                        for k in range(4):
                            for bank, other in ((1, 6), (2, 10)):
                                nc.tensor.matmul(psum[bank][0:n, k * n:(k + 1) * n], xp[:, 10 + k, t0:t0 + n],
                                                 xp[:, other + k, t0:t0 + n], start=True, stop=True)
                        turns = [(psum[3], e, xp[:, 14 + e, t0:t0 + n]) for e in range(4)]
                        turns += [(mix[:, 2], e, xp[:, 10 + e, t0:t0 + n]) for e in range(4)]
                    for bank, e, src in turns:
                        mm = nc.tensor.transpose(bank[0:n, e * P:(e + 1) * P], src, c_["ident"])
                    mm.then_inc(*b["scores"].one())
                    b["p_ready"].skip()
                    b["k_ready"].skip()
                    if t == 2:
                        pe.wait_ge(*b["dma_state"].now())
                    if kind == "gdn":
                        delta_rule(t, n)
                    pe.wait_ge(*b["v_copied"].next())
                    pe.wait_ge(*b["p_ready"].now())
                    if t:
                        pe.wait_ge(*b["q_ready"].next())
                    passed(t == 2 or kind == "mb")
                    outputs(kind, g, t, n)
                    b["o_copied"].skip(2 if kind == "ret" else 1)
                    states(kind, g, t, n)
                    b["state_new"].skip()
                if (kind, g) == ("mb", 0):
                    continue
                pe.wait_ge(*b["f_pre"].next())
                if kind == "mb":
                    pe.wait_ge(*b["f_sq"].next())
                    for k in range(4):
                        mm = nc.tensor.matmul(mix[:, 0, 0:T], ones, f_sq[:, k * T:(k + 1) * T], start=k == 0, stop=k == 3)
                    mm.then_inc(*b["f_sum"].one())
                else:
                    head_sums(f_sq)
                pe.wait_ge(*b["f_root"].next())
                passed()

        for name in START:
            nc.tensor.sem_inc(sems[name], unit_of(name))
        nc.tensor.sem_inc(sems["tiles_done"], AHEAD)
        nc.tensor.sem_inc(sems["hg_kv"], 3)
        b["hg_s"].skip()
        pe.wait_ge(b["dma_in"].sem, 32)
        with b.loop(DEPTH, "layer") as l:
            mlp(l, 0)
            feature_sum()
            wait_u()
            for tag in ("proj0", "conv0", "tail0"):
                products(tag, u, "u_ready")
            row_transposes(l)
            unit_norms(l)
            hgrn(l)
            scalar_decay(l)
            b["y_ready"].skip()
            sec = sections["merge0"]
            with b.passing(sec), b.loop(KD, sec.tag):
                pe.wait_ge(*b["y_ready"].now())
                for n, base in enumerate((Z, HG, RG, GZ)):
                    split_product(2 * n, sec, *u)
                    b[f"dma_w{sec.loads[2 * n][3]}"].skip()
                    r, q = sec.loads[2 * n + 1][3], sec.banks[2 * n + 1]
                    pe.wait_ge(*b[f"bank_free{q}"].now())
                    b[f"bank_free{q}"].skip()
                    pe.wait_ge(*b[f"dma_w{r}"].next())
                    for k in range(KB):
                        mm = nc.tensor.matmul(psum[q][:, 0:T], raw[r][:, k * P:(k + 1) * P],
                                              proj[:, base + k, :], start=k == 0, stop=k == KB - 1)
                    mm.then_inc(sems["tiles_done"], 1)
            b["merged"].skip(KD)
            products("out0", mrg, "merged")
            feature_sum()
            mlp(l, 1)


def constants():
    c = {}
    i, j = np.arange(P)[:, None], np.arange(P)[None, :]
    BIG = 1e30
    c["ones"], c["ident"] = np.ones((P, P)), np.eye(P)
    c["tri"] = (i <= j)
    c["neg"] = np.where(i <= j, 0, -BIG)
    c["pos"] = np.where(i > j, 0, BIG)
    seq = i // C == j // C
    half = lambda m: m[:, :64] * np.where(np.arange(P)[:, None] < 64, 1, 0)
    c["tri_s"], c["same_s"] = half((i <= j) & seq), half(seq)
    c["neg_s"] = np.where((i <= j) & seq, 0, -BIG)[:, :64]
    c["pos_s"] = np.where((i > j) & seq, 0, BIG)[:, :64]
    rot = np.zeros((P, P))
    for p in range(P):
        rot[p + 32 if p % 64 < 32 else p - 32, p] = -1 if p % 64 < 32 else 1
    c["rot"] = rot
    steps = np.arange(32, dtype=np.float32) * np.float32(1 / 31)
    inv = (1.0 / np.power(10000.0, steps.astype(np.float64))).astype(np.float32)
    pos = np.concatenate([np.arange(SEQ), np.tile(PAST_LEN + np.arange(DEC_SEQ), DEC_BATCH)]).astype(np.float32)
    ang = (pos[None, :] * np.tile(inv, 4)[:, None]).astype(np.float32).astype(np.float64)
    c["cos"], c["sin"] = np.cos(ang), np.sin(ang)
    c["b8"] = (i > j) & (i // 8 == j // 8)
    for m in (16, 32, 64, 128):
        c[f"b{m}"] = (i // m == j // m) & (i % m >= m // 2) & (j % m < m // 2)
    c["lgam"] = np.broadcast_to(np.log((1.0 - np.exp2(-5.0 - np.arange(4))).astype(np.float32)), (P, 4))
    c["pick"] = (i // C == np.arange(8)[None, :])
    c["eps"] = np.full((P, 1), EPS)
    return np.concatenate([np.asarray(c[k], np.float32) for k in CONST], axis=1)


OUTS = {"x": (P, KD, T), "st_conv": (DEPTH, P, NCONV, NS + 1, 3), "mb_p": (DEPTH, P, 256), "ret_p": (DEPTH, P, 256),
        "gdn_p": (DEPTH, P, 512), "hg_p": (DEPTH, P, 512), "mb_s": (DEPTH, P, NS * 256), "ret_s": (DEPTH, P, NS * 256),
        "gdn_s": (DEPTH, P, NS * 512), "hg_s": (DEPTH, NS, P, 512)}


def results(r):
    tok = r["x"].transpose(1, 0, 2).reshape(D_MODEL, T).T
    cv = r["st_conv"].transpose(0, 3, 4, 2, 1).reshape(DEPTH, NS + 1, 3, NCONV * P)
    mb = lambda x, n: x.reshape(DEPTH, 2, 64, n, 4, 64).transpose(0, 3, 1, 4, 2, 5).reshape(DEPTH, n, 8, 64, 64)
    ret = lambda x, n: x.reshape(DEPTH, 2, 64, n, 2, P).transpose(0, 3, 4, 1, 2, 5).reshape(DEPTH, n, 4, 64, P)
    gd = lambda x, n: x.reshape(DEPTH, P, n, 4, P).transpose(0, 2, 3, 1, 4)
    hg_p = r["hg_p"].reshape(DEPTH, P, 1, 4, P).transpose(0, 2, 3, 1, 4)
    hg_s = r["hg_s"].reshape(DEPTH, NS, P, 4, P).transpose(0, 1, 3, 2, 4)
    got = (tok[:SEQ].reshape(1, SEQ, D_MODEL), tok[SEQ:].reshape(DEC_BATCH, DEC_SEQ, D_MODEL),
           mb(r["mb_p"], 1), cv[:, :1, :, :768], hg_p, ret(r["ret_p"], 1), gd(r["gdn_p"], 1), cv[:, :1, :, 768:],
           mb(r["mb_s"], NS), cv[:, 1:, :, :768], hg_s, ret(r["ret_s"], NS), gd(r["gdn_s"], NS), cv[:, 1:, :, 768:])
    return tuple(np.ascontiguousarray(x) for x in got)


def layouts(x):
    A = {k: np.asarray(v) for k, v in x.items()}
    out = {}
    tok = np.concatenate([A["x_prompt"].reshape(SEQ, D_MODEL), A["x_sample"].reshape(-1, D_MODEL)])
    out["x"] = tok.T.reshape(KD, P, T).transpose(1, 0, 2)
    out["w_up"] = A["ffn_w_in"].reshape(DEPTH, 2, KD, P, 2, KF, P).transpose(0, 1, 5, 4, 3, 2, 6).reshape(DEPTH, 2, KF, 2, P, KD * P)
    out["w_down"] = A["ffn_w_out"].reshape(DEPTH, 2, KF, P, KD, P).transpose(0, 1, 4, 3, 2, 5).reshape(DEPTH, 2, KD, P, KF * P)
    w = A["w_in"]
    s = np.cumsum([0, 512, 768, 8, 512, 512, 512, 512, 256, 256, 512, 512, 1536, 512, 4, 4, 4096])
    seg = [w[:, :, s[i]:s[i + 1]] for i in range(16)]
    z, xbc, dt, hq, hf, hi, hg, rq, rk, rv, rg, qkv, gz, ga, gb, gates = seg
    cols = np.concatenate([z, hq, hf, hi, hg, rq, rk, rv, rg, gz, xbc, qkv], axis=2)
    out["w_proj"] = cols.reshape(DEPTH, KD, P, NPLAIN + NCONV, P).transpose(0, 3, 2, 1, 4).reshape(DEPTH, NPLAIN + NCONV, P, KD * P)
    small = np.zeros((DEPTH, D_MODEL, ROWS), np.float32)
    small[:, :, 0:8], small[:, :, 32:36], small[:, :, 64:68] = dt, ga, gb
    out["w_rows"] = small.reshape(DEPTH, KD, P, ROWS).transpose(0, 2, 1, 3).reshape(DEPTH, P, KD * ROWS)
    out["w_gate"] = gates.reshape(DEPTH, KD, P, 4, KD, P).transpose(0, 4, 3, 2, 1, 5).reshape(DEPTH, KD, 4, P, KD * P)
    out["w_branch"] = A["w_branch"].reshape(DEPTH, 4, KB, P, KD, P).transpose(0, 4, 1, 3, 2, 5).reshape(DEPTH, KD, 4, P, KB * P)
    out["w_out"] = A["w_out"].reshape(DEPTH, KD, P, KD, P).transpose(0, 3, 2, 1, 4).reshape(DEPTH, KD, P, KD * P)
    v = np.zeros((DEPTH, P, NV), np.float32)

    def put(at, rows):
        v[:, :, at:at + rows.shape[1]] = rows.transpose(0, 2, 1)

    put(V_G, A["norm_g"].reshape(DEPTH, 48, P))
    cw = np.concatenate([A["mb_conv_w"], A["gdn_conv_w"]], axis=2).reshape(DEPTH, 4, NCONV, P)
    put(V_CW, cw.transpose(0, 2, 1, 3).reshape(DEPTH, 72, P))
    put(V_CB, A["mb_conv_b"].reshape(DEPTH, 6, P))
    put(V_D, np.repeat(A["mb_d"], 64, axis=1).reshape(DEPTH, 4, P))
    put(V_MN, A["mb_norm"].reshape(DEPTH, 4, P))
    put(V_LB, np.broadcast_to(A["hg_lb_logits"].reshape(1, 8, P), (DEPTH, 8, P)))
    put(V_HN, A["hg_norm"].reshape(DEPTH, 1, P))
    put(V_GN, A["gdn_norm"].reshape(DEPTH, 1, P))
    v[:, 0:8, V_RB], v[:, 32:36, V_RB] = A["mb_dt_bias"], A["gdn_dt_bias"]
    v[:, 0:8, V_RA], v[:, 32:36, V_RA] = A["mb_a_log"], A["gdn_a_log"]
    v[1:, :, V_ON] = 1.0
    out["vec"] = v
    out["const"] = constants()
    cv = np.concatenate([A["state_ssm_conv"], A["state_gdn_conv"]], axis=3)
    out["st_conv"] = cv.reshape(DEPTH, NS, 3, NCONV, P).transpose(0, 4, 3, 1, 2).reshape(DEPTH, P, NCONV * NS * 3)
    out["st_mb"] = A["state_ssm"].reshape(DEPTH, NS, 2, 4, 64, 64).transpose(0, 2, 4, 1, 3, 5).reshape(DEPTH, P, NS * 256)
    out["st_ret"] = A["state_ret"].reshape(DEPTH, NS, 2, 2, 64, P).transpose(0, 3, 4, 1, 2, 5).reshape(DEPTH, P, NS * 256)
    out["st_gdn"] = A["state_gdn"].transpose(0, 3, 1, 2, 4).reshape(DEPTH, P, NS * 512)
    out["st_hg"] = A["state_hgrn"].transpose(0, 1, 3, 2, 4).reshape(DEPTH, NS, P, 512)
    return {k: np.ascontiguousarray(v) for k, v in out.items()}


def kernel(**inputs):
    import concourse.bacc as _bacc
    from concourse import mybir as _mybir
    from concourse.bass_utils import run_bass_kernel_spmd as _run

    arrays = {f"in_{k}": v for k, v in layouts(inputs).items()}

    def program(per_body):
        nc = _bacc.Bacc("TRN2", target_bir_lowering=False, num_devices=1)
        a = {k[3:]: nc.dram_tensor(k, v.shape, _mybir.dt.from_np(v.dtype), kind="ExternalInput").ap()
             for k, v in arrays.items()}
        o = {k: nc.dram_tensor(f"out_{k}", shape, F32, kind="ExternalOutput").ap() for k, shape in OUTS.items()}
        found = {}
        build(nc, a, o, per_body, found)
        return nc, found

    nc, _ = program(program({})[1])
    r = _run(nc, [arrays], core_ids=[0])
    return results({k: r.results[0][f"out_{k}"] for k in OUTS})
```

```python
from contextlib import ExitStack, contextmanager

import numpy as np

import concourse.bass as bass
from concourse import mybir

ALU = mybir.AluOpType
ACT = mybir.ActivationFunctionType
F32 = mybir.dt.float32
F32R = mybir.dt.float32r
AX_X = mybir.AxisListType.X

P = 128
D_MODEL, DEPTH = 1024, 2
SEQ, DEC_BATCH, DEC_SEQ, PAST_LEN = 256, 8, 8, 2048
T = SEQ + DEC_BATCH * DEC_SEQ
D_FF = 2816
KD = D_MODEL // P
KF = D_FF // P
KB = 4
C = 8
NC = T // C
NCP = SEQ // C
EPS = 1e-6
XW = SEQ + 3 + DEC_BATCH * (DEC_SEQ + 3)

Z, HQ, HF, HI, HG, RQ, RK, RV, RG, GZ = 0, 4, 8, 12, 16, 20, 22, 24, 28, 32
NPLAIN, NCONV = 36, 18
NSLOT = 4
SLOT = KD * P
DOWN_K = (8, 8, 6)
ROWS = 96

V_G, V_CW, V_CB, V_D, V_MN, V_LB, V_HN, V_GN, V_RB, V_RA, V_ON = 0, 48, 120, 126, 130, 134, 142, 143, 144, 145, 146
NV = 147

CONST, _at = {}, 0
for _name, _cols in (("ones", P), ("ident", P), ("tri", P), ("neg", P), ("pos", P), ("tri_s", 64), ("neg_s", 64),
                     ("pos_s", 64), ("same_s", 64), ("rot", P), ("cos", T), ("sin", T), ("b8", P), ("b16", P),
                     ("b32", P), ("b64", P), ("b128", P),
                     *((f"next{m}", P) for m in (2, 4, 8, 16, 32, 64, 128)), ("lgam", 4), ("pick", 8), ("eps", 1), ("eps4", 1)):
    CONST[_name] = (_at, _cols)
    _at += _cols
NCONST = _at
MB, RET, GDN, HGRN = 0, 8, 12, 16
TILES3 = ((0, 128), (128, 128), (256, 64))
NS = DEC_BATCH


START = ("dma_conv_out", "h_ready", "o_copied", "state_new", "vec_free", *(f"{n}{i}" for n in ("bank_free", "lo_ready") for i in range(NSLOT)))


def unit_of(name):
    return 16 if name.startswith("dma_") else 1


class Count:

    def __init__(self, sem, unit, name):
        self.sem, self.unit, self.name, self.terms = sem, unit, name, []
        self.n = unit if name in START else 0

    def at(self):
        e = self.n
        for reg, per in self.terms:
            if per:
                e = reg * per + e
        return e

    def one(self):
        self.n += self.unit
        return self.sem, self.unit

    def now(self):
        return self.sem, self.at()

    def next(self):
        self.n += self.unit
        return self.sem, self.at()

    def skip(self, k=1):
        self.n += k * self.unit


class Book:

    def __init__(self, eng, name, sems, per_body, seen):
        self.eng, self.name, self.sems, self.per_body, self.seen = eng, name, sems, per_body, seen
        self.counts = {}

    def __getitem__(self, name):
        if name not in self.counts:
            self.counts[name] = Count(self.sems[name], unit_of(name), name)
            self.counts[name].terms = [(r, self.per_body.get((self.name, tag, name), 0)) for r, tag in self.around]
        return self.counts[name]

    around = ()

    @contextmanager
    def passing(self, section):
        uses = {k: n for k, n in section.uses.items() if self.name == "pe" or not k.startswith("dma_")}
        start = {k: self[k].n for k in uses}
        yield
        for k, n in uses.items():
            self.counts[k].n = start[k] + n * self.counts[k].unit

    @contextmanager
    def loop(self, trips, tag):
        first = {k: unit_of(k) if k in START else 0 for k in self.sems}
        start = {**first, **{k: c.n for k, c in self.counts.items()}}
        outer = self.around
        with self.eng.Fori(0, trips) as i:
            self.around = (*outer, (i, tag))
            for k, c in self.counts.items():
                c.terms.append((i, self.per_body.get((self.name, tag, k), 0)))
            yield i
            for k, c in self.counts.items():
                per = c.n - start[k]
                self.seen[(self.name, tag, k)] = per
                c.terms.pop()
                c.n = start[k] + per * trips
        self.around = outer


def build(nc, a, o, per_body, seen):
    with ExitStack() as ctx:
        _build(nc, a, o, per_body, seen, ctx)


def _build(nc, a, o, per_body, seen, ctx):
    sems = {}

    def sem(*names):
        for n in names:
            sems[n] = ctx.enter_context(nc.semaphore(n))

    def sb(name, shape, dt=F32, stack=ctx):
        return stack.enter_context(nc.sbuf_tensor(name, shape, dt))

    h = sb("h", [P, KD, T])
    u_hi, u_lo = sb("u_hi", [P, KD, T], F32R), sb("u_lo", [P, KD, T], F32R)
    raw = [sb(f"w_raw{i}", [P, SLOT]) for i in range(NSLOT)]
    with ExitStack() as part:
        st_s = sb("st_s", [P, NS, 512], F32, part)
        hp = sb("hg_p", [P, 1280], F32, part)
        ho = sb("hg_o", [P, 4, T], F32, part)
        hf8, hf128 = sb("hg_fade8", [P, 4, T // 8], F32, part), sb("hg_fade128", [P, 4, 2], F32, part)
    w_hi = [sb(f"w_hi{i}", [P, SLOT], F32R) for i in range(NSLOT)]
    w_lo = [sb(f"w_lo{i}", [P, SLOT], F32R) for i in range(NSLOT)]
    vec = sb("vec", [P, NV])
    const = sb("const", [P, NCONST])
    c_ = {k: const[:, at:at + n] for k, (at, n) in CONST.items()}
    ones, eps_c = c_["ones"], c_["eps"]
    lb = sb("lb", [P, 32])
    la_tok, beta_tok, dt_tok = sb("la_tok", [P, 3, 16]), sb("beta_tok", [P, 3, 4]), sb("dt_tok", [P, 3, 8])
    cum_tok, ecum_tok = sb("cum_tok", [P, 3, 16]), sb("ecum_tok", [P, 3, 16])
    to_end, to_end_dt, beta_cum = sb("to_end", [P, 3, 16]), sb("to_end_dt", [P, 3, 8]), sb("beta_cum", [P, 3, 4])
    rows = sb("rows", [ROWS, T])
    with ExitStack() as part:
        hid_hi = sb("hid_hi", [P, KF, T], F32R, part)
        hid_lo = sb("hid_lo", [P, KF, T], F32R, part)
    part = ExitStack()
    proj = sb("proj", [P, NPLAIN, T], F32, ctx)
    with ExitStack() as part:
        m_hi = sb("m_hi", [P, KD, T], F32R, part)
        m_lo = sb("m_lo", [P, KD, T], F32R, part)
    xp = sb("xp", [P, NCONV, XW], F32, ctx)
    with ExitStack() as part:
        y = sb("y", [P, KD, T], F32, part)
        tmp = sb("tmp", [P, KD, T], F32, part)
        gate_s = [sb(f"gate_s{i}", [P, T], F32, part) for i in range(2)]
        hid_t = [sb(f"hid_t{i}", [P, T], F32, part) for i in range(2)]

        rms = sb("rms", [P, T], F32, part)



    with ExitStack() as part:
        hf1, hf2 = sb("hg_fade1", [P, 4 * T], F32, part), sb("hg_fade2", [P, 2 * T], F32, part)
        ht = sb("hg_masked", [P, 1280], F32, part)
    with ExitStack() as part:
        rx, re, ru, rt, rl, rb = (sb(f"row_{n}", [ROWS, T], F32, part) for n in "xeutlb")
        cacc = [sb(f"conv_acc{i}", [P, XW], F32, part) for i in range(2)]
        cin = sb("conv_in", [P, NCONV, NS, 3], F32, part)
        cout = sb("conv_out", [P, NCONV, NS + 1, 3], F32, part)
        lsq = [sb(f"l2_sq{i}", [P, T], F32, part) for i in range(4)]
        lrt = sb("l2_rt", [P, 4, T], F32, part)
    with ExitStack() as part:
        dm, em, dm2, ecb, pm, qd, kend, vtok, kb, vb, wn, nsk = (
            sb(f"sc_{n}", [P, 512], F32, part) for n in ("d", "e", "d2", "ecb", "p", "qd", "kend", "v", "kb", "vb", "wn", "nsk"))
        state = {MB: sb("st_mb", [P, 4, 64], F32, part), RET: sb("st_ret", [P, 2, 128], F32, part),
                 GDN: sb("st_gdn", [P, 4, 128], F32, part), HGRN: sb("st_hg", [P, 4, 128], F32, part)}
    work = proj[:, HQ:HQ + 12, :].rearrange("p k t -> p (k t)")
    W = [work[:, 512 * i:512 * i + 512] for i in range(7)]
    f_sq, f_rt, f_o = (work[:, 1280 * i:1280 * i + 1280] for i in range(3))

    f_ok = f_o.rearrange("p (k t) -> p k t", k=4)
    vm = [work[0:64, 1024 * i:1024 * i + 1024] for i in range(2)]

    GROUPS = (("hg", 0), ("mb", 0), ("mb", 1), ("ret", 0), ("gdn", 0))

    def acc_sample(acc):
        return acc[:, SEQ + 3:XW].rearrange("p (s t) -> p s t", s=NS)[:, :, 0:C]

    def over(x, shape):
        return x.to_broadcast(shape)

    def tri_of(t):
        return c_["tri"] if t < 2 else c_["tri_s"][0:64, :]

    psum = [ctx.enter_context(nc.psum_tensor(f"bank{i}", [P, 512], F32)) for i in range(4)]
    mix = ctx.enter_context(nc.psum_tensor("mix", [P, 4, 512], F32))

    sem("dma_in", "dma_vec", "dma_out", "v_step", "a_step", "p_step", "t_step")
    sem(*[f"{n}{i}" for n in ("dma_w", "hi_ready", "lo_ready", "bank_free") for i in range(NSLOT)])
    sem("tiles_done")
    sem("gate_ready", "hid_ready", "squares", "norm_sum", "root", "u_ready", "y_ready", "h_ready", "merged", "vec_free", "projected")
    sem("row_x", "row_e", "row_u", "row_ln", "rows_ready", "tok_t", "tok_copied", "tok_sums", "tok_exp", "tok_ready")
    sem("dma_conv", "dma_conv_out", "conv_filled", "conv_saved", "conv_sum", "conv_done")
    sem("l2_sq", "l2_sum", "l2_root", "l2_done", "bound_d", "bound_e", "hg_sig", "silus")
    sem("hg_q", "hg_sc", "hg_ready")
    sem("f_sq", "f_sum", "f_root", "f_pre", "mixer_done", "rot_ps", "rot_used", "rotated")
    sem("cum_bc", "cum_used", "ecb_ready", "dec_d", "dec_e", "scores", "v_copied", "p_ready", "q_ready", "k_ready",
        "o_done", "o_copied", "state_mm", "state_new", "dma_state", "dma_state_out", "gdn_mm", "gdn_ev", "vm_ready", "vm_used",
        "w_ready", "gdn_v", "o_part")

    block = ctx.enter_context(nc.Block())

    def book(eng, name):
        return Book(eng, name, sems, per_body, seen)

    sections = {}

    class Section:
        def __init__(self, name, f, trips, sources, banks):
            self.name, self.f, self.trips, self.sources, self.banks = name, f, trips, sources, banks
            self.n, self.base, self.lead = len(sources), sum(x.trips * x.n for x in sections.values()), 2
            self.tag = f"{name}{f}"
            sections[self.tag] = self
            self.loads, s = [], 0
            for j, (src, nk, split) in enumerate(sources):
                self.loads.append((src, nk, split, j % NSLOT, s % NSLOT if split else None))
                s += split
            self.uses = {f"bank_free{q}": trips * sum(x == q for x in banks) for q in range(4)}
            self.uses |= {f"dma_w{r}": trips * sum(x[3] == r for x in self.loads) for r in range(NSLOT)}

    def row(x, cols):
        return x[:, 0:cols]

    for f in range(2):
        Section("up", f, KF // 2, [(lambda l, i, m=m, g=g, f=f: a["w_up"][l, f, 2 * i + m, g], KD, True)
                                   for m in range(2) for g in range(2)], (0, 1, 2, 3))
        Section("down", f, 2, [(lambda l, i, m=m, q=q, f=f: a["w_down"][l, f, 4 * i + m][:, sum(DOWN_K[:q]) * P:sum(DOWN_K[:q + 1]) * P],
                                DOWN_K[q], True) for m in range(4) for q in range(3)], (0, 1, 2, 3))
        if f:
            break
        Section("proj", 0, NPLAIN // 4, [(lambda l, i, m=m: a["w_proj"][l, 4 * i + m], KD, True) for m in range(4)],
                (0, 1, 2, 3))
        Section("conv", 0, 4, [(lambda l, i, m=m: a["w_proj"][l, 4 * i + (NPLAIN + m)], KD, True) for m in range(4)],
                (0, 1, 2, 3))
        Section("tail", 0, 1, [(lambda l, i, m=m: a["w_proj"][l, NPLAIN + 16 + m], KD, True) for m in range(2)]
                + [(lambda l, i: a["w_rows"][l], KD * ROWS // P, True)], (0, 1, 2))
        Section("merge", 0, KD, [t for n in range(4) for t in (
            (lambda l, i, n=n: a["w_gate"][l, i, n], KD, True),
            (lambda l, i, n=n: a["w_branch"][l, i, n], KB, False))], (0, 1, 2, 3) * 2)
        sections["merge0"].lead = 4
        Section("out", 0, KD // 4, [(lambda l, i, m=m: a["w_out"][l, 4 * i + m], KD, True) for m in range(4)],
                (0, 1, 2, 3))
    ORDER = list(sections.values())
    TILES = sum(x.trips * x.n for x in ORDER)
    AHEAD = NSLOT

    def done(l, sec, i, j):
        return l * TILES + (i * sec.n + (AHEAD + sec.base + j + 1))

    def slot_empty(l, sec, i, j):
        return done(l, sec, i, j - (3 if sec.name == "merge" else NSLOT))

    @block.sync
    def _(sp):
        b = book(sp, "sp")

        def mixer_dmas(l):
            sp.wait_ge(*b["projected"].next())
            sp.dma_start(cin[:, :, :, :], a["st_conv"][l]).then_inc(*b["dma_conv"].one())
            sp.wait_ge(*b["conv_saved"].next())
            sp.dma_start(o["st_conv"][l], cout[:, :, :, :]).then_inc(*b["dma_conv_out"].one())
            sp.dma_start(st_s[:, :, :], a["st_hg"][l].rearrange("p (s n) -> p s n", s=NS)).then_inc(*b["dma_state"].one())
            b["state_new"].skip(3)
            sp.wait_ge(*b["state_new"].now())
            sp.dma_start(o["hg_p"][l], state[HGRN][:, :, :].rearrange("p h n -> p (h n)")).then_inc(*b["dma_state_out"].one())
            sp.dma_start(o["hg_s"][l].rearrange("p (s n) -> p s n", s=NS), st_s[:, :, :]).then_inc(*b["dma_state_out"].one())
            sp.wait_ge(*b["dma_state_out"].now())
            sp.dma_start(st_s[:, :, 0:256], a["st_mb"][l].rearrange("p (s n) -> p s n", s=NS)).then_inc(*b["dma_state"].one())
            sp.dma_start(st_s[:, :, 256:512], a["st_ret"][l].rearrange("p (s n) -> p s n", s=NS)).then_inc(*b["dma_state"].one())
            b["state_new"].skip(6)
            sp.wait_ge(*b["state_new"].now())
            sp.dma_start(o["mb_p"][l], state[MB][:, :, :].rearrange("p h n -> p (h n)")).then_inc(*b["dma_state_out"].one())
            sp.dma_start(o["mb_s"][l].rearrange("p (s n) -> p s n", s=NS), st_s[:, :, 0:256]).then_inc(*b["dma_state_out"].one())
            b["state_new"].skip(3)
            sp.wait_ge(*b["state_new"].now())
            sp.dma_start(o["ret_p"][l], state[RET][:, :, :].rearrange("p h n -> p (h n)")).then_inc(*b["dma_state_out"].one())
            sp.dma_start(o["ret_s"][l].rearrange("p (s n) -> p s n", s=NS), st_s[:, :, 256:512]).then_inc(*b["dma_state_out"].one())
            sp.wait_ge(*b["dma_state_out"].now())
            sp.dma_start(st_s[:, :, :], a["st_gdn"][l].rearrange("p (s n) -> p s n", s=NS)).then_inc(*b["dma_state"].one())
            b["state_new"].skip(3)
            sp.wait_ge(*b["state_new"].now())
            sp.dma_start(o["gdn_p"][l], state[GDN][:, :, :].rearrange("p h n -> p (h n)")).then_inc(*b["dma_state_out"].one())
            sp.dma_start(o["gdn_s"][l].rearrange("p (s n) -> p s n", s=NS), st_s[:, :, :]).then_inc(*b["dma_state_out"].one())

        sp.dma_start(h[:, :, :], a["x"]).then_inc(*b["dma_in"].one())
        sp.dma_start(const[:, :], a["const"]).then_inc(*b["dma_in"].one())
        with b.loop(DEPTH, "layer") as l:
            sp.wait_ge(*b["vec_free"].now())
            b["vec_free"].skip()
            sp.dma_start(vec[:, :], a["vec"][l]).then_inc(*b["dma_vec"].one())
            for sec in ORDER:
                if sec.name == "merge":
                    mixer_dmas(l)
                with b.loop(sec.trips, sec.tag) as i:
                    for j, (src, nk, split, r, _) in enumerate(sec.loads):
                        sp.wait_ge(*b[f"lo_ready{r}"].now())
                        if split:
                            b[f"lo_ready{r}"].skip()
                        if sec.name in ("merge", "out"):
                            sp.wait_ge(sems["tiles_done"], done(l, sec, i, j - NSLOT))
                        sp.dma_start(raw[r][:, 0:nk * P], src(l, i)).then_inc(*b[f"dma_w{r}"].one())
        sp.wait_ge(sems["h_ready"], 1 + 3 * KD * DEPTH)
        sp.dma_start(o["x"], h[:, :, :]).then_inc(*b["dma_out"].one())
        for name in ("dma_out", "dma_conv_out", "dma_state_out"):
            sp.wait_ge(*b[name].now())

    @block.gpsimd
    def _(pool):
        b = book(pool, "pool")
        def padded(x):
            return xp[:, :, 3 + SEQ:XW].rearrange("p m (s t) -> p m s t", s=NS)

        def passed():
            nc.gpsimd.sem_inc(sems["p_step"], 1)

        def conv_ends(l):
            pool.wait_ge(*b["projected"].next())
            passed()
            nc.gpsimd.memset(xp[:, :, 0:3], 0.0)
            pool.wait_ge(*b["dma_conv"].next())
            passed()
            nc.gpsimd.tensor_copy(padded(xp)[:, :, :, 0:3], cin[:, :, :, :]).then_inc(*b["conv_filled"].one())
            pool.wait_ge(*b["dma_conv_out"].now())
            b["dma_conv_out"].skip()
            passed()
            nc.gpsimd.tensor_copy(cout[:, :, 0, :], xp[:, :, SEQ:SEQ + 3])
            nc.gpsimd.tensor_copy(cout[:, :, 1:, :], padded(xp)[:, :, :, C:C + 3]).then_inc(*b["conv_saved"].one())



        with b.loop(DEPTH, "layer") as l:
            for sec in ORDER:
                if sec.name == "merge":
                    conv_ends(l)

                with b.loop(sec.trips, sec.tag) as i:
                    for j, (_, nk, split, r, s) in enumerate(sec.loads):
                        if not split:
                            continue
                        n = nk * P
                        pool.wait_ge(*b[f"hi_ready{s}"].next())
                        pool.wait_ge(sems["tiles_done"], slot_empty(l, sec, i, j))
                        nc.gpsimd.tensor_tensor(w_lo[s][:, 0:n], raw[r][:, 0:n], w_hi[s][:, 0:n].bitcast(F32),
                                                ALU.subtract).then_inc(*b[f"lo_ready{r}"].one())



    @block.scalar
    def _(act):
        b = book(act, "act")
        step = b["a_step"]

        def hi(l, sec, i, j):
            _, nk, split, r, s = sec.loads[j]
            if not split:
                b[f"dma_w{r}"].skip()
                return
            act.wait_ge(*b[f"dma_w{r}"].next())
            act.wait_ge(sems["tiles_done"], slot_empty(l, sec, i, j))
            nc.scalar.activation(w_hi[s][:, 0:nk * P], raw[r][:, 0:nk * P], ACT.Copy).then_inc(
                *b[f"hi_ready{s}"].one())

        def first(l, sec):
            for j in range(sec.lead):
                hi(l, sec, 0, j)

        def dense(l, sec, evacuate):
            with b.passing(sec):
                if sec.trips > 1:
                    with b.loop(sec.trips - 1, sec.tag) as i:
                        for j in range(sec.n):
                            a = j + sec.lead
                            hi(l, sec, i + a // sec.n if a >= sec.n else i, a % sec.n)
                            evacuate(i, j)
                for j in range(sec.n):
                    if j + sec.lead < sec.n:
                        hi(l, sec, sec.trips - 1, j + sec.lead)
                    evacuate(sec.trips - 1, j)

        def tile_done(l, sec, i, j):
            act.wait_ge(sems["tiles_done"], done(l, sec, i, j))

        def squares(fresh=True):
            for k in range(KD):
                if fresh:
                    act.wait_ge(*b["h_ready"].next())
                nc.scalar.activation(tmp[:, k, :], h[:, k, :], ACT.Square).then_inc(*b["squares"].one())

        def inverse_root(dst, src, scale, count):
            nc.scalar.activation(dst, src, ACT.Ln, scale=scale, bias=eps_c).then_inc(*step.one())
            act.wait_ge(*step.now())
            nc.scalar.activation(dst, dst, ACT.Exp, scale=-0.5).then_inc(*count.one())

        def root(half=False):
            act.wait_ge(*b["norm_sum"].next())
            nc.scalar.activation(rms[:, :], mix[:, 0, 0:T], ACT.Sqrt, scale=(4.0 if half else 1.0) / D_MODEL,
                                 bias=c_["eps4"] if half else eps_c).then_inc(*b["root"].one())

        def gating(l, sec, func):
            def evacuate(i, j):
                q = sec.banks[j]
                if q % 2 == 0:
                    tile_done(l, sec, i, j)
                    act.wait_ge(*b[f"bank_free{q + 1}"].now())
                    b[f"bank_free{q + 1}"].skip()
                    nc.scalar.activation(gate_s[q // 2][:, :], psum[q][:, 0:T], func).then_inc(
                        *b[f"bank_free{q}"].one())
            return evacuate

        def with_squares(l, sec, to):
            def evacuate(i, j):
                out = to(i, j)
                if out is None:
                    return
                q, k = out
                tile_done(l, sec, i, j)
                nc.scalar.activation(y[:, k, :], psum[q][:, 0:T], ACT.Copy)
                nc.scalar.activation(tmp[:, k, :], psum[q][:, 0:T], ACT.Square).then_inc(*b[f"bank_free{q}"].one())
            return evacuate

        def copying(l, sec, to):
            def evacuate(i, j):
                q, dst = to(i, j)
                tile_done(l, sec, i, j)
                nc.scalar.activation(dst, psum[q][:, 0:T], ACT.Copy).then_inc(*b[f"bank_free{q}"].one())
            return evacuate

        def padded(l, sec, first_tile):
            def evacuate(i, j):
                if sec.name == "tail" and j == 2:
                    tile_done(l, sec, i, j)
                    nc.scalar.activation(rows[:, :], psum[j][0:ROWS, 0:T], ACT.Copy).then_inc(
                        *b[f"bank_free{j}"].one())
                    return
                m = sec.n * i + (first_tile + j)
                tile_done(l, sec, i, j)
                nc.scalar.activation(xp[:, m, 3:3 + SEQ], psum[j][:, 0:SEQ], ACT.Copy)
                nc.scalar.activation(
                    xp[:, m, 3 + SEQ:XW].rearrange("p (s t) -> p s t", s=DEC_BATCH)[:, :, 3:],
                    psum[j][:, SEQ:T].rearrange("p (s t) -> p s t", s=DEC_BATCH), ACT.Copy).then_inc(
                    *b[f"bank_free{j}"].one())
            return evacuate

        def wait_copies():
            for q in range(4):
                act.wait_ge(*b[f"bank_free{q}"].now())

        def rows_and_tokens(l):
            nc.scalar.activation(rt[:, :], rows[:, :], ACT.Sigmoid).then_inc(*step.one())
            act.wait_ge(*step.now())
            act.wait_ge(*b["row_x"].next())
            nc.scalar.activation(re[:, :], rx[:, :], ACT.Abs).then_inc(*step.one())
            act.wait_ge(*step.now())
            nc.scalar.activation(re[:, :], re[:, :], ACT.Exp, scale=-1.0).then_inc(*step.one())
            nc.scalar.activation(lb[0:ROWS, 30:31], vec[0:ROWS, V_RA:V_RA + 1], ACT.Exp).then_inc(*b["row_e"].one())
            act.wait_ge(*b["bound_d"].next())
            nc.scalar.activation(lb[:, 4:12], lb[:, 4:12], ACT.Exp).then_inc(*b["bound_e"].one())
            act.wait_ge(*b["row_u"].next())
            nc.scalar.activation(rl[:, :], ru[:, :], ACT.Ln).then_inc(*b["row_ln"].one())
            for t, (t0, n) in enumerate(TILES3):
                act.wait_ge(*b["tok_t"].next())
                nc.scalar.activation(la_tok[0:n, t, 0:8], psum[t][0:n, 0:8], ACT.Copy)
                nc.scalar.activation(la_tok[0:n, t, 12:16], psum[t][0:n, 32:36], ACT.Copy)
                nc.scalar.activation(beta_tok[0:n, t, :], psum[t][0:n, 64:68], ACT.Copy)
                nc.scalar.activation(dt_tok[0:n, t, :], psum[t][0:n, 128:136], ACT.Copy)
                nc.scalar.activation(la_tok[0:n, t, 8:12], c_["lgam"][0:n, :], ACT.Copy).then_inc(*b["tok_copied"].one())
            act.wait_ge(*b["tok_exp"].next())
            for t, (t0, n) in enumerate(TILES3):
                nc.scalar.activation(to_end[0:n, t, :], to_end[0:n, t, :], ACT.Exp).then_inc(*step.one())
                nc.scalar.activation(ecum_tok[0:n, t, :], cum_tok[0:n, t, :], ACT.Exp).then_inc(*b["tok_ready"].one())

        def convolutions(l):
            act.wait_ge(*b["conv_saved"].next())
            for m in range(NCONV):
                act.wait_ge(*b["conv_sum"].next())
                acc = cacc[m % 2]
                bias = {"bias": vec[:, V_CB + m:V_CB + m + 1]} if m < 6 else {}
                nc.scalar.activation(xp[:, m, 0:SEQ], acc[:, 0:SEQ], ACT.Silu, **bias)
                nc.scalar.activation(xp[:, m, SEQ:T].rearrange("p (s t) -> p s t", s=NS),
                                     acc_sample(acc), ACT.Silu, **bias).then_inc(*b["conv_done"].one())

        def unit_norms(l):
            act.wait_ge(*b["conv_done"].now())
            for half in range(2):
                for e in range(4):
                    if half:
                        act.wait_ge(*b["l2_sum"].now())
                    nc.scalar.activation(lsq[e][:, :], xp[:, 6 + 4 * half + e, 0:T], ACT.Square).then_inc(*b["l2_sq"].one())
                b["l2_sum"].skip(4)
                act.wait_ge(*b["l2_sum"].now())
                if half:
                    act.wait_ge(*b["l2_done"].next())
                inverse_root(lrt[:, :, :], mix[:, :, 0:T], 1.0, b["l2_root"])
            b["l2_done"].skip()

        def silus(l):
            for at in (Z, HG, RG, GZ):
                nc.scalar.activation(proj[:, at:at + 4, :], proj[:, at:at + 4, :], ACT.Silu).then_inc(*b["silus"].one())

        def hgrn(l):
            nc.scalar.activation(proj[:, HQ:HQ + 4, :], proj[:, HQ:HQ + 4, :], ACT.Silu).then_inc(*step.one())
            nc.scalar.activation(proj[:, HF:HF + 4, :], proj[:, HF:HF + 4, :], ACT.Sigmoid).then_inc(*b["hg_sig"].one())

        def f_norm(scale, banks, src):
            act.wait_ge(*b["f_pre"].next())
            nc.scalar.activation(f_sq.rearrange("p (k t) -> p k t", k=4), src, ACT.Square).then_inc(*b["f_sq"].one())
            act.wait_ge(*b["f_sum"].next())
            if banks == 4:
                inverse_root(f_rt.rearrange("p (k t) -> p k t", k=4), mix[:, :, 0:T], scale, b["f_root"])
            else:
                inverse_root(f_rt[:, 0:T], mix[:, 0, 0:T], scale, b["f_root"])

        def scalar_decay(l):
            for kind, g in GROUPS:
                if kind == "gdn":
                    act.wait_ge(*b["f_root"].now())
                for t, (t0, n) in enumerate(TILES3):
                    if kind == "hg":
                        act.wait_ge(*b["scores"].next())
                        nc.scalar.activation(vtok[0:n, :], psum[3][0:n, :], ACT.Copy).then_inc(*b["v_copied"].one())
                        act.wait_ge(*b["o_done"].next())
                        nc.scalar.activation(ho[:, :, t0:t0 + n], mix[:, 0, 0:4 * n].rearrange("p (k t) -> p k t", k=4),
                                             ACT.Copy).then_inc(*b["o_copied"].one())
                        continue
                    act.wait_ge(*b["cum_bc"].next())
                    nc.scalar.activation(ecb[:, 0:4 * n], psum[0][:, 0:4 * n], ACT.Exp).then_inc(*b["ecb_ready"].one())
                    act.wait_ge(*b["dec_d"].next())
                    nc.scalar.activation(em[0:n, 0:4 * n], dm[0:n, 0:4 * n], ACT.Exp).then_inc(*b["dec_e"].one())
                    if kind == "gdn":
                        nc.scalar.activation(dm2[0:n, 0:4 * n], dm2[0:n, 0:4 * n], ACT.Exp, scale=-1.0).then_inc(
                            *b["dec_e"].one())
                    act.wait_ge(*b["scores"].next())
                    w = 256 if kind == "mb" else 512
                    nc.scalar.activation(vtok[0:n, 0:w], psum[3][0:n, 0:w], ACT.Copy).then_inc(*b["v_copied"].one())
                    if kind == "gdn":
                        def copy(dst, src, **kw):
                            act.wait_ge(*b["gdn_mm"].next())
                            nc.scalar.activation(dst, src, ACT.Copy, **kw).then_inc(*b["gdn_ev"].one())
                        m = 4 * n
                        copy(W[2][0:n, 0:m], psum[1][0:n, 0:m])
                        b["gdn_mm"].skip()
                        copy(W[5][0:n, 0:m], psum[2][0:n, 0:m])
                        b["gdn_mm"].skip()
                        copy(W[4][0:n, 0:m], psum[2][0:n, 0:m])
                        copy(W[2][0:n, 0:m], psum[1][0:n, 0:m])
                        if t < 2:
                            copy(W[5][0:n, 0:m], psum[2][0:n, 0:m])
                            for m2 in (16, 32, 64, 128):
                                copy(W[6][0:n, 0:m], psum[1][0:n, 0:m])
                                b["gdn_mm"].skip()
                                if m2 < 128:
                                    copy(W[5][0:n, 0:m], psum[1][0:n, 0:m])
                        if t:
                            copy(nsk[:, 0:m], psum[1][:, 0:m], scale=-1.0)
                        if t < 2:
                            copy(wn[0:n, :], psum[2][0:n, :])
                        else:
                            copy(W[6][:, 0:m], psum[2][:, 0:m])
                            copy(wn[0:n, :], psum[1][0:n, :])
                    act.wait_ge(*b["o_done"].next())
                    if kind == "mb":
                        nc.scalar.activation(f_o.rearrange("p (k t) -> p k t", k=4)[:, 2 * g:2 * g + 2, t0:t0 + n],
                                             mix[:, 0, 0:2 * n].rearrange("p (k t) -> p k t", k=2), ACT.Copy).then_inc(
                            *b["o_copied"].one())
                    elif kind == "gdn":
                        nc.scalar.activation(xp[:, 0:4, t0:t0 + n], mix[:, 0, 0:4 * n].rearrange("p (k t) -> p k t", k=4),
                                             ACT.Copy).then_inc(*b["o_copied"].one())
                    else:
                        for r in range(2):
                            nc.scalar.activation(xp[:, r:4:2, t0:t0 + n],
                                                 mix[:, r, 0:2 * n].rearrange("p (k t) -> p k t", k=2),
                                                 ACT.Copy).then_inc(*b["o_copied"].one())
                if (kind, g) != ("mb", 0):
                    if kind == "mb":
                        f_norm(1.0 / 512, 1, f_ok)
                    else:
                        f_norm(1.0 / P, 4, ho[:, :, :] if kind == "hg" else xp[:, 0:4, 0:T])

        act.wait_ge(b["dma_in"].sem, 32)
        with b.loop(DEPTH, "layer") as l:
            for f in range(2):
                up, down = sections[f"up{f}"], sections[f"down{f}"]
                first(l, up)
                if f == 0:
                    act.wait_ge(*b["h_ready"].now())
                squares(fresh=f == 1)
                root()
                dense(l, up, gating(l, up, ACT.Silu))
                first(l, down)
                dense(l, down, with_squares(l, down, lambda i, j: (j // 3, 4 * i + j // 3) if j % 3 == 2 else None))
                if f == 0:
                    first(l, sections["proj0"])
                root(half=True)
                if f == 1:
                    b["h_ready"].skip(KD)
                    continue
                squares()
                root()
                sec = sections["proj0"]
                dense(l, sec, copying(l, sec, lambda i, j: (j, proj[:, 4 * i + j, :])))
                sec = sections["conv0"]
                first(l, sec)
                dense(l, sec, padded(l, sec, 0))
                sec = sections["tail0"]
                first(l, sec)
                dense(l, sec, padded(l, sec, 16))
                wait_copies()
                nc.scalar.sem_inc(sems["projected"], 1)
                rows_and_tokens(l)
                convolutions(l)
                unit_norms(l)
                silus(l)
                hgrn(l)
                scalar_decay(l)
                sec = sections["merge0"]
                first(l, sec)
                dense(l, sec, gating(l, sec, ACT.Sigmoid))
                sec = sections["out0"]
                first(l, sec)
                dense(l, sec, with_squares(l, sec, lambda i, j: (j, 4 * i + j)))
                root()

    @block.vector
    def _(dve):
        b = book(dve, "dve")
        step = b["v_step"]



        def inverse():
            dve.wait_ge(*b["root"].next())
            nc.vector.reciprocal(rms[:, :], rms[:, :]).then_inc(*step.one())
            dve.wait_ge(*step.now())

        def norm_in(g):
            inverse()
            for k in range(KD + 2):
                own, at = step.now()
                if k < KD:
                    nc.vector.scalar_tensor_tensor(out=tmp[:, k, :], in0=h[:, k, :],
                                                   scalar=vec[:, g * KD + k:g * KD + k + 1], in1=rms[:, :], op0=ALU.mult,
                                                   op1=ALU.mult).then_inc(*step.one())
                if 1 <= k <= KD:
                    dve.wait_ge(own, at)
                    nc.vector.tensor_copy(u_hi[:, k - 1, :], tmp[:, k - 1, :]).then_inc(*step.one())
                if k >= 2:
                    dve.wait_ge(own, at)
                    nc.vector.tensor_tensor(u_lo[:, k - 2, :], tmp[:, k - 2, :], u_hi[:, k - 2, :].bitcast(F32),
                                            ALU.subtract).then_inc(*b["u_ready"].one())

        def norm_out(g):
            inverse()
            for k in range(KD + 1):
                if k < KD:
                    nc.vector.scalar_tensor_tensor(out=tmp[:, k, :], in0=y[:, k, :], scalar=vec[:, g * KD + k:g * KD + k + 1],
                                                   in1=rms[:, :], op0=ALU.mult, op1=ALU.mult).then_inc(*step.one())
                if k:
                    own, at = step.now()
                    dve.wait_ge(own, at - (k < KD))
                    nc.vector.tensor_tensor(h[:, k - 1, :], h[:, k - 1, :], tmp[:, k - 1, :], ALU.add).then_inc(
                        *b["h_ready"].one())
            dve.wait_ge(*b["h_ready"].now())

        def gated(l, sec, i, j):
            q = sec.banks[j]
            dve.wait_ge(*b[f"bank_free{q - 1}"].next())
            dve.wait_ge(sems["tiles_done"], done(l, sec, i, j))
            nc.vector.tensor_tensor(hid_t[q // 2][:, :], gate_s[q // 2][:, :], psum[q][:, 0:T],
                                    ALU.mult).then_inc(*b[f"bank_free{q}"].one())
            dve.wait_ge(*b[f"bank_free{q}"].now())
            return hid_t[q // 2][:, :]

        def hidden(l, f):
            sec = sections[f"up{f}"]
            with b.passing(sec), b.loop(sec.trips, sec.tag) as i:
                for m in range(2):
                    t = gated(l, sec, i, 2 * m + 1)
                    nc.vector.tensor_copy(hid_hi[:, 2 * i + m, :], t).then_inc(*step.one())
                    dve.wait_ge(*step.now())
                    nc.vector.tensor_tensor(hid_lo[:, 2 * i + m, :], t, hid_hi[:, 2 * i + m, :].bitcast(F32),
                                            ALU.subtract).then_inc(*b["hid_ready"].one())
            with b.passing(sections[f"down{f}"]):
                pass


        def rows_and_tokens(l):
            V = nc.vector
            V.tensor_scalar(rx[:, :], rows[:, :], vec[0:ROWS, V_RB:V_RB + 1], None, ALU.add).then_inc(*b["row_x"].one())
            V.tensor_tensor(lb[:, 0:4], vec[:, V_LB:V_LB + 4], vec[:, V_LB + 4:V_LB + 8], ALU.max).then_inc(*step.one())
            dve.wait_ge(*step.now())
            for x in range(2):
                V.tensor_tensor(lb[:, 4 + 4 * x:8 + 4 * x], vec[:, V_LB + 4 * x:V_LB + 4 * x + 4], lb[:, 0:4],
                                ALU.subtract).then_inc(*(step if x == 0 else b["bound_d"]).one())
            dve.wait_ge(*b["row_e"].next())
            V.tensor_scalar(ru[:, :], re[:, :], 1.0, None, ALU.add).then_inc(*b["row_u"].one())
            fix, inv = cacc[0][0:ROWS, 0:T], cacc[1][0:ROWS, 0:T]
            dve.wait_ge(*b["row_u"].now())
            V.tensor_scalar(fix, ru[:, :], -1.0, None, ALU.add).then_inc(*step.one())
            V.reciprocal(inv, ru[:, :]).then_inc(*step.one())
            V.tensor_scalar(rx[:, :], rx[:, :], 0.0, None, ALU.max).then_inc(*step.one())
            dve.wait_ge(*step.now())
            V.tensor_tensor(fix, fix, re[:, :], ALU.subtract).then_inc(*step.one())
            dve.wait_ge(*step.now())
            V.tensor_tensor(fix, fix, inv, ALU.mult).then_inc(*step.one())
            dve.wait_ge(*b["row_ln"].next())
            V.tensor_tensor(rl[:, :], rl[:, :], rx[:, :], ALU.add).then_inc(*step.one())
            dve.wait_ge(*step.now())
            V.tensor_tensor(rl[:, :], rl[:, :], fix, ALU.subtract).then_inc(*step.one())
            dve.wait_ge(*step.now())
            V.tensor_scalar(rb[0:64, :], rl[0:64, :], lb[0:64, 30:31], -1.0, ALU.mult, ALU.mult)
            V.tensor_copy(rb[64:ROWS, :], rt[64:ROWS, :]).then_inc(*b["rows_ready"].one())
            dve.wait_ge(*b["bound_e"].next())
            V.tensor_tensor(lb[:, 12:16], lb[:, 4:8], lb[:, 8:12], ALU.add).then_inc(*step.one())
            dve.wait_ge(*step.now())
            V.reciprocal(lb[:, 12:16], lb[:, 12:16]).then_inc(*step.one())
            dve.wait_ge(*step.now())
            V.tensor_tensor(lb[:, 16:20], lb[:, 4:8], lb[:, 12:16], ALU.mult)
            V.tensor_tensor(lb[:, 20:24], lb[:, 8:12], lb[:, 12:16], ALU.mult).then_inc(*step.one())
            dve.wait_ge(*step.now())
            V.tensor_tensor(lb[:, 24:28], lb[:, 16:20], lb[:, 20:24], ALU.add).then_inc(*step.one())
            dve.wait_ge(*step.now())
            V.tensor_tensor(lb[:, 24:28], lb[:, 24:28], lb[:, 16:20], ALU.subtract).then_inc(*step.one())
            dve.wait_ge(*step.now())
            V.tensor_scalar(lb[:, 24:28], lb[:, 24:28], vec[:, V_ON:V_ON + 1], None, ALU.mult).then_inc(*step.one())
            dve.wait_ge(*step.now())
            V.tensor_scalar(lb[:, 20:24], lb[:, 24:28], -1.0, 1.0, ALU.mult, ALU.add).then_inc(*step.one())
            for t, (t0, n) in enumerate(TILES3):
                dve.wait_ge(*b["tok_sums"].next())
                V.tensor_copy(cum_tok[0:n, t, :], psum[t][0:n, 0:16]).then_inc(*step.one())
            dve.wait_ge(*step.now())
            for t, (t0, n) in enumerate(TILES3):
                V.tensor_tensor(to_end[0:n, t, :], psum[t][0:n, 16:32], cum_tok[0:n, t, :], ALU.subtract).then_inc(
                    *(step if t < 2 else b["tok_exp"]).one())
            for t, (t0, n) in enumerate(TILES3):
                dve.wait_ge(*b["tok_ready"].next())
                V.tensor_tensor(to_end_dt[0:n, t, :], to_end[0:n, t, 0:8], dt_tok[0:n, t, :], ALU.mult)
                V.tensor_tensor(beta_cum[0:n, t, :], ecum_tok[0:n, t, 12:16], beta_tok[0:n, t, :], ALU.mult).then_inc(*step.one())

        def convolutions(l):
            dve.wait_ge(*b["conv_filled"].next())
            n = XW - 3
            for m in range(0, NCONV, 2):
                for j in range(4):
                    for e in range(2):
                        tap = vec[:, V_CW + 4 * (m + e) + j:V_CW + 4 * (m + e) + j + 1]
                        src, acc = xp[:, m + e, j:j + n], cacc[e][:, 0:n]
                        if j == 0:
                            if m:
                                dve.wait_ge(*b["conv_done"].next())
                            nc.vector.tensor_scalar(acc, src, tap, None, ALU.mult).then_inc(*step.one())
                            continue
                        own, at = step.now()
                        dve.wait_ge(own, at - ((j, e) != (3, 1)))
                        nc.vector.scalar_tensor_tensor(out=acc, in0=src, scalar=tap, in1=acc, op0=ALU.mult,
                                                       op1=ALU.add).then_inc(*(step if j < 3 else b["conv_sum"]).one())
            b["conv_done"].skip(2)

        def unit_norms(l):
            for half in range(2):
                dve.wait_ge(*b["l2_root"].next())
                x = xp[:, 6 + 4 * half:10 + 4 * half, 0:T]
                if half:
                    nc.vector.tensor_tensor(x, x, lrt[:, :, :], ALU.mult).then_inc(*b["l2_done"].one())
                else:
                    nc.vector.scalar_tensor_tensor(out=x, in0=x, scalar=P ** -0.5, in1=lrt[:, :, :], op0=ALU.mult,
                                                   op1=ALU.mult).then_inc(*b["l2_done"].one())

        def hgrn(l):
            V = nc.vector
            dve.wait_ge(*b["hg_sig"].next())
            dve.wait_ge(*b["dma_conv_out"].next())
            for k in range(4):
                V.tensor_scalar(hf1[:, k * T:(k + 1) * T], proj[:, HF + k, :], lb[:, 20 + k:21 + k], lb[:, 24 + k:25 + k],
                                ALU.mult, ALU.add).then_inc(*step.one())
            dve.wait_ge(*step.now())
            f1 = hf1[:, :].rearrange("p (k t) -> p k t", k=4)
            V.tensor_scalar(proj[:, HF:HF + 4, :], f1, -1.0, 1.0, ALU.mult, ALU.add).then_inc(*b["hg_q"].one())
            fades = f1
            for level, s in enumerate((0, 1, 2, 4, 8, 16, 32, 64)):
                dve.wait_ge(*b["hg_sc"].next())
                dve.wait_ge(*b["hg_q"].now())
                if s == 0:
                    V.tensor_tensor(proj[:, HQ:HQ + 4, :], proj[:, HQ:HQ + 4, :], f1, ALU.mult).then_inc(*b["hg_q"].one())
                else:
                    width = T if s < 8 else SEQ
                    nb = width // (2 * s)
                    pairs = fades.rearrange("p k (c two) -> p k c two", two=2)

                    def halves(at, which):
                        return proj[:, at:at + 4, 0:width].rearrange("p k (c two t) -> p k c two t", two=2, t=s)[:, :, :, which]

                    for at, which in ((HQ, 1), (HF, 0)):
                        x = halves(at, which)
                        V.tensor_tensor(x, x, over(pairs[:, :, :, 1 - which:2 - which], [P, 4, nb, s]), ALU.mult).then_inc(
                            *step.one())
                    if s == 4:
                        new = hf8[:, :, :]
                    elif s == 64:
                        new = hf128[:, :, :]
                    else:
                        new = (hf2 if level % 2 else hf1)[:, 0:4 * nb].rearrange("p (k c) -> p k c", k=4)
                    V.tensor_tensor(new, pairs[:, :, :, 0], pairs[:, :, :, 1], ALU.mult).then_inc(*b["hg_q"].one())
                    fades = hf8[:, :, 0:SEQ // 8] if s == 4 else new
                mask = c_["ident"] if s == 0 else c_[f"next{2 * s}"]
                parts = [(mix[:, 2 * (level % 2):2 * (level % 2) + 2, :].rearrange("p t (k i) -> p (t k) i", i=P), P, 0, 8)]
                if s < 8:
                    parts.append((psum[level % 2][0:64, 0:256].rearrange("p (k i) -> p k i", i=64), 64, 1024, 4))
                dve.wait_ge(*step.now())
                for src, n, c0, count in parts:
                    dst = (ht if level else hp)[0:n, c0:c0 + count * n].rearrange("p (k i) -> p k i", i=n)
                    V.tensor_tensor(dst, src, over(mask[0:n, 0:n].unsqueeze(1), [n, count, n]), ALU.mult).then_inc(*step.one())
                if level:
                    dve.wait_ge(*step.now())
                    for _, n, c0, count in parts:
                        sl = slice(c0, c0 + count * n)
                        V.tensor_tensor(hp[0:n, sl], hp[0:n, sl], ht[0:n, sl], ALU.add).then_inc(
                            *(b["hg_ready"] if s == 64 else step).one())
            dve.wait_ge(*b["hg_ready"].now())

        def rotate(l):
            dve.wait_ge(*b["rot_ps"].next())
            turned = f_sq.rearrange("p (k t) -> p k t", k=4)
            x = proj[:, RQ:RQ + 4, :]
            nc.vector.tensor_tensor(turned, mix[:, :, 0:T], over(c_["sin"].unsqueeze(1), [P, 4, T]), ALU.mult)
            nc.vector.tensor_tensor(x, x, over(c_["cos"].unsqueeze(1), [P, 4, T]), ALU.mult).then_inc(*step.one())
            dve.wait_ge(*step.now())
            nc.vector.tensor_tensor(x, x, turned, ALU.add).then_inc(*step.one())
            dve.wait_ge(*step.now())
            nc.vector.tensor_scalar(proj[:, RK:RK + 2, :], proj[:, RK:RK + 2, :], 64 ** -0.5, None, ALU.mult).then_inc(
                *b["rotated"].one())

        def by_head(x, n):
            return x.rearrange("p (k i) -> p k i", i=n)

        def odd_even(x, n, r):
            return x.rearrange("p (k r i) -> p r k i", r=2, i=n)[:, r]

        def delta_rule(t, t0, n):
            V, m = nc.vector, 4 * n
            heads = lambda i: by_head(W[i][0:n, 0:m], n)
            eye = over(c_["ident"][0:n, 0:n].unsqueeze(1), [n, 4, n])
            dve.wait_ge(*b["dec_e"].next())
            for k in range(4):
                V.scalar_tensor_tensor(out=W[0][0:n, k * n:(k + 1) * n], in0=psum[2][0:n, k * n:(k + 1) * n],
                                       scalar=beta_tok[0:n, t, k:k + 1], in1=dm2[0:n, k * n:(k + 1) * n], op0=ALU.mult,
                                       op1=ALU.mult).then_inc(*(step if t < 2 or k < 3 else b["gdn_v"]).one())
            if t < 2:
                dve.wait_ge(*step.now())
                V.tensor_tensor(heads(1), heads(0), over(c_["b8"].unsqueeze(1), [n, 4, n]), ALU.mult).then_inc(
                    *b["gdn_v"].one())
            dve.wait_ge(*b["gdn_ev"].next())
            V.tensor_tensor(heads(3), eye, heads(2), ALU.subtract).then_inc(*step.one())
            b["gdn_mm"].skip()
            dve.wait_ge(*b["gdn_mm"].next())
            V.tensor_copy(W[4][0:n, 0:m], psum[1][0:n, 0:m]).then_inc(*b["gdn_v"].one())
            dve.wait_ge(*b["gdn_ev"].next())
            V.tensor_tensor(heads(6), eye, heads(5), ALU.add).then_inc(*step.one())
            b["gdn_mm"].skip()
            dve.wait_ge(*b["gdn_mm"].next())
            V.tensor_tensor(heads(1), eye, by_head(psum[1][0:n, 0:m], n), ALU.add).then_inc(*b["gdn_v"].one())
            b["gdn_mm"].skip(2)
            b["gdn_ev"].skip(2)
            if t < 2:
                b["gdn_mm"].skip()
                b["gdn_ev"].skip()
                for m2 in (16, 32, 64, 128):
                    dve.wait_ge(*b["gdn_mm"].now())
                    V.tensor_tensor(heads(1), heads(0), over(c_[f"b{m2}"].unsqueeze(1), [n, 4, n]), ALU.mult).then_inc(
                        *b["gdn_v"].one())
                    b["gdn_mm"].skip()
                    b["gdn_ev"].skip()
                    dve.wait_ge(*b["gdn_mm"].next())
                    V.tensor_tensor(W[2][0:n, 0:m], W[2][0:n, 0:m], psum[2][0:n, 0:m], ALU.subtract).then_inc(
                        *b["gdn_v"].one())
                    if m2 < 128:
                        b["gdn_mm"].skip()
                        b["gdn_ev"].skip()
            b["gdn_mm"].skip(1 + (t > 0) + (t == 2))
            b["gdn_ev"].skip(1 + (t > 0) + (t == 2))

        def new_state(kind, g, t, n):
            V = nc.vector
            at = {"hg": 0, "mb": 0, "ret": 256, "gdn": 0}[kind]
            width = 64 if kind == "mb" else P
            own = {"hg": HGRN, "mb": MB, "ret": RET, "gdn": GDN}[kind]

            def place(k):
                if kind == "mb":
                    return slice(64 * g, 64 * g + 64), k
                if kind == "ret":
                    return slice(64 * (k % 2), 64 * (k % 2) + 64), k // 2
                return slice(0, P), k

            if t < 2:
                dve.wait_ge(*b["state_mm"].next())
                for k in range(4):
                    pr, pos = place(k)
                    dst, src = state[own][pr, pos, :], mix[pr, 3, pos * width:(pos + 1) * width]
                    if t == 0:
                        up = V.tensor_copy(dst, src)
                    else:
                        whole = hf128[:, k, 1:2] if kind == "hg" else ecb[pr, k * n + n - 1:k * n + n]
                        up = V.scalar_tensor_tensor(out=dst, in0=dst, scalar=whole, in1=src,
                                                    op0=ALU.mult, op1=ALU.add)
                    up.then_inc(*(step if k < 3 else b["state_new"]).one())
                return

            def masked(k):
                src = wn if kind == "gdn" else vtok
                V.tensor_tensor(vm[k % 2][:, 0:NS * width].rearrange("p (s d) -> p s d", s=NS),
                                over(src[0:n, k * width:(k + 1) * width].unsqueeze(1), [n, NS, width]),
                                over(c_["pick"][0:n, :].unsqueeze(2), [n, NS, width]), ALU.mult).then_inc(
                    *b["vm_ready"].one())

            dve.wait_ge(*b["o_done"].now())
            masked(0)
            masked(1)
            for k in range(4):
                pr, pos = place(k)
                dst = st_s[pr, :, at + pos * width:at + (pos + 1) * width]
                rows_ = pr.stop - pr.start
                if kind == "hg":
                    whole = hf8[:, k, SEQ // 8:].unsqueeze(2)
                else:
                    whole = ecb[pr, k * n:(k + 1) * n].rearrange("p (s t) -> p s t", t=C)[:, :, C - 1:C]
                V.tensor_tensor(dst, dst, over(whole, [rows_, NS, width]), ALU.mult).then_inc(*step.one())
                dve.wait_ge(*b["state_mm"].next())
                dve.wait_ge(*step.now())
                bank = 2 if k % 2 == 0 else 0
                kvs = mix[pr, bank:bank + NS * width // 512, :].rearrange("p b f -> p (b f)").rearrange("p (s d) -> p s d", s=NS)
                V.tensor_tensor(dst, dst, kvs, ALU.add).then_inc(*(step if k < 3 else b["state_new"]).one())
                if k < 2:
                    masked(k + 2)

        def scalar_decay(l):
            V = nc.vector
            for kind, g in GROUPS:
                col = {"hg": 0, "mb": 4 * g, "ret": RET, "gdn": GDN}[kind]
                b["dma_state"].skip({("mb", 0): 2, ("hg", 0): 1, ("gdn", 0): 1}.get((kind, g), 0))
                if (kind, g) == ("mb", 0):
                    rotate(l)
                for t, (t0, n) in enumerate(TILES3):
                    m = 4 * n
                    if kind == "hg":
                        dve.wait_ge(*b["scores"].next())
                        V.tensor_copy(kend[0:n, :], mix[0:n, 2, :]).then_inc(*b["k_ready"].one())
                        b["v_copied"].skip()
                        b["o_done"].skip()
                        if t == 2:
                            dve.wait_ge(*b["v_copied"].now())
                            dve.wait_ge(*b["dma_state"].now())
                        new_state(kind, g, t, n)
                        b["o_copied"].skip()
                        continue
                    dve.wait_ge(*b["ecb_ready"].next())
                    neg, pos = (c_["neg"], c_["pos"]) if t < 2 else (c_["neg_s"][0:n, :], c_["pos_s"][0:n, :])
                    for k in range(4):
                        cum = cum_tok[0:n, t, col + k:col + k + 1]
                        src, sl = psum[0][0:n, k * n:(k + 1) * n], slice(k * n, (k + 1) * n)
                        last = V.scalar_tensor_tensor(out=dm[0:n, sl], in0=src, scalar=cum, in1=neg, op0=ALU.subtract,
                                                      op1=ALU.add)
                        if kind == "gdn":
                            last = V.scalar_tensor_tensor(out=dm2[0:n, sl], in0=src, scalar=cum, in1=pos,
                                                          op0=ALU.subtract, op1=ALU.add)
                    last.then_inc(*b["dec_d"].one())
                    dve.wait_ge(*b["scores"].next())
                    dve.wait_ge(*b["dec_e"].next())
                    if kind == "mb":
                        for k in range(4):
                            V.scalar_tensor_tensor(out=pm[0:n, k * n:(k + 1) * n], in0=psum[1][0:n, 0:n],
                                                   scalar=dt_tok[0:n, t, col + k:col + k + 1],
                                                   in1=em[0:n, k * n:(k + 1) * n], op0=ALU.mult, op1=ALU.mult).then_inc(
                                *(step if k < 3 else b["p_ready"]).one())
                    elif kind == "ret":
                        for r in range(2):
                            V.tensor_tensor(odd_even(pm[0:n, 0:m], n, r), by_head(psum[1 + r][0:n, 0:2 * n], n),
                                            odd_even(em[0:n, 0:m], n, r), ALU.mult).then_inc(
                                *(step if r == 0 else b["p_ready"]).one())
                    else:
                        V.tensor_tensor(pm[0:n, 0:m], psum[1][0:n, 0:m], em[0:n, 0:m], ALU.mult).then_inc(*b["p_ready"].one())
                    if t:
                        if kind == "mb":
                            pr = slice(64 * g, 64 * g + 64)
                            V.tensor_tensor(by_head(qd[pr, 0:m], n), over(xp[pr, 5, t0:t0 + n].unsqueeze(1), [64, 4, n]),
                                            by_head(ecb[pr, 0:m], n), ALU.mult).then_inc(*b["q_ready"].one())
                        elif kind == "ret":
                            for r in range(2):
                                pr = slice(64 * r, 64 * r + 64)
                                V.tensor_tensor(odd_even(qd[pr, 0:m], n, r), proj[pr, RQ:RQ + 2, t0:t0 + n],
                                                odd_even(ecb[pr, 0:m], n, r), ALU.mult).then_inc(
                                    *(step if r == 0 else b["q_ready"]).one())
                        else:
                            V.tensor_tensor(by_head(qd[:, 0:m], n), xp[:, 6:10, t0:t0 + n], by_head(ecb[:, 0:m], n),
                                            ALU.mult).then_inc(*b["q_ready"].one())
                    if kind == "mb":
                        V.tensor_tensor(by_head(kend[0:n, 0:256], 64), over(mix[0:n, 2, 64 * g:64 * g + 64].unsqueeze(1), [n, 4, 64]),
                                        over(to_end_dt[0:n, t, col:col + 4].unsqueeze(2), [n, 4, 64]), ALU.mult).then_inc(
                            *b["k_ready"].one())
                    elif kind == "ret":
                        V.tensor_tensor(by_head(kend[0:n, 0:256], 64), by_head(mix[0:n, 2, 0:256], 64),
                                        over(to_end[0:n, t, RET:RET + 4].unsqueeze(2), [n, 4, 64]), ALU.mult).then_inc(
                            *b["k_ready"].one())
                    else:
                        keys = by_head(mix[0:n, 2, :], P)
                        V.tensor_tensor(by_head(kend[0:n, :], P), keys, over(to_end[0:n, t, GDN:GDN + 4].unsqueeze(2), [n, 4, P]),
                                        ALU.mult)
                        V.tensor_tensor(by_head(kb[0:n, :], P), keys, over(beta_cum[0:n, t, :].unsqueeze(2), [n, 4, P]),
                                        ALU.mult).then_inc(*b["k_ready"].one())
                        dve.wait_ge(*b["v_copied"].now())
                    b["v_copied"].skip()
                    if kind == "gdn":
                        dve.wait_ge(*b["v_copied"].now())
                        V.tensor_tensor(by_head(vb[0:n, :], P), by_head(vtok[0:n, :], P),
                                        over(beta_tok[0:n, t, :].unsqueeze(2), [n, 4, P]), ALU.mult).then_inc(*step.one())
                        delta_rule(t, t0, n)
                    b["o_done"].skip()
                    if t == 2:
                        dve.wait_ge(*b["v_copied"].now())
                        dve.wait_ge(*b["dma_state"].now())
                    new_state(kind, g, t, n)
                    b["o_copied"].skip(2 if kind == "ret" else 1)
                if (kind, g) == ("mb", 0):
                    continue
                dve.wait_ge(*b["o_copied"].now())
                if kind == "mb":
                    for k in range(4):
                        V.scalar_tensor_tensor(out=f_ok[:, k], in0=xp[:, k, 0:T], scalar=vec[:, V_D + k:V_D + k + 1],
                                               in1=f_ok[:, k], op0=ALU.mult, op1=ALU.add).then_inc(*step.one())
                    dve.wait_ge(*step.now())
                    V.tensor_tensor(f_ok, f_ok, proj[:, Z:Z + 4, :], ALU.mult).then_inc(*b["f_pre"].one())
                    dve.wait_ge(*b["f_root"].next())

                    for k in range(4):
                        V.scalar_tensor_tensor(out=proj[:, Z + k, :], in0=f_ok[:, k], scalar=vec[:, V_MN + k:V_MN + k + 1],
                                               in1=f_rt[:, 0:T], op0=ALU.mult, op1=ALU.mult).then_inc(*step.one())
                    continue
                dve.wait_ge(*b["state_new"].now())
                V.sem_inc(sems["f_pre"], 1)
                b["f_pre"].skip()
                dve.wait_ge(*b["f_root"].next())

                out = ho[:, :, :] if kind == "hg" else xp[:, 0:4, 0:T]
                gate = {"hg": HG, "ret": RG, "gdn": GZ}[kind]
                root = f_rt.rearrange("p (k t) -> p k t", k=4)
                if kind == "ret":
                    V.tensor_tensor(root, out, root, ALU.mult).then_inc(*step.one())
                else:
                    V.scalar_tensor_tensor(out=root, in0=out, scalar=vec[:, V_HN:V_HN + 1] if kind == "hg" else
                                           vec[:, V_GN:V_GN + 1], in1=root, op0=ALU.mult,
                                           op1=ALU.mult).then_inc(*step.one())
                    if kind == "gdn":
                        b["dma_state_out"].skip(8)
                        dve.wait_ge(*b["dma_state_out"].now())
                    else:
                        b["silus"].skip(4)
                        dve.wait_ge(*b["silus"].now())
                dve.wait_ge(*step.now())
                V.tensor_tensor(proj[:, gate:gate + 4, :], proj[:, gate:gate + 4, :], root, ALU.mult).then_inc(
                    *(b["y_ready"] if kind == "gdn" else step).one())

        dve.wait_ge(b["dma_in"].sem, 32)
        with b.loop(DEPTH, "layer") as l:
            dve.wait_ge(*b["dma_vec"].next())
            norm_in(0)
            hidden(l, 0)
            norm_out(1)
            norm_in(2)
            for sec in ("proj0", "conv0", "tail0"):
                with b.passing(sections[sec]):
                    pass
            dve.wait_ge(*b["projected"].next())
            rows_and_tokens(l)
            convolutions(l)
            unit_norms(l)
            hgrn(l)
            scalar_decay(l)
            sec = sections["merge0"]
            with b.passing(sec), b.loop(KD, sec.tag) as i:
                for n in range(4):
                    t = gated(l, sec, i, 2 * n + 1)
                    if n == 1:
                        nc.vector.tensor_tensor(tmp[:, 0, :], hid_t[0][:, :], t, ALU.add).then_inc(*step.one())
                    elif n > 1:
                        nc.vector.tensor_tensor(tmp[:, 0, :], tmp[:, 0, :], t, ALU.add).then_inc(*step.one())
                    if n:
                        dve.wait_ge(*step.now())
                nc.vector.tensor_copy(m_hi[:, i, :], tmp[:, 0, :]).then_inc(*step.one())
                dve.wait_ge(*step.now())
                nc.vector.tensor_tensor(m_lo[:, i, :], tmp[:, 0, :], m_hi[:, i, :].bitcast(F32),
                                        ALU.subtract).then_inc(*b["merged"].one())
            with b.passing(sections["out0"]):
                pass
            norm_out(3)
            norm_in(4)
            hidden(l, 1)
            norm_out(5)
            nc.vector.sem_inc(sems["vec_free"], 1)

    @block.tensor
    def _(pe):
        b = book(pe, "pe")

        def split_product(j, sec, x_hi, x_lo, k0=0, first=True, last=True, ready=None):
            _, nk, _, r, s = sec.loads[j]
            nk = KD if (sec.name, j) == ("tail", 2) else nk
            bank = sec.banks[j if sec.name != "down" else j // 3]
            if first:
                pe.wait_ge(*b[f"bank_free{bank}"].now())
                b[f"bank_free{bank}"].skip()
            pe.wait_ge(*b[f"lo_ready{r}"].next())
            rows_out = ROWS if (sec.name, j) == ("tail", 2) else P
            out = psum[bank][0:rows_out, 0:T]
            for k in range(nk):
                if ready is not None:
                    pe.wait_ge(ready.sem, ready.at() - (KD - 1 - k))
                lhs_hi, lhs_lo = (w[s][:, k * rows_out:(k + 1) * rows_out] for w in (w_hi, w_lo))
                nc.tensor.matmul(out, lhs_hi, x_hi(k0 + k), start=(first and k == 0), stop=False)
                nc.tensor.matmul(out, lhs_hi, x_lo(k0 + k), start=False, stop=False)
                mm = nc.tensor.matmul(out, lhs_lo, x_hi(k0 + k), start=False, stop=(last and k == nk - 1))
            mm.then_inc(sems["tiles_done"], 1)

        u = (lambda k: u_hi[:, k, :]), (lambda k: u_lo[:, k, :])
        hid = (lambda k: hid_hi[:, k, :]), (lambda k: hid_lo[:, k, :])
        mrg = (lambda k: m_hi[:, k, :]), (lambda k: m_lo[:, k, :])

        def feature_sum(of_y=False):
            for k in range(KD):
                if not of_y:
                    pe.wait_ge(*b["squares"].next())
                elif k >= 4:
                    pe.wait_ge(*b[f"bank_free{k % 4}"].now())
                mm = nc.tensor.matmul(mix[:, 0, 0:T], ones, tmp[:, k, :], start=k == 0, stop=k == KD - 1)
            mm.then_inc(*b["norm_sum"].one())

        def products(tag, x, ready):
            sec = sections[tag]
            with b.passing(sec), b.loop(sec.trips, sec.tag):
                for j in range(sec.n):
                    split_product(j, sec, *x, ready=b[ready] if j == 0 else None)

        def wait_u():
            b["u_ready"].skip(KD)

        def mlp(l, f):
            feature_sum()
            wait_u()
            products(f"up{f}", u, "u_ready")
            b["hid_ready"].skip(KF)
            sec = sections[f"down{f}"]
            with b.passing(sec), b.loop(sec.trips, sec.tag):
                pe.wait_ge(*b["hid_ready"].now())
                for j in range(sec.n):
                    q = j % 3
                    split_product(j, sec, *hid, k0=sum(DOWN_K[:q]), first=q == 0, last=q == 2)
            feature_sum(of_y=True)


        def passed(narrow=True):
            if narrow:
                nc.tensor.sem_inc(sems["t_step"], 1)

        def row_transposes(l):
            pe.wait_ge(*b["rows_ready"].next())
            for t, (t0, n) in enumerate(TILES3):
                nc.tensor.transpose(psum[t][0:n, 0:ROWS], rb[:, t0:t0 + n], c_["ident"][0:ROWS, 0:ROWS])
                nc.tensor.transpose(psum[t][0:n, 128:136], rl[0:8, t0:t0 + n], c_["ident"][0:8, 0:8]).then_inc(
                    *b["tok_t"].one())
            for t, (t0, n) in enumerate(TILES3):
                pe.wait_ge(*b["tok_copied"].next())
                passed(t == 2)
                whole = ones[0:n, 0:n] if t < 2 else c_["same_s"][0:n, :]
                nc.tensor.matmul(psum[t][0:n, 0:16], tri_of(t), la_tok[0:n, t, :], start=True, stop=True)
                nc.tensor.matmul(psum[t][0:n, 16:32], whole, la_tok[0:n, t, :], start=True, stop=True).then_inc(
                    *b["tok_sums"].one())

        def unit_norms(l):
            for half in range(2):
                for e in range(4):
                    pe.wait_ge(*b["l2_sq"].next())
                    if half:
                        pe.wait_ge(*b["l2_root"].now())
                    nc.tensor.matmul(mix[:, e, 0:T], ones, lsq[e][:, :], start=True, stop=True).then_inc(*b["l2_sum"].one())
                b["l2_root"].skip()

        def head_sums(src):
            pe.wait_ge(*b["f_sq"].next())
            for k in range(4):
                mm = nc.tensor.matmul(mix[:, k, 0:T], ones, src[:, k * T:(k + 1) * T], start=True, stop=True)
            mm.then_inc(*b["f_sum"].one())

        def hgrn(l):
            for level, s in enumerate((0, 1, 2, 4, 8, 16, 32, 64)):
                pe.wait_ge(*b["hg_q"].next())
                for t, (t0, n) in enumerate(TILES3[:3 if s < 8 else 2]):
                    out = mix[:, 2 * (level % 2) + t, :] if t < 2 else psum[level % 2][0:64, 0:256]
                    for k in range(4):
                        mm = nc.tensor.matmul(out[:, k * n:(k + 1) * n], proj[:, HF + k, t0:t0 + n],
                                              proj[:, HQ + k, t0:t0 + n], start=True, stop=True)
                mm.then_inc(*b["hg_sc"].one())
            b["hg_q"].skip()
            pe.wait_ge(*b["hg_ready"].next())

        def delta_rule(t, n):
            m = 4 * n

            def heads(bank, lhs, rhs):
                passed(n == 64)
                for k in range(4):
                    mm = nc.tensor.matmul(psum[bank][0:n, k * n:(k + 1) * n], lhs[0:n, k * n:(k + 1) * n],
                                          rhs[0:n, k * n:(k + 1) * n], start=True, stop=True)
                mm.then_inc(*b["gdn_mm"].one())

            def transposes(bank, src):
                passed(n == 64)
                for k in range(4):
                    mm = nc.tensor.transpose(psum[bank][0:n, k * n:(k + 1) * n], src[0:n, k * n:(k + 1) * n],
                                             c_["ident"][0:n, 0:n])
                mm.then_inc(*b["gdn_mm"].one())

            def evacuated():
                pe.wait_ge(*b["gdn_ev"].next())

            def from_vector():
                pe.wait_ge(*b["gdn_v"].next())

            X = W[1] if t < 2 else W[0]
            from_vector()
            pe.wait_ge(*b["p_ready"].now())
            transposes(1, X)
            evacuated()
            heads(1, W[2], X)
            heads(2, X, W[2])
            from_vector()
            evacuated()
            heads(1, W[5], W[4])
            from_vector()
            heads(2, W[6], W[1])
            evacuated()
            heads(1, W[4], W[3])
            evacuated()
            if t < 2:
                transposes(2, W[2])
                for m2 in (16, 32, 64, 128):
                    from_vector()
                    evacuated()
                    heads(1, W[1], W[2])
                    evacuated()
                    heads(2, W[5], W[6])
                    from_vector()
                    if m2 < 128:
                        transposes(1, W[2])
            if t:
                for k in range(4):
                    mm = nc.tensor.matmul(psum[1][:, k * n:(k + 1) * n], kb[0:n, k * P:(k + 1) * P],
                                          W[2][0:n, k * n:(k + 1) * n], start=True, stop=True)
                mm.then_inc(*b["gdn_mm"].one())
                evacuated()
            if t < 2:
                for k in range(4):
                    out = psum[2][0:n, k * P:(k + 1) * P]
                    mm = nc.tensor.matmul(out, W[2][0:n, k * n:(k + 1) * n], vb[0:n, k * P:(k + 1) * P], start=True,
                                          stop=t == 0)
                    if t:
                        mm = nc.tensor.matmul(out, nsk[:, k * n:(k + 1) * n], state[GDN][:, k, :], start=False, stop=True)
                mm.then_inc(*b["gdn_mm"].one())
            else:
                for k in range(4):
                    nc.tensor.matmul(psum[2][:, k * n:(k + 1) * n], vb[0:n, k * P:(k + 1) * P],
                                     W[2][0:n, k * n:(k + 1) * n], start=True, stop=False)
                    for s in range(NS):
                        at = k * n + C * s
                        mm = nc.tensor.matmul(psum[2][:, at:at + C], st_s[:, s, k * P:(k + 1) * P], nsk[:, at:at + C],
                                              start=False, stop=s == NS - 1)
                mm.then_inc(*b["gdn_mm"].one())
                evacuated()
                passed()
                for k in range(4):
                    mm = nc.tensor.transpose(psum[1][0:n, k * P:(k + 1) * P], W[6][:, k * n:(k + 1) * n], c_["ident"])
                mm.then_inc(*b["gdn_mm"].one())
            evacuated()

        def outputs(kind, g, t, t0, n):
            vals = wn if kind == "gdn" else vtok
            width = 64 if kind == "mb" else P

            def place(k):
                if kind == "mb":
                    return mix[64 * (k % 2):64 * (k % 2) + 64, 0, (k // 2) * n:(k // 2 + 1) * n]
                if kind == "ret":
                    return mix[:, k % 2, (k // 2) * n:(k // 2 + 1) * n]
                return mix[:, 0, k * n:(k + 1) * n]

            def state_of(k, s):
                at = k // 2 if kind == "ret" else k
                pr = {"mb": slice(64 * g, 64 * g + 64), "ret": slice(64 * (k % 2), 64 * (k % 2) + 64)}.get(
                          kind, slice(0, P))
                if s is None:
                    own = {"hg": HGRN, "mb": MB, "ret": RET, "gdn": GDN}[kind]
                    return state[own][pr, at, :], pr
                c0 = 256 if kind == "ret" else 0
                return st_s[pr, s, c0 + at * width:c0 + (at + 1) * width], pr

            def query(k, at, count):
                if kind == "hg":
                    return proj[:, HQ + k, t0 + at:t0 + at + count]
                return qd[state_of(k, None)[1], k * n + at:k * n + at + count]

            def inside(k, start):
                weights = hp[0:n, 512 * t + k * n:512 * t + (k + 1) * n] if kind == "hg" else pm[0:n, k * n:(k + 1) * n]
                return nc.tensor.matmul(place(k), vals[0:n, k * width:(k + 1) * width], weights,
                                        start=start, stop=t == 0)

            def before(k):
                if t == 1:
                    st, pr = state_of(k, None)
                    return nc.tensor.matmul(place(k), st, query(k, 0, n), start=False, stop=True)
                for s in range(NS):
                    st, pr = state_of(k, s)
                    mm = nc.tensor.matmul(place(k)[:, C * s:C * s + C], st, query(k, C * s, C),
                                          start=False, stop=s == NS - 1)
                return mm

            if t == 2 and kind in ("mb", "ret"):
                for k in range(4):
                    inside(k, True).then_inc(*b["o_part"].one())
                    pe.wait_ge(*b["o_part"].now())
                    passed()
                    mm = before(k)
            else:
                for k in range(4):
                    mm = inside(k, True)
                    if t:
                        mm = before(k)
            mm.then_inc(*b["o_done"].one())

        def states(kind, g, t, n):
            vals = wn if kind == "gdn" else vtok
            width = 64 if kind == "mb" else P
            key = P if kind in ("hg", "gdn") else 64
            pe.wait_ge(*b["k_ready"].now())
            passed()
            for k in range(4):
                pr = {"mb": slice(64 * g, 64 * g + 64), "ret": slice(64 * (k % 2), 64 * (k % 2) + 64)}.get(
                          kind, slice(0, P))
                at = k // 2 if kind == "ret" else k
                keys = kend[0:n, k * key:(k + 1) * key]
                if t < 2:
                    mm = nc.tensor.matmul(mix[pr, 3, at * width:(at + 1) * width], keys, vals[0:n, k * width:(k + 1) * width],
                                          start=True, stop=True)
                    continue
                pe.wait_ge(*b["vm_ready"].next())
                if k == 1:
                    pe.wait_ge(*b["o_copied"].now())
                passed()
                bank = 2 if k % 2 == 0 else 0
                for half in range(NS * width // 512):
                    mm = nc.tensor.matmul(mix[pr, bank + half, :], keys, vm[k % 2][:, 512 * half:512 * half + 512],
                                          start=True, stop=True)
                mm.then_inc(*b["state_mm"].one())
            if t < 2:
                mm.then_inc(*b["state_mm"].one())

        def scalar_decay(l):
            for kind, g in GROUPS:
                col = {"hg": 0, "mb": 4 * g, "ret": RET, "gdn": GDN}[kind]
                b["dma_state"].skip({("mb", 0): 2, ("hg", 0): 1, ("gdn", 0): 1}.get((kind, g), 0))
                if (kind, g) == ("mb", 0):
                    for k in range(4):
                        mm = nc.tensor.matmul(mix[:, k, 0:T], c_["rot"], proj[:, RQ + k, :], start=True, stop=True)
                    mm.then_inc(*b["rot_ps"].one())
                    b["rotated"].skip()
                pr = slice(64 * g, 64 * g + 64)
                for t, (t0, n) in enumerate(TILES3):
                    pe.wait_ge(*b["state_new"].now())
                    pe.wait_ge(*b["o_copied"].now())
                    passed(t == 2)
                    if kind != "hg":
                        for k in range(4):
                            mm = nc.tensor.matmul(psum[0][:, k * n:(k + 1) * n],
                                                  la_tok[0:n, t, col + k:col + k + 1].to_broadcast([n, P]),
                                                  tri_of(t)[0:n, 0:n], start=True, stop=True)
                        mm.then_inc(*b["cum_bc"].one())
                        pe.wait_ge(*b["rotated"].now())
                        passed(t == 2)
                    if kind == "hg":
                        turns = [(bank, e, proj[:, at + e, t0:t0 + n]) for bank, at in ((psum[3], HI), (mix[:, 2], HF))
                                 for e in range(4)]
                    elif kind == "mb":
                        nc.tensor.matmul(psum[1][0:n, 0:n], xp[pr, 4, t0:t0 + n], xp[pr, 5, t0:t0 + n], start=True, stop=True)
                        turns = [(psum[3], e, xp[:, 2 * g + e, t0:t0 + n]) for e in range(2)]
                        turns.append((mix[:, 2], 0, xp[:, 4, t0:t0 + n]))
                    elif kind == "ret":
                        for k in range(4):
                            r = slice(64 * (k % 2), 64 * (k % 2) + 64)
                            nc.tensor.matmul(psum[1 + k % 2][0:n, (k // 2) * n:(k // 2 + 1) * n], proj[r, RK + k // 2, t0:t0 + n],
                                             proj[r, RQ + k // 2, t0:t0 + n], start=True, stop=True)
                        turns = [(psum[3], e, proj[:, RV + e, t0:t0 + n]) for e in range(4)]
                        turns += [(mix[:, 2], e, proj[:, RK + e, t0:t0 + n]) for e in range(2)]
                    else:
                        for k in range(4):
                            for bank, other in ((1, 6), (2, 10)):
                                nc.tensor.matmul(psum[bank][0:n, k * n:(k + 1) * n], xp[:, 10 + k, t0:t0 + n],
                                                 xp[:, other + k, t0:t0 + n], start=True, stop=True)
                        turns = [(psum[3], e, xp[:, 14 + e, t0:t0 + n]) for e in range(4)]
                        turns += [(mix[:, 2], e, xp[:, 10 + e, t0:t0 + n]) for e in range(4)]
                    for bank, e, src in turns:
                        mm = nc.tensor.transpose(bank[0:n, e * P:(e + 1) * P], src, c_["ident"])
                    mm.then_inc(*b["scores"].one())
                    if kind != "hg":
                        b["p_ready"].skip()
                    b["k_ready"].skip()
                    if t == 2:
                        pe.wait_ge(*b["dma_state"].now())
                    if kind == "gdn":
                        delta_rule(t, n)
                    pe.wait_ge(*b["v_copied"].next())
                    pe.wait_ge(*b["p_ready"].now())
                    if t and kind != "hg":
                        pe.wait_ge(*b["q_ready"].next())
                    passed(t == 2 or kind == "mb")
                    outputs(kind, g, t, t0, n)
                    b["o_copied"].skip(2 if kind == "ret" else 1)
                    states(kind, g, t, n)
                    b["state_new"].skip()
                if (kind, g) == ("mb", 0):
                    continue
                pe.wait_ge(*b["f_pre"].next())
                if kind == "mb":
                    pe.wait_ge(*b["f_sq"].next())
                    for k in range(4):
                        mm = nc.tensor.matmul(mix[:, 0, 0:T], ones, f_sq[:, k * T:(k + 1) * T], start=k == 0, stop=k == 3)
                    mm.then_inc(*b["f_sum"].one())
                else:
                    head_sums(f_sq)
                pe.wait_ge(*b["f_root"].next())
                passed()

        for name in START:
            nc.tensor.sem_inc(sems[name], unit_of(name))
        nc.tensor.sem_inc(sems["tiles_done"], AHEAD)
        pe.wait_ge(b["dma_in"].sem, 32)
        with b.loop(DEPTH, "layer") as l:
            mlp(l, 0)
            feature_sum()
            wait_u()
            for tag in ("proj0", "conv0", "tail0"):
                products(tag, u, "u_ready")
            row_transposes(l)
            unit_norms(l)
            hgrn(l)
            scalar_decay(l)
            b["y_ready"].skip()
            sec = sections["merge0"]
            with b.passing(sec), b.loop(KD, sec.tag):
                pe.wait_ge(*b["y_ready"].now())
                for n, base in enumerate((Z, HG, RG, GZ)):
                    split_product(2 * n, sec, *u)
                    b[f"dma_w{sec.loads[2 * n][3]}"].skip()
                    r, q = sec.loads[2 * n + 1][3], sec.banks[2 * n + 1]
                    pe.wait_ge(*b[f"bank_free{q}"].now())
                    b[f"bank_free{q}"].skip()
                    pe.wait_ge(*b[f"dma_w{r}"].next())
                    for k in range(KB):
                        mm = nc.tensor.matmul(psum[q][:, 0:T], raw[r][:, k * P:(k + 1) * P],
                                              proj[:, base + k, :], start=k == 0, stop=k == KB - 1)
                    mm.then_inc(sems["tiles_done"], 1)
            b["merged"].skip(KD)
            products("out0", mrg, "merged")
            feature_sum(of_y=True)
            mlp(l, 1)


def constants():
    c = {}
    i, j = np.arange(P)[:, None], np.arange(P)[None, :]
    BIG = 1e30
    c["ones"], c["ident"] = np.ones((P, P)), np.eye(P)
    c["tri"] = (i <= j)
    c["neg"] = np.where(i <= j, 0, -BIG)
    c["pos"] = np.where(i > j, 0, BIG)
    seq = i // C == j // C
    half = lambda m: m[:, :64] * np.where(np.arange(P)[:, None] < 64, 1, 0)
    c["tri_s"], c["same_s"] = half((i <= j) & seq), half(seq)
    c["neg_s"] = np.where((i <= j) & seq, 0, -BIG)[:, :64]
    c["pos_s"] = np.where((i > j) & seq, 0, BIG)[:, :64]
    rot = np.zeros((P, P))
    for p in range(P):
        rot[p + 32 if p % 64 < 32 else p - 32, p] = -1 if p % 64 < 32 else 1
    c["rot"] = rot
    steps = np.arange(32, dtype=np.float32) * np.float32(1 / 31)
    inv = (1.0 / np.power(10000.0, steps.astype(np.float64))).astype(np.float32)
    pos = np.concatenate([np.arange(SEQ), np.tile(PAST_LEN + np.arange(DEC_SEQ), DEC_BATCH)]).astype(np.float32)
    ang = (pos[None, :] * np.tile(inv, 4)[:, None]).astype(np.float32).astype(np.float64)
    c["cos"], c["sin"] = np.cos(ang), np.sin(ang)
    c["b8"] = (i > j) & (i // 8 == j // 8)
    for m in (16, 32, 64, 128):
        c[f"b{m}"] = (i // m == j // m) & (i % m >= m // 2) & (j % m < m // 2)
    for m in (2, 4, 8, 16, 32, 64, 128):
        c[f"next{m}"] = (i // m == j // m) & (i % m < m // 2) & (j % m >= m // 2)
    c["lgam"] = np.broadcast_to(np.log((1.0 - np.exp2(-5.0 - np.arange(4))).astype(np.float32)), (P, 4))
    c["pick"] = (i // C == np.arange(8)[None, :])
    c["eps"], c["eps4"] = np.full((P, 1), EPS), np.full((P, 1), 4 * EPS)
    return np.concatenate([np.asarray(c[k], np.float32) for k in CONST], axis=1)


OUTS = {"x": (P, KD, T), "st_conv": (DEPTH, P, NCONV, NS + 1, 3), "mb_p": (DEPTH, P, 256), "ret_p": (DEPTH, P, 256),
        "gdn_p": (DEPTH, P, 512), "hg_p": (DEPTH, P, 512), "mb_s": (DEPTH, P, NS * 256), "ret_s": (DEPTH, P, NS * 256),
        "gdn_s": (DEPTH, P, NS * 512), "hg_s": (DEPTH, P, NS * 512)}


def results(r):
    tok = r["x"].transpose(1, 0, 2).reshape(D_MODEL, T).T
    cv = r["st_conv"].transpose(0, 3, 4, 2, 1).reshape(DEPTH, NS + 1, 3, NCONV * P)
    mb = lambda x, n: x.reshape(DEPTH, 2, 64, n, 4, 64).transpose(0, 3, 1, 4, 2, 5).reshape(DEPTH, n, 8, 64, 64)
    ret = lambda x, n: x.reshape(DEPTH, 2, 64, n, 2, P).transpose(0, 3, 4, 1, 2, 5).reshape(DEPTH, n, 4, 64, P)
    gd = lambda x, n: x.reshape(DEPTH, P, n, 4, P).transpose(0, 2, 3, 1, 4)
    got = (tok[:SEQ].reshape(1, SEQ, D_MODEL), tok[SEQ:].reshape(DEC_BATCH, DEC_SEQ, D_MODEL),
           mb(r["mb_p"], 1), cv[:, :1, :, :768], gd(r["hg_p"], 1), ret(r["ret_p"], 1), gd(r["gdn_p"], 1), cv[:, :1, :, 768:],
           mb(r["mb_s"], NS), cv[:, 1:, :, :768], gd(r["hg_s"], NS), ret(r["ret_s"], NS), gd(r["gdn_s"], NS), cv[:, 1:, :, 768:])
    return tuple(np.ascontiguousarray(x) for x in got)


def layouts(x):
    A = {k: np.asarray(v) for k, v in x.items()}
    out = {}
    tok = np.concatenate([A["x_prompt"].reshape(SEQ, D_MODEL), A["x_sample"].reshape(-1, D_MODEL)])
    out["x"] = tok.T.reshape(KD, P, T).transpose(1, 0, 2)
    out["w_up"] = A["ffn_w_in"].reshape(DEPTH, 2, KD, P, 2, KF, P).transpose(0, 1, 5, 4, 3, 2, 6).reshape(DEPTH, 2, KF, 2, P, KD * P)
    out["w_down"] = A["ffn_w_out"].reshape(DEPTH, 2, KF, P, KD, P).transpose(0, 1, 4, 3, 2, 5).reshape(DEPTH, 2, KD, P, KF * P)
    w = A["w_in"]
    s = np.cumsum([0, 512, 768, 8, 512, 512, 512, 512, 256, 256, 512, 512, 1536, 512, 4, 4, 4096])
    seg = [w[:, :, s[i]:s[i + 1]] for i in range(16)]
    z, xbc, dt, hq, hf, hi, hg, rq, rk, rv, rg, qkv, gz, ga, gb, gates = seg
    cols = np.concatenate([z, hq, hf, hi, hg, rq, rk, rv, rg, gz, xbc, qkv], axis=2)
    out["w_proj"] = cols.reshape(DEPTH, KD, P, NPLAIN + NCONV, P).transpose(0, 3, 2, 1, 4).reshape(DEPTH, NPLAIN + NCONV, P, KD * P)
    small = np.zeros((DEPTH, D_MODEL, ROWS), np.float32)
    small[:, :, 0:8], small[:, :, 32:36], small[:, :, 64:68] = dt, ga, gb
    out["w_rows"] = small.reshape(DEPTH, KD, P, ROWS).transpose(0, 2, 1, 3).reshape(DEPTH, P, KD * ROWS)
    out["w_gate"] = gates.reshape(DEPTH, KD, P, 4, KD, P).transpose(0, 4, 3, 2, 1, 5).reshape(DEPTH, KD, 4, P, KD * P)
    out["w_branch"] = A["w_branch"].reshape(DEPTH, 4, KB, P, KD, P).transpose(0, 4, 1, 3, 2, 5).reshape(DEPTH, KD, 4, P, KB * P)
    out["w_out"] = A["w_out"].reshape(DEPTH, KD, P, KD, P).transpose(0, 3, 2, 1, 4).reshape(DEPTH, KD, P, KD * P)
    v = np.zeros((DEPTH, P, NV), np.float32)

    def put(at, rows):
        v[:, :, at:at + rows.shape[1]] = rows.transpose(0, 2, 1)

    put(V_G, A["norm_g"].reshape(DEPTH, 48, P))
    cw = np.concatenate([A["mb_conv_w"], A["gdn_conv_w"]], axis=2).reshape(DEPTH, 4, NCONV, P)
    put(V_CW, cw.transpose(0, 2, 1, 3).reshape(DEPTH, 72, P))
    put(V_CB, A["mb_conv_b"].reshape(DEPTH, 6, P))
    put(V_D, np.repeat(A["mb_d"], 64, axis=1).reshape(DEPTH, 4, P))
    put(V_MN, A["mb_norm"].reshape(DEPTH, 4, P))
    put(V_LB, np.broadcast_to(A["hg_lb_logits"].reshape(1, 8, P), (DEPTH, 8, P)))
    put(V_HN, A["hg_norm"].reshape(DEPTH, 1, P))
    put(V_GN, A["gdn_norm"].reshape(DEPTH, 1, P))
    v[:, 0:8, V_RB], v[:, 32:36, V_RB] = A["mb_dt_bias"], A["gdn_dt_bias"]
    v[:, 0:8, V_RA], v[:, 32:36, V_RA] = A["mb_a_log"], A["gdn_a_log"]
    v[1:, :, V_ON] = 1.0
    out["vec"] = v
    out["const"] = constants()
    cv = np.concatenate([A["state_ssm_conv"], A["state_gdn_conv"]], axis=3)
    out["st_conv"] = cv.reshape(DEPTH, NS, 3, NCONV, P).transpose(0, 4, 3, 1, 2).reshape(DEPTH, P, NCONV * NS * 3)
    out["st_mb"] = A["state_ssm"].reshape(DEPTH, NS, 2, 4, 64, 64).transpose(0, 2, 4, 1, 3, 5).reshape(DEPTH, P, NS * 256)
    out["st_ret"] = A["state_ret"].reshape(DEPTH, NS, 2, 2, 64, P).transpose(0, 3, 4, 1, 2, 5).reshape(DEPTH, P, NS * 256)
    out["st_gdn"] = A["state_gdn"].transpose(0, 3, 1, 2, 4).reshape(DEPTH, P, NS * 512)
    out["st_hg"] = A["state_hgrn"].transpose(0, 3, 1, 2, 4).reshape(DEPTH, P, NS * 512)
    return {k: np.ascontiguousarray(v) for k, v in out.items()}


def kernel(**inputs):
    import concourse.bacc as _bacc
    from concourse import mybir as _mybir
    from concourse.bass_utils import run_bass_kernel_spmd as _run

    arrays = {f"in_{k}": v for k, v in layouts(inputs).items()}

    def program(per_body):
        nc = _bacc.Bacc("TRN2", target_bir_lowering=False, num_devices=1)
        a = {k[3:]: nc.dram_tensor(k, v.shape, _mybir.dt.from_np(v.dtype), kind="ExternalInput").ap()
             for k, v in arrays.items()}
        o = {k: nc.dram_tensor(f"out_{k}", shape, F32, kind="ExternalOutput").ap() for k, shape in OUTS.items()}
        found = {}
        build(nc, a, o, per_body, found)
        return nc, found

    nc, _ = program(program({})[1])
    r = _run(nc, [arrays], core_ids=[0])
    return results({k: r.results[0][f"out_{k}"] for k in OUTS})
```

```python
from contextlib import ExitStack, contextmanager

import numpy as np

import concourse.bass as bass
from concourse import mybir

ALU = mybir.AluOpType
ACT = mybir.ActivationFunctionType
F32 = mybir.dt.float32
F32R = mybir.dt.float32r


P = 128
D_MODEL, DEPTH = 1024, 2
SEQ, DEC_BATCH, DEC_SEQ, PAST_LEN = 256, 8, 8, 2048
T = SEQ + DEC_BATCH * DEC_SEQ
D_FF = 2816
KD = D_MODEL // P
KF = D_FF // P
KB = 4
C = DEC_SEQ

EPS = 1e-6
XW = SEQ + 3 + DEC_BATCH * (DEC_SEQ + 3)

Z, HQ, HF, HI, HG, RQ, RK, RV, RG, GZ = 0, 4, 8, 12, 16, 20, 22, 24, 28, 32
NPLAIN, NCONV = 36, 18
NSLOT = 4
SLOT = KD * P
DOWN_K = (8, 8, 6)
ROWS = 96

V_G, V_CW, V_CB, V_D, V_MN, V_LB, V_HN, V_GN, V_RB, V_RA, V_ON = 0, 48, 120, 126, 130, 134, 142, 143, 144, 145, 146
NV = 147

CONST, _at = {}, 0
for _name, _cols in (("ones", P), ("ident", P), ("tri", P), ("neg", P), ("pos", P), ("tri_s", 64), ("neg_s", 64),
                     ("pos_s", 64), ("same_s", 64), ("rot", P), ("cos", T), ("sin", T), ("b8", P), ("b16", P),
                     ("b32", P), ("b64", P), ("b128", P),
                     *((f"next{m}", P) for m in (2, 4, 8, 16, 32, 64, 128)), ("lgam", 4), ("pick", 8), ("eps", 1), ("eps4", 1)):
    CONST[_name] = (_at, _cols)
    _at += _cols
NCONST = _at
MB, RET, GDN, HGRN = 0, 8, 12, 16
TILES3 = ((0, 128), (128, 128), (256, 64))
NS = DEC_BATCH


START = ("dma_conv_out", "h_ready", "o_copied", "state_new", "p_ready", "k_ready", "v_copied", *(f"{n}{i}" for n in ("bank_free", "lo_ready") for i in range(NSLOT)))


def unit_of(name):
    return 16 if name.startswith("dma_") else 1


class Count:

    def __init__(self, sem, unit, name):
        self.sem, self.unit, self.name, self.terms = sem, unit, name, []
        self.n = unit if name in START else 0

    def at(self):
        e = self.n
        for reg, per in self.terms:
            if per:
                e = reg * per + e
        return e

    def one(self):
        self.n += self.unit
        return self.sem, self.unit

    def now(self):
        return self.sem, self.at()

    def next(self):
        self.n += self.unit
        return self.sem, self.at()

    def skip(self, k=1):
        self.n += k * self.unit


class Book:

    def __init__(self, eng, name, sems, per_body, seen):
        self.eng, self.name, self.sems, self.per_body, self.seen = eng, name, sems, per_body, seen
        self.counts = {}

    def __getitem__(self, name):
        if name not in self.counts:
            self.counts[name] = Count(self.sems[name], unit_of(name), name)
            self.counts[name].terms = [(r, self.per_body.get((self.name, tag, name), 0)) for r, tag in self.around]
        return self.counts[name]

    around = ()

    @contextmanager
    def passing(self, section):
        uses = {k: n for k, n in section.uses.items() if self.name == "pe" or not k.startswith("dma_")}
        start = {k: self[k].n for k in uses}
        yield
        for k, n in uses.items():
            self.counts[k].n = start[k] + n * self.counts[k].unit

    @contextmanager
    def loop(self, trips, tag):
        first = {k: unit_of(k) if k in START else 0 for k in self.sems}
        start = {**first, **{k: c.n for k, c in self.counts.items()}}
        outer = self.around
        with self.eng.Fori(0, trips) as i:
            self.around = (*outer, (i, tag))
            for k, c in self.counts.items():
                c.terms.append((i, self.per_body.get((self.name, tag, k), 0)))
            yield i
            for k, c in self.counts.items():
                per = c.n - start[k]
                self.seen[(self.name, tag, k)] = per
                c.terms.pop()
                c.n = start[k] + per * trips
        self.around = outer


def build(nc, a, o, per_body, seen):
    with ExitStack() as ctx:
        _build(nc, a, o, per_body, seen, ctx)


def _build(nc, a, o, per_body, seen, ctx):
    sems = {}

    def sem(*names):
        for n in names:
            sems[n] = ctx.enter_context(nc.semaphore(n))

    def sb(name, shape, dt=F32, stack=ctx):
        return stack.enter_context(nc.sbuf_tensor(name, shape, dt))

    h = sb("h", [P, KD, T])
    u_hi, u_lo = sb("u_hi", [P, KD, T], F32R), sb("u_lo", [P, KD, T], F32R)
    with ExitStack() as part:
        second = [sb(f"inv{i}", [P, 512], F32, part)[:, :] for i in range(7)]
    raw = [sb(f"w_raw{i}", [P, SLOT]) for i in range(NSLOT)]
    with ExitStack() as part:
        st_s = sb("st_s", [P, NS, 512], F32, part)
        hp = sb("hg_p", [P, 1280], F32, part)
        ho = sb("hg_o", [P, 4, T], F32, part)
        hf8, hf128 = sb("hg_fade8", [P, 4, T // 8], F32, part), sb("hg_fade128", [P, 4, 2], F32, part)
    with ExitStack() as part:
        sb("_st_s", [P, NS * 512], F32, part)
        set2 = [sb(f"sc2_{n}", [P, 512], F32, part) for n in ("p", "qd", "kend", "kb", "vb", "wn", "nsk")]
    w_hi = [sb(f"w_hi{i}", [P, SLOT], F32R) for i in range(NSLOT)]
    w_lo = [sb(f"w_lo{i}", [P, SLOT], F32R) for i in range(NSLOT)]
    vec = sb("vec", [P, NV])
    const = sb("const", [P, NCONST])
    c_ = {k: const[:, at:at + n] for k, (at, n) in CONST.items()}
    ones, eps_c = c_["ones"], c_["eps"]
    lb = sb("lb", [P, 32])
    la_tok, beta_tok, dt_tok = sb("la_tok", [P, 3, 16]), sb("beta_tok", [P, 3, 4]), sb("dt_tok", [P, 3, 8])
    cum_tok, ecum_tok = sb("cum_tok", [P, 3, 16]), sb("ecum_tok", [P, 3, 16])
    to_end, to_end_dt, beta_cum = sb("to_end", [P, 3, 16]), sb("to_end_dt", [P, 3, 8]), sb("beta_cum", [P, 3, 4])
    rows = sb("rows", [ROWS, T])
    with ExitStack() as part:
        hid_hi = sb("hid_hi", [P, KF, T], F32R, part)
        hid_lo = sb("hid_lo", [P, KF, T], F32R, part)
    proj = sb("proj", [P, NPLAIN, T], F32, ctx)
    with ExitStack() as part:
        m_hi = sb("m_hi", [P, KD, T], F32R, part)
        m_lo = sb("m_lo", [P, KD, T], F32R, part)
    xp = sb("xp", [P, NCONV, XW], F32, ctx)
    with ExitStack() as part:
        y = sb("y", [P, KD, T], F32, part)
        tmp = sb("tmp", [P, KD, T], F32, part)
        gate_s = [sb(f"gate_s{i}", [P, T], F32, part) for i in range(2)]
        hid_t = [sb(f"hid_t{i}", [P, T], F32, part) for i in range(2)]

        rms = sb("rms", [P, T], F32, part)



    with ExitStack() as part:
        hf1, hf2 = sb("hg_fade1", [P, 4 * T], F32, part), sb("hg_fade2", [P, 2 * T], F32, part)
        ht = sb("hg_masked", [P, 1280], F32, part)
    with ExitStack() as part:
        rx, re, ru, rt, rl, rb = (sb(f"row_{n}", [ROWS, T], F32, part) for n in "xeutlb")

        cin = sb("conv_in", [P, NCONV, NS, 3], F32, part)
        cout = sb("conv_out", [P, NCONV, NS + 1, 3], F32, part)

    with ExitStack() as part:
        dm, em, dm2, ecb, pm, qd, kend, vtok, kb, vb, wn, nsk = (
            sb(f"sc_{n}", [P, 512], F32, part) for n in ("d", "e", "d2", "ecb", "p", "qd", "kend", "v", "kb", "vb", "wn", "nsk"))
        state = {MB: sb("st_mb", [P, 4, 64], F32, part), RET: sb("st_ret", [P, 2, 128], F32, part),
                 GDN: sb("st_gdn", [P, 4, 128], F32, part), HGRN: sb("st_hg", [P, 4, 128], F32, part)}
        cacc = [sb(f"conv_acc{i}", [P, XW], F32, part) for i in range(2)]
    work = proj[:, HQ:HQ + 12, :].rearrange("p k t -> p (k t)")
    W = [work[:, 512 * i:512 * i + 512] for i in range(7)]
    psum = [ctx.enter_context(nc.psum_tensor(f"bank{i}", [P, 512], F32)) for i in range(4)]
    mix = ctx.enter_context(nc.psum_tensor("mix", [P, 4, 512], F32))
    SETS = (dict(W=W, bufs=(pm, qd, kend, kb, vb, wn, nsk), x=0, banks=(psum[1], psum[2])),
            dict(W=second, bufs=tuple(set2), x=1, banks=(psum[3], psum[0])))
    PLAIN = (dict(ecb=ecb, v=vtok, p=pm, q=qd, k=kend), dict(ecb=dm2, v=wn, p=kb, q=vb, k=nsk))

    def buffers(kind, x):
        if kind == "gdn":
            p, q, k, _, _, v, _ = SETS[x]["bufs"]
            return ecb, v, p, q, k
        return tuple(PLAIN[x][n] for n in ("ecb", "v", "p", "q", "k"))

    ORDERS = {"mb": [("prepare", 0), ("prepare", 1), ("finish", 0), ("prepare", 2), ("finish", 1), ("finish", 2)],
              "gdn": [("prepare", 0), ("prepare", 1), ("invert", 0), ("finish", 0), ("finish", 1), ("prepare", 2),
                      ("invert", 1), ("finish", 2)]}
    ORDERS["hg"] = ORDERS["ret"] = ORDERS["mb"]
    PAIRS = (((0, *TILES3[0]), (1, *TILES3[1])), ((2, *TILES3[2]),))
    f_sq, f_rt, f_o = (work[:, 4 * T * i:4 * T * (i + 1)] for i in range(3))
    f_ok = f_o.rearrange("p (k t) -> p k t", k=4)
    lsq = [x.rearrange("p (k t) -> p k t", k=4) for x in (f_sq, f_o)]
    lrt = [x.rearrange("p (k t) -> p k t", k=4) for x in (f_rt, f_sq)]
    vm = [work[0:64, 1024 * i:1024 * i + 1024] for i in range(2)]

    CONV_AT = [range(*x) for x in ((0, 2), (2, 12), (12, NCONV))]
    GROUPS = (("hg", 0), ("mb", 0), ("mb", 1), ("ret", 0), ("gdn", 0))

    def acc_sample(acc):
        return acc[:, SEQ + 3:XW].rearrange("p (s t) -> p s t", s=NS)[:, :, 0:C]

    def over(x, shape):
        return x.to_broadcast(shape)

    def tri_of(t):
        return c_["tri"] if t < 2 else c_["tri_s"][0:64, :]


    sem("dma_in", "dma_vec", "dma_out", "v_step", "a_step", "p_step", "t_step", "s_step")
    sem(*[f"{n}{i}" for n in ("dma_w", "hi_ready", "lo_ready", "bank_free") for i in range(NSLOT)])
    sem("tiles_done")
    sem("hid_ready", "squares", "norm_sum", "root", "u_ready", "y_ready", "h_ready", "merged", "projected")
    sem("row_x", "row_e", "row_u", "row_ln", "rows_ready", "tok_t", "tok_copied", "tok_sums", "tok_exp", "tok_ready")
    sem("dma_conv", "dma_conv_out", "conv_filled", "conv_saved", "conv_sum", "conv_done")
    sem("l2_sq", "l2_sum", "l2_root", "l2_done", "bound_d", "bound_e", "hg_sig", "silus")
    sem("hg_q", "hg_sc", "hg_ready", "hg_out")
    sem("f_pre", "f_sq", "f_sum", "f_root", "rot_ps", "rotated")
    sem("cum_bc", "ecb_ready", "dec_d", "dec_e", "scores", "v_copied", "p_ready", "q_ready", "k_ready", "o_part",
        "o_done", "o_copied", "vm_ready", "state_mm", "state_new", "dma_state", "dma_state_out")
    sem(*[f"gdn_{n}{x}" for n in ("mm", "ev", "v") for x in range(2)])

    block = ctx.enter_context(nc.Block())

    def book(eng, name):
        return Book(eng, name, sems, per_body, seen)

    sections = {}

    class Section:
        def __init__(self, name, f, trips, sources, banks):
            self.name, self.f, self.trips, self.sources, self.banks = name, f, trips, sources, banks
            self.n, self.base, self.lead = len(sources), sum(x.trips * x.n for x in sections.values()), 2
            self.tag = f"{name}{f}"
            sections[self.tag] = self
            self.loads, s = [], 0
            for j, (src, nk, split) in enumerate(sources):
                self.loads.append((src, nk, split, j % NSLOT, s % NSLOT if split else None))
                s += split
            self.uses = {f"bank_free{q}": trips * sum(x == q for x in banks) for q in range(4)}
            self.uses |= {f"dma_w{r}": trips * sum(x[3] == r for x in self.loads) for r in range(NSLOT)}



    for f in range(2):
        Section("up", f, KF // 2, [(lambda l, i, m=m, g=g, f=f: a["w_up"][l, f, 2 * i + m, g], KD, True)
                                   for m in range(2) for g in range(2)], (0, 1, 2, 3))
        Section("down", f, 2, [(lambda l, i, m=m, q=q, f=f: a["w_down"][l, f, 4 * i + m][:, sum(DOWN_K[:q]) * P:sum(DOWN_K[:q + 1]) * P],
                                DOWN_K[q], True) for m in range(4) for q in range(3)], (0, 1, 2, 3))
        if f:
            break
        Section("proj", 0, NPLAIN // 4, [(lambda l, i, m=m: a["w_proj"][l, 4 * i + m], KD, True) for m in range(4)],
                (0, 1, 2, 3))
        Section("conv", 0, 4, [(lambda l, i, m=m: a["w_proj"][l, 4 * i + (NPLAIN + m)], KD, True) for m in range(4)],
                (0, 1, 2, 3))
        Section("tail", 0, 1, [(lambda l, i, m=m: a["w_proj"][l, NPLAIN + 16 + m], KD, True) for m in range(2)]
                + [(lambda l, i: a["w_rows"][l], KD * ROWS // P, True)], (0, 1, 2))
        Section("merge", 0, KD, [t for n in range(4) for t in (
            (lambda l, i, n=n: a["w_gate"][l, i, n], KD, True),
            (lambda l, i, n=n: a["w_branch"][l, i, n], KB, False))], (0, 1, 2, 3) * 2)
        sections["merge0"].lead = 4
        Section("out", 0, KD // 4, [(lambda l, i, m=m: a["w_out"][l, 4 * i + m], KD, True) for m in range(4)],
                (0, 1, 2, 3))
    ORDER = list(sections.values())
    TILES = sum(x.trips * x.n for x in ORDER)
    AHEAD = NSLOT

    def done(l, sec, i, j):
        return l * TILES + (i * sec.n + (AHEAD + sec.base + j + 1))

    def slot_empty(l, sec, i, j):
        return done(l, sec, i, j - (3 if sec.name == "merge" else NSLOT))

    @block.sync
    def _(sp):
        b = book(sp, "sp")

        def mixer_dmas(l):
            sp.wait_ge(*b["projected"].next())
            sp.dma_start(cin[:, :, :, :], a["st_conv"][l]).then_inc(*b["dma_conv"].one())
            sp.wait_ge(*b["conv_saved"].next())
            sp.dma_start(o["st_conv"][l], cout[:, :, :, :]).then_inc(*b["dma_conv_out"].one())
            sp.dma_start(st_s[:, :, :], a["st_hg"][l].rearrange("p (s n) -> p s n", s=NS)).then_inc(*b["dma_state"].one())
            b["state_new"].skip(3)
            sp.wait_ge(*b["state_new"].now())
            sp.dma_start(o["hg_p"][l], state[HGRN][:, :, :].rearrange("p h n -> p (h n)")).then_inc(*b["dma_state_out"].one())
            sp.dma_start(o["hg_s"][l].rearrange("p (s n) -> p s n", s=NS), st_s[:, :, :]).then_inc(*b["dma_state_out"].one())
            sp.wait_ge(*b["dma_state_out"].now())
            sp.dma_start(st_s[:, :, 0:256], a["st_mb"][l].rearrange("p (s n) -> p s n", s=NS)).then_inc(*b["dma_state"].one())
            sp.dma_start(st_s[:, :, 256:512], a["st_ret"][l].rearrange("p (s n) -> p s n", s=NS)).then_inc(*b["dma_state"].one())
            b["state_new"].skip(6)
            sp.wait_ge(*b["state_new"].now())
            sp.dma_start(o["mb_p"][l], state[MB][:, :, :].rearrange("p h n -> p (h n)")).then_inc(*b["dma_state_out"].one())
            sp.dma_start(o["mb_s"][l].rearrange("p (s n) -> p s n", s=NS), st_s[:, :, 0:256]).then_inc(*b["dma_state_out"].one())
            b["state_new"].skip(3)
            sp.wait_ge(*b["state_new"].now())
            sp.dma_start(o["ret_p"][l], state[RET][:, :, :].rearrange("p h n -> p (h n)")).then_inc(*b["dma_state_out"].one())
            sp.dma_start(o["ret_s"][l].rearrange("p (s n) -> p s n", s=NS), st_s[:, :, 256:512]).then_inc(*b["dma_state_out"].one())
            sp.wait_ge(*b["dma_state_out"].now())
            sp.dma_start(st_s[:, :, :], a["st_gdn"][l].rearrange("p (s n) -> p s n", s=NS)).then_inc(*b["dma_state"].one())
            b["dma_state_out"].skip(2)
            b["state_new"].skip(2)
            sp.wait_ge(*b["state_new"].now())
            nc.sync.sem_inc(sems["s_step"], 1)
            b["state_new"].skip()

        sp.dma_start(h[:, :, :], a["x"]).then_inc(*b["dma_in"].one())
        sp.dma_start(const[:, :], a["const"]).then_inc(*b["dma_in"].one())
        with b.loop(DEPTH, "layer") as l:

            for sec in ORDER:
                if sec.name == "merge":
                    mixer_dmas(l)
                with b.loop(sec.trips, sec.tag) as i:
                    for j, (src, nk, split, r, _) in enumerate(sec.loads):
                        sp.wait_ge(*b[f"lo_ready{r}"].now())
                        if split:
                            b[f"lo_ready{r}"].skip()
                        if sec.name in ("merge", "out"):
                            sp.wait_ge(sems["tiles_done"], done(l, sec, i, j - NSLOT))
                        sp.dma_start(raw[r][:, 0:nk * P], src(l, i)).then_inc(*b[f"dma_w{r}"].one())
        sp.wait_ge(sems["h_ready"], 1 + KD + 3 * KD * DEPTH)
        sp.dma_start(o["x"], h[:, :, :]).then_inc(*b["dma_out"].one())
        for name in ("dma_out", "dma_conv_out", "dma_state_out"):
            sp.wait_ge(*b[name].now())

    @block.gpsimd
    def _(pool):
        b = book(pool, "pool")
        def padded(x):
            return xp[:, :, 3 + SEQ:XW].rearrange("p m (s t) -> p m s t", s=NS)

        def passed():
            nc.gpsimd.sem_inc(sems["p_step"], 1)

        def conv_ends(l):
            pool.wait_ge(*b["projected"].next())
            passed()
            nc.gpsimd.memset(xp[:, :, 0:3], 0.0)
            pool.wait_ge(*b["dma_conv"].next())
            passed()
            nc.gpsimd.tensor_copy(padded(xp)[:, :, :, 0:3], cin[:, :, :, :]).then_inc(*b["conv_filled"].one())
            pool.wait_ge(*b["dma_conv_out"].now())
            b["dma_conv_out"].skip()
            passed()
            nc.gpsimd.tensor_copy(cout[:, :, 0, :], xp[:, :, SEQ:SEQ + 3])
            nc.gpsimd.tensor_copy(cout[:, :, 1:, :], padded(xp)[:, :, :, C:C + 3]).then_inc(*b["conv_saved"].one())



        with b.loop(DEPTH, "layer") as l:
            for sec in ORDER:
                if sec.name == "merge":
                    conv_ends(l)

                with b.loop(sec.trips, sec.tag) as i:
                    for j, (_, nk, split, r, s) in enumerate(sec.loads):
                        if not split:
                            continue
                        n = nk * P
                        pool.wait_ge(*b[f"hi_ready{s}"].next())
                        pool.wait_ge(sems["tiles_done"], slot_empty(l, sec, i, j))
                        nc.gpsimd.tensor_tensor(w_lo[s][:, 0:n], raw[r][:, 0:n], w_hi[s][:, 0:n].bitcast(F32),
                                                ALU.subtract).then_inc(*b[f"lo_ready{r}"].one())



    @block.scalar
    def _(act):
        b = book(act, "act")
        step = b["a_step"]

        def hi(l, sec, i, j):
            _, nk, split, r, s = sec.loads[j]
            if not split:
                b[f"dma_w{r}"].skip()
                return
            act.wait_ge(*b[f"dma_w{r}"].next())
            act.wait_ge(sems["tiles_done"], slot_empty(l, sec, i, j))
            nc.scalar.activation(w_hi[s][:, 0:nk * P], raw[r][:, 0:nk * P], ACT.Copy).then_inc(
                *b[f"hi_ready{s}"].one())

        def first(l, sec):
            for j in range(sec.lead):
                hi(l, sec, 0, j)

        def dense(l, sec, evacuate, then=None):
            with b.passing(sec):
                if sec.trips > 1:
                    with b.loop(sec.trips - 1, sec.tag) as i:
                        for j in range(sec.n):
                            a = j + sec.lead
                            hi(l, sec, i + a // sec.n if a >= sec.n else i, a % sec.n)
                            evacuate(i, j)
                for j in range(sec.n):
                    a = j + sec.lead - sec.n
                    if a < 0:
                        hi(l, sec, sec.trips - 1, j + sec.lead)
                    elif then and a < then.lead:
                        hi(l, then, 0, a)
                    evacuate(sec.trips - 1, j)

        def tile_done(l, sec, i, j):
            act.wait_ge(sems["tiles_done"], done(l, sec, i, j))

        def squares():
            for k in range(KD):
                act.wait_ge(*b["h_ready"].next())
                nc.scalar.activation(tmp[:, k, :], h[:, k, :], ACT.Square).then_inc(*b["squares"].one())

        def inverse_root(dst, src, scale, count):
            nc.scalar.activation(dst, src, ACT.Ln, scale=scale, bias=eps_c).then_inc(*step.one())
            act.wait_ge(*step.now())
            nc.scalar.activation(dst, dst, ACT.Exp, scale=-0.5).then_inc(*count.one())

        def root(half=False):
            act.wait_ge(*b["norm_sum"].next())
            nc.scalar.activation(rms[:, :], mix[:, 0, 0:T], ACT.Sqrt, scale=(4.0 if half else 1.0) / D_MODEL,
                                 bias=c_["eps4"] if half else eps_c).then_inc(*b["root"].one())

        def gating(l, sec, func):
            def evacuate(i, j):
                q = sec.banks[j]
                if q % 2 == 0:
                    tile_done(l, sec, i, j)
                    act.wait_ge(*b[f"bank_free{q + 1}"].now())
                    b[f"bank_free{q + 1}"].skip()
                    nc.scalar.activation(gate_s[q // 2][:, :], psum[q][:, 0:T], func).then_inc(
                        *b[f"bank_free{q}"].one())
            return evacuate

        def with_squares(l, sec, to):
            def evacuate(i, j):
                out = to(i, j)
                if out is None:
                    return
                q, k = out
                tile_done(l, sec, i, j)
                nc.scalar.activation(y[:, k, :], psum[q][:, 0:T], ACT.Copy)
                nc.scalar.activation(tmp[:, k, :], psum[q][:, 0:T], ACT.Square).then_inc(*b[f"bank_free{q}"].one())
            return evacuate

        def copying(l, sec, to):
            def evacuate(i, j):
                q, dst = to(i, j)
                tile_done(l, sec, i, j)
                nc.scalar.activation(dst, psum[q][:, 0:T], ACT.Copy).then_inc(*b[f"bank_free{q}"].one())
            return evacuate

        def padded(l, sec, first_tile):
            def evacuate(i, j):
                if sec.name == "tail" and j == 2:
                    tile_done(l, sec, i, j)
                    nc.scalar.activation(rows[:, :], psum[j][0:ROWS, 0:T], ACT.Copy).then_inc(
                        *b[f"bank_free{j}"].one())
                    return
                m = sec.n * i + (first_tile + j)
                tile_done(l, sec, i, j)
                nc.scalar.activation(xp[:, m, 3:3 + SEQ], psum[j][:, 0:SEQ], ACT.Copy)
                nc.scalar.activation(
                    xp[:, m, 3 + SEQ:XW].rearrange("p (s t) -> p s t", s=DEC_BATCH)[:, :, 3:],
                    psum[j][:, SEQ:T].rearrange("p (s t) -> p s t", s=DEC_BATCH), ACT.Copy).then_inc(
                    *b[f"bank_free{j}"].one())
            return evacuate

        def wait_copies():
            for q in range(4):
                act.wait_ge(*b[f"bank_free{q}"].now())

        def rows_and_tokens():
            nc.scalar.activation(rt[:, :], rows[:, :], ACT.Sigmoid).then_inc(*step.one())
            nc.scalar.activation(proj[:, HF:HF + 4, :], proj[:, HF:HF + 4, :], ACT.Sigmoid).then_inc(*step.one())
            act.wait_ge(*step.now())
            act.wait_ge(*b["row_x"].next())
            nc.scalar.activation(re[:, :], rx[:, :], ACT.Abs).then_inc(*step.one())
            act.wait_ge(*step.now())
            nc.scalar.activation(re[:, :], re[:, :], ACT.Exp, scale=-1.0).then_inc(*step.one())
            nc.scalar.activation(lb[0:ROWS, 30:31], vec[0:ROWS, V_RA:V_RA + 1], ACT.Exp).then_inc(*b["row_e"].one())
            act.wait_ge(*b["bound_d"].next())
            nc.scalar.activation(lb[:, 4:12], lb[:, 4:12], ACT.Exp).then_inc(*b["bound_e"].one())
            act.wait_ge(*b["row_u"].next())
            nc.scalar.activation(rl[:, :], ru[:, :], ACT.Ln).then_inc(*b["row_ln"].one())
            for t, (t0, n) in enumerate(TILES3):
                act.wait_ge(*b["tok_t"].next())
                nc.scalar.activation(la_tok[0:n, t, 0:8], psum[t][0:n, 0:8], ACT.Copy)
                nc.scalar.activation(la_tok[0:n, t, 12:16], psum[t][0:n, 32:36], ACT.Copy)
                nc.scalar.activation(beta_tok[0:n, t, :], psum[t][0:n, 64:68], ACT.Copy)
                nc.scalar.activation(dt_tok[0:n, t, :], psum[t][0:n, 128:136], ACT.Copy)
                nc.scalar.activation(la_tok[0:n, t, 8:12], c_["lgam"][0:n, :], ACT.Copy).then_inc(*b["tok_copied"].one())
            act.wait_ge(*b["tok_exp"].next())
            for t, (t0, n) in enumerate(TILES3):
                nc.scalar.activation(to_end[0:n, t, :], to_end[0:n, t, :], ACT.Exp).then_inc(*step.one())
                nc.scalar.activation(ecum_tok[0:n, t, :], cum_tok[0:n, t, :], ACT.Exp).then_inc(*b["tok_ready"].one())

        def convolutions(tiles):
            if tiles[0] == 0:
                act.wait_ge(*b["conv_saved"].next())
            for m in tiles:
                act.wait_ge(*b["conv_sum"].next())
                acc = cacc[m % 2]
                bias = {"bias": vec[:, V_CB + m:V_CB + m + 1]} if m < 6 else {}
                nc.scalar.activation(xp[:, m, 0:SEQ], acc[:, 0:SEQ], ACT.Silu, **bias)
                nc.scalar.activation(xp[:, m, SEQ:T].rearrange("p (s t) -> p s t", s=NS),
                                     acc_sample(acc), ACT.Silu, **bias).then_inc(*b["conv_done"].one())

        def unit_norms():
            act.wait_ge(*b["conv_done"].now())
            for half in range(2):
                nc.scalar.activation(lsq[half], xp[:, 6 + 4 * half:10 + 4 * half, 0:T], ACT.Square).then_inc(*b["l2_sq"].one())
            act.wait_ge(*b["hg_out"].next())
            act.wait_ge(*b["l2_sum"].next())
            for e in range(4):
                nc.scalar.activation(lrt[0][:, e, :], psum[e][:, 0:T], ACT.Ln, bias=eps_c)
            act.wait_ge(*b["l2_sum"].next())
            nc.scalar.activation(lrt[1], mix[:, :, 0:T], ACT.Ln, bias=eps_c).then_inc(*step.one())
            act.wait_ge(*step.now())
            for half in range(2):
                nc.scalar.activation(lrt[half], lrt[half], ACT.Exp, scale=-0.5).then_inc(*b["l2_root"].one())

        def silus(l):
            for at in (Z, HG, RG, GZ):
                nc.scalar.activation(proj[:, at:at + 4, :], proj[:, at:at + 4, :], ACT.Silu).then_inc(*b["silus"].one())

        def hgrn(l):
            act.wait_ge(*step.now())
            nc.scalar.activation(proj[:, HQ:HQ + 4, :], proj[:, HQ:HQ + 4, :], ACT.Silu).then_inc(*b["hg_sig"].one())

        def f_norm(scale, banks, src):
            act.wait_ge(*b["f_pre"].next())
            nc.scalar.activation(f_sq.rearrange("p (k t) -> p k t", k=4), src, ACT.Square).then_inc(*b["f_sq"].one())
            act.wait_ge(*b["f_sum"].next())
            if banks == 4:
                inverse_root(f_rt.rearrange("p (k t) -> p k t", k=4), mix[:, :, 0:T], scale, b["f_root"])
            else:
                inverse_root(f_rt[:, 0:T], mix[:, 0, 0:T], scale, b["f_root"])


        def gdn_tiles():
            def copy(x, dst, src, **kw):
                act.wait_ge(*b[f"gdn_mm{x}"].next())
                nc.scalar.activation(dst, src, ACT.Copy, **kw).then_inc(*b[f"gdn_ev{x}"].one())

            act.wait_ge(*b["f_root"].now())
            for pair in PAIRS:
                for t, t0, n in pair:
                    act.wait_ge(*b["cum_bc"].next())
                    nc.scalar.activation(ecb[:, 0:4 * n], psum[0][:, 0:4 * n], ACT.Exp).then_inc(*b["ecb_ready"].one())
                    act.wait_ge(*b["dec_d"].next())
                    nc.scalar.activation(em[0:n, 0:4 * n], dm[0:n, 0:4 * n], ACT.Exp).then_inc(*b["dec_e"].one())
                    nc.scalar.activation(dm2[0:n, 0:4 * n], dm2[0:n, 0:4 * n], ACT.Exp, scale=-1.0).then_inc(
                        *b["dec_e"].one())
                    act.wait_ge(*b["scores"].next())
                    nc.scalar.activation(vtok[0:n, :], psum[3][0:n, :], ACT.Copy).then_inc(*b["v_copied"].one())
                stages = [("A", 2), None, ("B", 5), None, ("B", 4), ("A", 2)]
                if pair[0][0] < 2:
                    stages += [("B", 5)]
                    for m2 in (16, 32, 64, 128):
                        stages += [("A", 6), None] + [("A", 5)] * (m2 < 128)
                for stage in stages:
                    for x, (t, t0, n) in enumerate(pair):
                        if stage is None:
                            b[f"gdn_mm{x}"].skip()
                            continue
                        bank, to = stage
                        copy(x, SETS[x]["W"][to][0:n, 0:4 * n], SETS[x]["banks"][bank == "B"][0:n, 0:4 * n])
                for x, (t, t0, n) in enumerate(pair):
                    A, B = SETS[x]["banks"]
                    *_, wn_, nsk_ = SETS[x]["bufs"]
                    m = 4 * n
                    if t:
                        copy(x, nsk_[:, 0:m], A[:, 0:m], scale=-1.0)
                    if t < 2:
                        copy(x, wn_[0:n, :], B[0:n, :])
                    else:
                        copy(x, W[6][:, 0:m], B[:, 0:m])
                        copy(x, wn_[0:n, :], A[0:n, :])
                    act.wait_ge(*b["o_done"].next())
                    nc.scalar.activation(xp[:, 0:4, t0:t0 + n], mix[:, 0, 0:m].rearrange("p (k t) -> p k t", k=4),
                                         ACT.Copy).then_inc(*b["o_copied"].one())

        def scalar_decay(l):
            for kind, g in GROUPS:
                if kind == "gdn":
                    gdn_tiles()
                for what, t in ORDERS[kind] if kind != "gdn" else ():
                    (t0, n), (ecb, vtok, *_) = TILES3[t], buffers(kind, t % 2)
                    if what == "prepare":
                        if kind != "hg":
                            act.wait_ge(*b["cum_bc"].next())
                            nc.scalar.activation(ecb[:, 0:4 * n], psum[0][:, 0:4 * n], ACT.Exp).then_inc(*b["ecb_ready"].one())
                            act.wait_ge(*b["dec_d"].next())
                            nc.scalar.activation(em[0:n, 0:4 * n], dm[0:n, 0:4 * n], ACT.Exp).then_inc(*b["dec_e"].one())
                        act.wait_ge(*b["scores"].next())
                        w = 256 if kind == "mb" else 512
                        nc.scalar.activation(vtok[0:n, 0:w], psum[3][0:n, 0:w], ACT.Copy).then_inc(*b["v_copied"].one())
                        continue
                    act.wait_ge(*b["o_done"].next())
                    if kind == "hg":
                        nc.scalar.activation(ho[:, :, t0:t0 + n], mix[:, 0, 0:4 * n].rearrange("p (k t) -> p k t", k=4),
                                             ACT.Copy).then_inc(*b["o_copied"].one())
                        convolutions(CONV_AT[t])
                    elif kind == "mb":
                        nc.scalar.activation(f_o.rearrange("p (k t) -> p k t", k=4)[:, 2 * g:2 * g + 2, t0:t0 + n],
                                             mix[:, 0, 0:2 * n].rearrange("p (k t) -> p k t", k=2), ACT.Copy).then_inc(
                            *b["o_copied"].one())
                    else:
                        for r in range(2):
                            nc.scalar.activation(xp[:, r:4:2, t0:t0 + n],
                                                 mix[:, r, 0:2 * n].rearrange("p (k t) -> p k t", k=2),
                                                 ACT.Copy).then_inc(*b["o_copied"].one())
                if kind == "gdn":
                    b["state_new"].skip(3 * len(GROUPS))
                    act.wait_ge(*b["state_new"].now())
                    b["dma_state_out"].skip(6)
                    for dst, src in ((o["gdn_p"][l], state[GDN][:, :, :].rearrange("p h n -> p (h n)")),
                                     (o["gdn_s"][l].rearrange("p (s n) -> p s n", s=NS), st_s[:, :, :])):
                        act.dma_start(dst, src).then_inc(*b["dma_state_out"].one())
                if (kind, g) != ("mb", 0):
                    if kind == "mb":
                        f_norm(1.0 / 512, 1, f_ok)
                    else:
                        f_norm(1.0 / P, 4, ho[:, :, :] if kind == "hg" else xp[:, 0:4, 0:T])
                    if kind == "gdn":
                        act.wait_ge(*b["dma_state_out"].now())
                    if kind == "hg":
                        unit_norms()

        act.wait_ge(b["dma_in"].sem, 32)
        with b.loop(DEPTH, "layer") as l:
            for f in range(2):
                up, down = sections[f"up{f}"], sections[f"down{f}"]
                first(l, up)
                squares()
                if f == 0:
                    act.dma_start(vec[:, :], a["vec"][l]).then_inc(*b["dma_vec"].one())
                root()
                dense(l, up, gating(l, up, ACT.Silu), then=down)
                dense(l, down, with_squares(l, down, lambda i, j: (j // 3, 4 * i + j // 3) if j % 3 == 2 else None))
                if f == 0:
                    first(l, sections["proj0"])
                root(half=True)
                if f == 1:
                    continue
                squares()
                root()
                sec = sections["proj0"]
                dense(l, sec, copying(l, sec, lambda i, j: (j, proj[:, 4 * i + j, :])), then=sections["conv0"])
                sec = sections["conv0"]
                dense(l, sec, padded(l, sec, 0), then=sections["tail0"])
                sec = sections["tail0"]
                dense(l, sec, padded(l, sec, 16))
                wait_copies()
                nc.scalar.sem_inc(sems["projected"], 1)
                rows_and_tokens()
                hgrn(l)
                silus(l)
                scalar_decay(l)
                sec = sections["merge0"]
                first(l, sec)
                dense(l, sec, gating(l, sec, ACT.Sigmoid), then=sections["out0"])
                sec = sections["out0"]
                dense(l, sec, with_squares(l, sec, lambda i, j: (j, 4 * i + j)))
                root()

    @block.vector
    def _(dve):
        b = book(dve, "dve")
        step = b["v_step"]



        def inverse():
            dve.wait_ge(*b["root"].next())
            nc.vector.reciprocal(rms[:, :], rms[:, :]).then_inc(*step.one())
            dve.wait_ge(*step.now())

        def norm_in(g):
            inverse()
            for k in range(KD + 2):
                own, at = step.now()
                if k < KD:
                    nc.vector.scalar_tensor_tensor(out=tmp[:, k, :], in0=h[:, k, :],
                                                   scalar=vec[:, g * KD + k:g * KD + k + 1], in1=rms[:, :], op0=ALU.mult,
                                                   op1=ALU.mult).then_inc(*step.one())
                if 1 <= k <= KD:
                    dve.wait_ge(own, at)
                    nc.vector.tensor_copy(u_hi[:, k - 1, :], tmp[:, k - 1, :]).then_inc(*step.one())
                if k >= 2:
                    dve.wait_ge(own, at)
                    nc.vector.tensor_tensor(u_lo[:, k - 2, :], tmp[:, k - 2, :], u_hi[:, k - 2, :].bitcast(F32),
                                            ALU.subtract).then_inc(*b["u_ready"].one())

        def norm_out(g):
            inverse()
            for k in range(KD + 1):
                if k < KD:
                    nc.vector.scalar_tensor_tensor(out=tmp[:, k, :], in0=y[:, k, :], scalar=vec[:, g * KD + k:g * KD + k + 1],
                                                   in1=rms[:, :], op0=ALU.mult, op1=ALU.mult).then_inc(*step.one())
                if k:
                    own, at = step.now()
                    dve.wait_ge(own, at - (k < KD))
                    nc.vector.tensor_tensor(h[:, k - 1, :], h[:, k - 1, :], tmp[:, k - 1, :], ALU.add).then_inc(
                        *b["h_ready"].one())
            dve.wait_ge(*b["h_ready"].now())

        def gated(l, sec, i, j):
            q = sec.banks[j]
            dve.wait_ge(*b[f"bank_free{q - 1}"].next())
            dve.wait_ge(sems["tiles_done"], done(l, sec, i, j))
            nc.vector.tensor_tensor(hid_t[q // 2][:, :], gate_s[q // 2][:, :], psum[q][:, 0:T],
                                    ALU.mult).then_inc(*b[f"bank_free{q}"].one())
            dve.wait_ge(*b[f"bank_free{q}"].now())
            return hid_t[q // 2][:, :]

        def hidden(l, f):
            sec = sections[f"up{f}"]
            with b.passing(sec), b.loop(sec.trips, sec.tag) as i:
                for m in range(2):
                    t = gated(l, sec, i, 2 * m + 1)
                    nc.vector.tensor_copy(hid_hi[:, 2 * i + m, :], t).then_inc(*step.one())
                    dve.wait_ge(*step.now())
                    nc.vector.tensor_tensor(hid_lo[:, 2 * i + m, :], t, hid_hi[:, 2 * i + m, :].bitcast(F32),
                                            ALU.subtract).then_inc(*b["hid_ready"].one())
            with b.passing(sections[f"down{f}"]):
                pass


        def rows_and_tokens():
            V = nc.vector
            V.tensor_scalar(rx[:, :], rows[:, :], vec[0:ROWS, V_RB:V_RB + 1], None, ALU.add).then_inc(*b["row_x"].one())
            V.tensor_tensor(lb[:, 0:4], vec[:, V_LB:V_LB + 4], vec[:, V_LB + 4:V_LB + 8], ALU.max).then_inc(*step.one())
            dve.wait_ge(*step.now())
            for x in range(2):
                V.tensor_tensor(lb[:, 4 + 4 * x:8 + 4 * x], vec[:, V_LB + 4 * x:V_LB + 4 * x + 4], lb[:, 0:4],
                                ALU.subtract).then_inc(*(step if x == 0 else b["bound_d"]).one())
            rotate(l)
            dve.wait_ge(*b["row_e"].next())
            V.tensor_scalar(ru[:, :], re[:, :], 1.0, None, ALU.add).then_inc(*b["row_u"].one())
            fix, inv = cacc[0][0:ROWS, 0:T], cacc[1][0:ROWS, 0:T]
            dve.wait_ge(*b["row_u"].now())
            V.tensor_scalar(fix, ru[:, :], -1.0, None, ALU.add).then_inc(*step.one())
            V.reciprocal(inv, ru[:, :]).then_inc(*step.one())
            V.tensor_scalar(rx[:, :], rx[:, :], 0.0, None, ALU.max).then_inc(*step.one())
            dve.wait_ge(*step.now())
            V.tensor_tensor(fix, fix, re[:, :], ALU.subtract).then_inc(*step.one())
            dve.wait_ge(*step.now())
            V.tensor_tensor(fix, fix, inv, ALU.mult).then_inc(*step.one())
            dve.wait_ge(*b["row_ln"].next())
            V.tensor_tensor(rl[:, :], rl[:, :], rx[:, :], ALU.add).then_inc(*step.one())
            dve.wait_ge(*step.now())
            V.tensor_tensor(rl[:, :], rl[:, :], fix, ALU.subtract).then_inc(*step.one())
            dve.wait_ge(*step.now())
            V.tensor_scalar(rb[0:64, :], rl[0:64, :], lb[0:64, 30:31], -1.0, ALU.mult, ALU.mult)
            V.tensor_copy(rb[64:ROWS, :], rt[64:ROWS, :]).then_inc(*b["rows_ready"].one())
            dve.wait_ge(*b["bound_e"].next())
            V.tensor_tensor(lb[:, 12:16], lb[:, 4:8], lb[:, 8:12], ALU.add).then_inc(*step.one())
            dve.wait_ge(*step.now())
            V.reciprocal(lb[:, 12:16], lb[:, 12:16]).then_inc(*step.one())
            dve.wait_ge(*step.now())
            V.tensor_tensor(lb[:, 16:20], lb[:, 4:8], lb[:, 12:16], ALU.mult)
            V.tensor_tensor(lb[:, 20:24], lb[:, 8:12], lb[:, 12:16], ALU.mult).then_inc(*step.one())
            dve.wait_ge(*step.now())
            V.tensor_tensor(lb[:, 24:28], lb[:, 16:20], lb[:, 20:24], ALU.add).then_inc(*step.one())
            dve.wait_ge(*step.now())
            V.tensor_tensor(lb[:, 24:28], lb[:, 24:28], lb[:, 16:20], ALU.subtract).then_inc(*step.one())
            dve.wait_ge(*step.now())
            V.tensor_scalar(lb[:, 24:28], lb[:, 24:28], vec[:, V_ON:V_ON + 1], None, ALU.mult).then_inc(*step.one())
            dve.wait_ge(*step.now())
            V.tensor_scalar(lb[:, 20:24], lb[:, 24:28], -1.0, 1.0, ALU.mult, ALU.add).then_inc(*step.one())
            for t, (t0, n) in enumerate(TILES3):
                dve.wait_ge(*b["tok_sums"].next())
                V.tensor_copy(cum_tok[0:n, t, :], psum[t][0:n, 0:16]).then_inc(*step.one())
            dve.wait_ge(*step.now())
            for t, (t0, n) in enumerate(TILES3):
                V.tensor_tensor(to_end[0:n, t, :], psum[t][0:n, 16:32], cum_tok[0:n, t, :], ALU.subtract).then_inc(
                    *(step if t < 2 else b["tok_exp"]).one())
            for t, (t0, n) in enumerate(TILES3):
                dve.wait_ge(*b["tok_ready"].next())
                V.tensor_tensor(to_end_dt[0:n, t, :], to_end[0:n, t, 0:8], dt_tok[0:n, t, :], ALU.mult)
                V.tensor_tensor(beta_cum[0:n, t, :], ecum_tok[0:n, t, 12:16], beta_tok[0:n, t, :], ALU.mult).then_inc(*step.one())

        def convolutions(tiles):
            if tiles[0] == 0:
                dve.wait_ge(*b["conv_filled"].next())
            n = XW - 3
            for m in tiles[::2]:
                for j in range(4):
                    for e in range(2):
                        tap = vec[:, V_CW + 4 * (m + e) + j:V_CW + 4 * (m + e) + j + 1]
                        src, acc = xp[:, m + e, j:j + n], cacc[e][:, 0:n]
                        if j == 0:
                            if m:
                                dve.wait_ge(*b["conv_done"].next())
                            nc.vector.tensor_scalar(acc, src, tap, None, ALU.mult).then_inc(*step.one())
                            continue
                        own, at = step.now()
                        dve.wait_ge(own, at - ((j, e) != (3, 1)))
                        nc.vector.scalar_tensor_tensor(out=acc, in0=src, scalar=tap, in1=acc, op0=ALU.mult,
                                                       op1=ALU.add).then_inc(*(step if j < 3 else b["conv_sum"]).one())
            if tiles[-1] == NCONV - 1:
                b["conv_done"].skip(2)

        def unit_norms():
            for half in range(2):
                dve.wait_ge(*b["l2_root"].next())
                x = xp[:, 6 + 4 * half:10 + 4 * half, 0:T]
                if half:
                    nc.vector.tensor_tensor(x, x, lrt[1], ALU.mult).then_inc(*b["l2_done"].one())
                else:
                    nc.vector.scalar_tensor_tensor(out=x, in0=x, scalar=P ** -0.5, in1=lrt[0], op0=ALU.mult,
                                                   op1=ALU.mult).then_inc(*b["l2_done"].one())

        def hgrn(l):
            V = nc.vector
            dve.wait_ge(*b["hg_sig"].next())
            dve.wait_ge(*b["dma_conv_out"].next())
            for k in range(4):
                V.tensor_scalar(hf1[:, k * T:(k + 1) * T], proj[:, HF + k, :], lb[:, 20 + k:21 + k], lb[:, 24 + k:25 + k],
                                ALU.mult, ALU.add).then_inc(*step.one())
            dve.wait_ge(*step.now())
            f1 = hf1[:, :].rearrange("p (k t) -> p k t", k=4)
            V.tensor_scalar(proj[:, HF:HF + 4, :], f1, -1.0, 1.0, ALU.mult, ALU.add).then_inc(*b["hg_q"].one())
            fades = f1
            for level, s in enumerate((0, 1, 2, 4, 8, 16, 32, 64)):
                dve.wait_ge(*b["hg_sc"].next())
                dve.wait_ge(*b["hg_q"].now())
                if s == 0:
                    V.tensor_tensor(proj[:, HQ:HQ + 4, :], proj[:, HQ:HQ + 4, :], f1, ALU.mult).then_inc(*b["hg_q"].one())
                else:
                    width = T if s < 8 else SEQ
                    nb = width // (2 * s)
                    pairs = fades.rearrange("p k (c two) -> p k c two", two=2)

                    def halves(at, which):
                        return proj[:, at:at + 4, 0:width].rearrange("p k (c two t) -> p k c two t", two=2, t=s)[:, :, :, which]

                    for at, which in ((HQ, 1), (HF, 0)):
                        x = halves(at, which)
                        V.tensor_tensor(x, x, over(pairs[:, :, :, 1 - which:2 - which], [P, 4, nb, s]), ALU.mult).then_inc(
                            *step.one())
                    if s == 4:
                        new = hf8[:, :, :]
                    elif s == 64:
                        new = hf128[:, :, :]
                    else:
                        new = (hf2 if level % 2 else hf1)[:, 0:4 * nb].rearrange("p (k c) -> p k c", k=4)
                    V.tensor_tensor(new, pairs[:, :, :, 0], pairs[:, :, :, 1], ALU.mult).then_inc(*b["hg_q"].one())
                    fades = hf8[:, :, 0:SEQ // 8] if s == 4 else new
                mask = c_["ident"] if s == 0 else c_[f"next{2 * s}"]
                parts = [(mix[:, 2 * (level % 2):2 * (level % 2) + 2, :].rearrange("p t (k i) -> p (t k) i", i=P), P, 0, 8)]
                if s < 8:
                    parts.append((psum[level % 2][0:64, 0:256].rearrange("p (k i) -> p k i", i=64), 64, 1024, 4))
                dve.wait_ge(*step.now())
                for src, n, c0, count in parts:
                    dst = (ht if level else hp)[0:n, c0:c0 + count * n].rearrange("p (k i) -> p k i", i=n)
                    V.tensor_tensor(dst, src, over(mask[0:n, 0:n].unsqueeze(1), [n, count, n]), ALU.mult).then_inc(*step.one())
                if level:
                    dve.wait_ge(*step.now())
                    for _, n, c0, count in parts:
                        sl = slice(c0, c0 + count * n)
                        V.tensor_tensor(hp[0:n, sl], hp[0:n, sl], ht[0:n, sl], ALU.add).then_inc(
                            *(b["hg_ready"] if s == 64 else step).one())
            dve.wait_ge(*b["hg_ready"].now())

        def rotate(l):
            dve.wait_ge(*b["rot_ps"].next())
            turned = ho[:, :, :]
            x = proj[:, RQ:RQ + 4, :]
            nc.vector.tensor_tensor(turned, mix[:, :, 0:T], over(c_["sin"].unsqueeze(1), [P, 4, T]), ALU.mult)
            nc.vector.tensor_tensor(x, x, over(c_["cos"].unsqueeze(1), [P, 4, T]), ALU.mult).then_inc(*step.one())
            dve.wait_ge(*step.now())
            nc.vector.tensor_tensor(x, x, turned, ALU.add).then_inc(*step.one())
            dve.wait_ge(*step.now())
            nc.vector.tensor_scalar(proj[:, RK:RK + 2, :], proj[:, RK:RK + 2, :], 64 ** -0.5, None, ALU.mult).then_inc(
                *b["rotated"].one())

        def by_head(x, n):
            return x.rearrange("p (k i) -> p k i", i=n)

        def odd_even(x, n, r):
            return x.rearrange("p (k r i) -> p r k i", r=2, i=n)[:, r]

        def heads_of(x, i, n):
            return by_head(SETS[x]["W"][i][0:n, 0:4 * n], n)

        def coupling(x, t, n):
            W_, V = SETS[x]["W"], nc.vector
            dve.wait_ge(*b["dec_e"].next())
            for k in range(4):
                V.scalar_tensor_tensor(out=W_[0][0:n, k * n:(k + 1) * n], in0=psum[2][0:n, k * n:(k + 1) * n],
                                       scalar=beta_tok[0:n, t, k:k + 1], in1=dm2[0:n, k * n:(k + 1) * n], op0=ALU.mult,
                                       op1=ALU.mult).then_inc(*(step if t < 2 or k < 3 else b[f"gdn_v{x}"]).one())
            if t < 2:
                dve.wait_ge(*step.now())
                V.tensor_tensor(heads_of(x, 1, n), heads_of(x, 0, n), over(c_["b8"].unsqueeze(1), [n, 4, n]), ALU.mult).then_inc(
                    *b[f"gdn_v{x}"].one())

        def delta_rule(pair):
            V = nc.vector
            n = pair[0][2]
            m = 4 * n
            xs = range(len(pair))
            eye = over(c_["ident"][0:n, 0:n].unsqueeze(1), [n, 4, n])
            for x in xs:
                dve.wait_ge(*b[f"gdn_ev{x}"].next())
                V.tensor_tensor(heads_of(x, 3, n), eye, heads_of(x, 2, n), ALU.subtract).then_inc(*step.one())
            for x in xs:
                b[f"gdn_mm{x}"].skip()
                dve.wait_ge(*b[f"gdn_mm{x}"].next())
                V.tensor_copy(SETS[x]["W"][4][0:n, 0:m], SETS[x]["banks"][0][0:n, 0:m]).then_inc(*b[f"gdn_v{x}"].one())
            for x in xs:
                dve.wait_ge(*b[f"gdn_ev{x}"].next())
                V.tensor_tensor(heads_of(x, 6, n), eye, heads_of(x, 5, n), ALU.add).then_inc(*step.one())
            for x in xs:
                b[f"gdn_mm{x}"].skip()
                dve.wait_ge(*b[f"gdn_mm{x}"].next())
                V.tensor_tensor(heads_of(x, 1, n), eye, by_head(SETS[x]["banks"][0][0:n, 0:m], n), ALU.add).then_inc(
                    *b[f"gdn_v{x}"].one())
                b[f"gdn_mm{x}"].skip(2)
                b[f"gdn_ev{x}"].skip(2)
            if pair[0][0] < 2:
                for x in xs:
                    b[f"gdn_mm{x}"].skip()
                    b[f"gdn_ev{x}"].skip()
                for m2 in (16, 32, 64, 128):
                    for x in xs:
                        dve.wait_ge(*b[f"gdn_mm{x}"].now())
                        V.tensor_tensor(heads_of(x, 1, n), heads_of(x, 0, n), over(c_[f"b{m2}"].unsqueeze(1), [n, 4, n]),
                                        ALU.mult).then_inc(*b[f"gdn_v{x}"].one())
                    for x in xs:
                        b[f"gdn_mm{x}"].skip()
                        b[f"gdn_ev{x}"].skip()
                        dve.wait_ge(*b[f"gdn_mm{x}"].next())
                        tt = SETS[x]["W"][2][0:n, 0:m]
                        V.tensor_tensor(tt, tt, SETS[x]["banks"][1][0:n, 0:m], ALU.subtract).then_inc(*b[f"gdn_v{x}"].one())
                        if m2 < 128:
                            b[f"gdn_mm{x}"].skip()
                            b[f"gdn_ev{x}"].skip()
            for x, (t, _, _) in enumerate(pair):
                b[f"gdn_mm{x}"].skip(1 + (t > 0) + (t == 2))
                b[f"gdn_ev{x}"].skip(1 + (t > 0) + (t == 2))

        def new_state(kind, g, t, n, x):
            V = nc.vector
            ecb, vtok, *_ = buffers(kind, x)
            at = {"hg": 0, "mb": 0, "ret": 256, "gdn": 0}[kind]
            width = 64 if kind == "mb" else P
            own = {"hg": HGRN, "mb": MB, "ret": RET, "gdn": GDN}[kind]

            def place(k):
                if kind == "mb":
                    return slice(64 * g, 64 * g + 64), k
                if kind == "ret":
                    return slice(64 * (k % 2), 64 * (k % 2) + 64), k // 2
                return slice(0, P), k

            if t < 2:
                dve.wait_ge(*b["state_mm"].next())
                for k in range(4):
                    pr, pos = place(k)
                    dst, src = state[own][pr, pos, :], mix[pr, 3, pos * width:(pos + 1) * width]
                    if t == 0:
                        up = V.tensor_copy(dst, src)
                    else:
                        whole = hf128[:, k, 1:2] if kind == "hg" else ecb[pr, k * n + n - 1:k * n + n]
                        up = V.scalar_tensor_tensor(out=dst, in0=dst, scalar=whole, in1=src,
                                                    op0=ALU.mult, op1=ALU.add)
                    up.then_inc(*(step if k < 3 else b["state_new"]).one())
                return

            def masked(k):
                src = vtok
                V.tensor_tensor(vm[k % 2][:, 0:NS * width].rearrange("p (s d) -> p s d", s=NS),
                                over(src[0:n, k * width:(k + 1) * width].unsqueeze(1), [n, NS, width]),
                                over(c_["pick"][0:n, :].unsqueeze(2), [n, NS, width]), ALU.mult).then_inc(
                    *b["vm_ready"].one())

            dve.wait_ge(*b["o_done"].now())
            masked(0)
            masked(1)
            for k in range(4):
                pr, pos = place(k)
                dst = st_s[pr, :, at + pos * width:at + (pos + 1) * width]
                rows_ = pr.stop - pr.start
                if kind == "hg":
                    whole = hf8[:, k, SEQ // 8:].unsqueeze(2)
                else:
                    whole = ecb[pr, k * n:(k + 1) * n].rearrange("p (s t) -> p s t", t=C)[:, :, C - 1:C]
                V.tensor_tensor(dst, dst, over(whole, [rows_, NS, width]), ALU.mult).then_inc(*step.one())
                dve.wait_ge(*b["state_mm"].next())
                dve.wait_ge(*step.now())
                bank = 2 if k % 2 == 0 else 0
                kvs = mix[pr, bank:bank + NS * width // 512, :].rearrange("p b f -> p (b f)").rearrange("p (s d) -> p s d", s=NS)
                V.tensor_tensor(dst, dst, kvs, ALU.add).then_inc(*(step if k < 3 else b["state_new"]).one())
                if k < 2:
                    masked(k + 2)
                if kind == "hg" and k < 3:
                    convolutions(CONV_AT[2][2 * k:2 * k + 2])

        def scalar_decay(l):
            V = nc.vector
            for kind, g in GROUPS:
                col = {"hg": 0, "mb": 4 * g, "ret": RET, "gdn": GDN}[kind]
                b["dma_state"].skip({("mb", 0): 2, ("hg", 0): 1, ("gdn", 0): 1}.get((kind, g), 0))

                for what, t in ORDERS[kind]:
                    if what == "invert":
                        delta_rule(PAIRS[t])
                        continue
                    (t0, n), x = TILES3[t], t % 2
                    m = 4 * n
                    ecb, vtok, pm, qd, kend = buffers(kind, x)
                    _, _, _, kb, vb, _, _ = SETS[x]["bufs"]
                    v_in = PLAIN[0]["v"]
                    if (what, kind) == ("prepare", "hg"):
                        dve.wait_ge(*b["scores"].next())
                        V.tensor_copy(kend[0:n, :], mix[0:n, 2, :]).then_inc(*b["k_ready"].one())
                        if t == 1:
                            convolutions(CONV_AT[0])
                        b["v_copied"].skip()
                        continue
                    if what == "prepare":
                        dve.wait_ge(*b["ecb_ready"].next())
                        neg, pos = (c_["neg"], c_["pos"]) if t < 2 else (c_["neg_s"][0:n, :], c_["pos_s"][0:n, :])
                        for k in range(4):
                            cum = cum_tok[0:n, t, col + k:col + k + 1]
                            src, sl = psum[0][0:n, k * n:(k + 1) * n], slice(k * n, (k + 1) * n)
                            last = V.scalar_tensor_tensor(out=dm[0:n, sl], in0=src, scalar=cum, in1=neg, op0=ALU.subtract,
                                                          op1=ALU.add)
                            if kind == "gdn":
                                last = V.scalar_tensor_tensor(out=dm2[0:n, sl], in0=src, scalar=cum, in1=pos,
                                                              op0=ALU.subtract, op1=ALU.add)
                        last.then_inc(*b["dec_d"].one())
                        dve.wait_ge(*b["scores"].next())
                        dve.wait_ge(*b["dec_e"].next())
                        if kind == "mb":
                            for k in range(4):
                                V.scalar_tensor_tensor(out=pm[0:n, k * n:(k + 1) * n], in0=psum[1][0:n, 0:n],
                                                       scalar=dt_tok[0:n, t, col + k:col + k + 1],
                                                       in1=em[0:n, k * n:(k + 1) * n], op0=ALU.mult, op1=ALU.mult).then_inc(
                                    *(step if k < 3 else b["p_ready"]).one())
                        elif kind == "ret":
                            for r in range(2):
                                V.tensor_tensor(odd_even(pm[0:n, 0:m], n, r), by_head(psum[1 + r][0:n, 0:2 * n], n),
                                                odd_even(em[0:n, 0:m], n, r), ALU.mult).then_inc(
                                    *(step if r == 0 else b["p_ready"]).one())
                        else:
                            V.tensor_tensor(pm[0:n, 0:m], psum[1][0:n, 0:m], em[0:n, 0:m], ALU.mult).then_inc(*b["p_ready"].one())
                        if t:
                            if kind == "mb":
                                pr = slice(64 * g, 64 * g + 64)
                                V.tensor_tensor(by_head(qd[pr, 0:m], n), over(xp[pr, 5, t0:t0 + n].unsqueeze(1), [64, 4, n]),
                                                by_head(ecb[pr, 0:m], n), ALU.mult).then_inc(*b["q_ready"].one())
                            elif kind == "ret":
                                for r in range(2):
                                    pr = slice(64 * r, 64 * r + 64)
                                    V.tensor_tensor(odd_even(qd[pr, 0:m], n, r), proj[pr, RQ:RQ + 2, t0:t0 + n],
                                                    odd_even(ecb[pr, 0:m], n, r), ALU.mult).then_inc(
                                        *(step if r == 0 else b["q_ready"]).one())
                            else:
                                V.tensor_tensor(by_head(qd[:, 0:m], n), xp[:, 6:10, t0:t0 + n], by_head(ecb[:, 0:m], n),
                                                ALU.mult).then_inc(*b["q_ready"].one())
                        if kind == "mb":
                            V.tensor_tensor(by_head(kend[0:n, 0:256], 64), over(mix[0:n, 2, 64 * g:64 * g + 64].unsqueeze(1), [n, 4, 64]),
                                            over(to_end_dt[0:n, t, col:col + 4].unsqueeze(2), [n, 4, 64]), ALU.mult).then_inc(
                                *b["k_ready"].one())
                        elif kind == "ret":
                            V.tensor_tensor(by_head(kend[0:n, 0:256], 64), by_head(mix[0:n, 2, 0:256], 64),
                                            over(to_end[0:n, t, RET:RET + 4].unsqueeze(2), [n, 4, 64]), ALU.mult).then_inc(
                                *b["k_ready"].one())
                        else:
                            keys = by_head(mix[0:n, 2, :], P)
                            V.tensor_tensor(by_head(kend[0:n, :], P), keys, over(to_end[0:n, t, GDN:GDN + 4].unsqueeze(2), [n, 4, P]),
                                            ALU.mult)
                            V.tensor_tensor(by_head(kb[0:n, :], P), keys, over(beta_cum[0:n, t, :].unsqueeze(2), [n, 4, P]),
                                            ALU.mult).then_inc(*b["k_ready"].one())
                            dve.wait_ge(*b["v_copied"].now())
                        b["v_copied"].skip()
                        if kind == "gdn":
                            dve.wait_ge(*b["v_copied"].now())
                            V.tensor_tensor(by_head(vb[0:n, :], P), by_head(v_in[0:n, :], P),
                                            over(beta_tok[0:n, t, :].unsqueeze(2), [n, 4, P]), ALU.mult).then_inc(*step.one())
                            coupling(x, t, n)
                        continue
                    b["o_done"].skip()
                    if (kind, t) == ("hg", 2):
                        convolutions(CONV_AT[1])
                    if t == 2:
                        dve.wait_ge(*b["v_copied"].now())
                        dve.wait_ge(*b["dma_state"].now())
                    new_state(kind, g, t, n, x)
                    b["o_copied"].skip(2 if kind == "ret" else 1)
                if (kind, g) == ("mb", 0):
                    continue
                dve.wait_ge(*b["o_copied"].now())
                if kind == "mb":
                    for k in range(4):
                        V.scalar_tensor_tensor(out=f_ok[:, k], in0=xp[:, k, 0:T], scalar=vec[:, V_D + k:V_D + k + 1],
                                               in1=f_ok[:, k], op0=ALU.mult, op1=ALU.add).then_inc(*step.one())
                    dve.wait_ge(*step.now())
                    V.tensor_tensor(f_ok, f_ok, proj[:, Z:Z + 4, :], ALU.mult).then_inc(*b["f_pre"].one())
                    dve.wait_ge(*b["f_root"].next())

                    for k in range(4):
                        V.scalar_tensor_tensor(out=proj[:, Z + k, :], in0=f_ok[:, k], scalar=vec[:, V_MN + k:V_MN + k + 1],
                                               in1=f_rt[:, 0:T], op0=ALU.mult, op1=ALU.mult).then_inc(*step.one())
                    continue
                dve.wait_ge(*b["state_new"].now())
                V.sem_inc(sems["f_pre"], 1)
                b["f_pre"].skip()
                dve.wait_ge(*b["f_root"].next())

                out = ho[:, :, :] if kind == "hg" else xp[:, 0:4, 0:T]
                gate = {"hg": HG, "ret": RG, "gdn": GZ}[kind]
                root = f_rt.rearrange("p (k t) -> p k t", k=4)
                if kind == "ret":
                    V.tensor_tensor(root, out, root, ALU.mult).then_inc(*step.one())
                else:
                    V.scalar_tensor_tensor(out=root, in0=out, scalar=vec[:, V_HN:V_HN + 1] if kind == "hg" else
                                           vec[:, V_GN:V_GN + 1], in1=root, op0=ALU.mult,
                                           op1=ALU.mult).then_inc(*step.one())
                    if kind == "gdn":
                        b["dma_state_out"].skip(8)
                        dve.wait_ge(*b["dma_state_out"].now())
                    else:
                        b["silus"].skip(4)
                        dve.wait_ge(*b["silus"].now())
                dve.wait_ge(*step.now())
                V.tensor_tensor(proj[:, gate:gate + 4, :], proj[:, gate:gate + 4, :], root, ALU.mult).then_inc(
                    *{"hg": b["hg_out"], "ret": step, "gdn": b["y_ready"]}[kind].one())
                if kind == "hg":
                    unit_norms()

        b["h_ready"].skip(KD)
        dve.wait_ge(b["dma_in"].sem, 32)
        with b.loop(DEPTH, "layer") as l:
            dve.wait_ge(*b["dma_vec"].next())
            norm_in(0)
            hidden(l, 0)
            norm_out(1)
            norm_in(2)
            for sec in ("proj0", "conv0", "tail0"):
                with b.passing(sections[sec]):
                    pass
            dve.wait_ge(*b["projected"].next())
            rows_and_tokens()
            hgrn(l)
            scalar_decay(l)
            sec = sections["merge0"]
            with b.passing(sec), b.loop(KD, sec.tag) as i:
                for n in range(4):
                    t = gated(l, sec, i, 2 * n + 1)
                    if n == 1:
                        nc.vector.tensor_tensor(tmp[:, 0, :], hid_t[0][:, :], t, ALU.add).then_inc(*step.one())
                    elif n > 1:
                        nc.vector.tensor_tensor(tmp[:, 0, :], tmp[:, 0, :], t, ALU.add).then_inc(*step.one())
                    if n:
                        dve.wait_ge(*step.now())
                nc.vector.tensor_copy(m_hi[:, i, :], tmp[:, 0, :]).then_inc(*step.one())
                dve.wait_ge(*step.now())
                nc.vector.tensor_tensor(m_lo[:, i, :], tmp[:, 0, :], m_hi[:, i, :].bitcast(F32),
                                        ALU.subtract).then_inc(*b["merged"].one())
            with b.passing(sections["out0"]):
                pass
            norm_out(3)
            norm_in(4)
            hidden(l, 1)
            norm_out(5)


    @block.tensor
    def _(pe):
        b = book(pe, "pe")

        def split_product(j, sec, x_hi, x_lo, k0=0, first=True, last=True, ready=None):
            _, nk, _, r, s = sec.loads[j]
            nk = KD if (sec.name, j) == ("tail", 2) else nk
            bank = sec.banks[j if sec.name != "down" else j // 3]
            if first:
                pe.wait_ge(*b[f"bank_free{bank}"].now())
                b[f"bank_free{bank}"].skip()
            pe.wait_ge(*b[f"lo_ready{r}"].next())
            rows_out = ROWS if (sec.name, j) == ("tail", 2) else P
            out = psum[bank][0:rows_out, 0:T]
            for k in range(nk):
                if ready is not None:
                    pe.wait_ge(ready.sem, ready.at() - (KD - 1 - k))
                lhs_hi, lhs_lo = (w[s][:, k * rows_out:(k + 1) * rows_out] for w in (w_hi, w_lo))
                nc.tensor.matmul(out, lhs_hi, x_hi(k0 + k), start=(first and k == 0), stop=False)
                nc.tensor.matmul(out, lhs_hi, x_lo(k0 + k), start=False, stop=False)
                mm = nc.tensor.matmul(out, lhs_lo, x_hi(k0 + k), start=False, stop=(last and k == nk - 1))
            mm.then_inc(sems["tiles_done"], 1)

        u = (lambda k: u_hi[:, k, :]), (lambda k: u_lo[:, k, :])
        hid = (lambda k: hid_hi[:, k, :]), (lambda k: hid_lo[:, k, :])
        mrg = (lambda k: m_hi[:, k, :]), (lambda k: m_lo[:, k, :])

        def feature_sum(of_y=False):
            for k in range(KD):
                if not of_y:
                    pe.wait_ge(*b["squares"].next())
                elif k >= 4:
                    pe.wait_ge(*b[f"bank_free{k % 4}"].now())
                mm = nc.tensor.matmul(mix[:, 0, 0:T], ones, tmp[:, k, :], start=k == 0, stop=k == KD - 1)
            mm.then_inc(*b["norm_sum"].one())

        def products(tag, x, ready):
            sec = sections[tag]
            with b.passing(sec), b.loop(sec.trips, sec.tag):
                for j in range(sec.n):
                    split_product(j, sec, *x, ready=b[ready] if j == 0 else None)

        def wait_u():
            b["u_ready"].skip(KD)

        def mlp(l, f):
            feature_sum()
            wait_u()
            products(f"up{f}", u, "u_ready")
            b["hid_ready"].skip(KF)
            sec = sections[f"down{f}"]
            with b.passing(sec), b.loop(sec.trips, sec.tag):
                pe.wait_ge(*b["hid_ready"].now())
                for j in range(sec.n):
                    q = j % 3
                    split_product(j, sec, *hid, k0=sum(DOWN_K[:q]), first=q == 0, last=q == 2)
            feature_sum(of_y=True)


        def passed(narrow=True):
            if narrow:
                nc.tensor.sem_inc(sems["t_step"], 1)

        def row_transposes():
            pe.wait_ge(*b["projected"].next())
            for k in range(4):
                mm = nc.tensor.matmul(mix[:, k, 0:T], c_["rot"], proj[:, RQ + k, :], start=True, stop=True)
            mm.then_inc(*b["rot_ps"].one())
            b["rotated"].skip()
            pe.wait_ge(*b["rows_ready"].next())
            for t, (t0, n) in enumerate(TILES3):
                nc.tensor.transpose(psum[t][0:n, 0:ROWS], rb[:, t0:t0 + n], c_["ident"][0:ROWS, 0:ROWS])
                nc.tensor.transpose(psum[t][0:n, 128:136], rl[0:8, t0:t0 + n], c_["ident"][0:8, 0:8]).then_inc(
                    *b["tok_t"].one())
            for t, (t0, n) in enumerate(TILES3):
                pe.wait_ge(*b["tok_copied"].next())
                passed(t == 2)
                whole = ones[0:n, 0:n] if t < 2 else c_["same_s"][0:n, :]
                nc.tensor.matmul(psum[t][0:n, 0:16], tri_of(t), la_tok[0:n, t, :], start=True, stop=True)
                nc.tensor.matmul(psum[t][0:n, 16:32], whole, la_tok[0:n, t, :], start=True, stop=True).then_inc(
                    *b["tok_sums"].one())

        def unit_norms():
            for half in range(2):
                pe.wait_ge(*b["l2_sq"].next())
                for e in range(4):
                    out = mix[:, e, 0:T] if half else psum[e][:, 0:T]
                    mm = nc.tensor.matmul(out, ones, lsq[half][:, e, :], start=True, stop=True)
                mm.then_inc(*b["l2_sum"].one())

        def head_sums(src):
            pe.wait_ge(*b["f_sq"].next())
            for k in range(4):
                mm = nc.tensor.matmul(mix[:, k, 0:T], ones, src[:, k * T:(k + 1) * T], start=True, stop=True)
            mm.then_inc(*b["f_sum"].one())

        def hgrn(l):
            for level, s in enumerate((0, 1, 2, 4, 8, 16, 32, 64)):
                pe.wait_ge(*b["hg_q"].next())
                for t, (t0, n) in enumerate(TILES3[:3 if s < 8 else 2]):
                    out = mix[:, 2 * (level % 2) + t, :] if t < 2 else psum[level % 2][0:64, 0:256]
                    for k in range(4):
                        mm = nc.tensor.matmul(out[:, k * n:(k + 1) * n], proj[:, HF + k, t0:t0 + n],
                                              proj[:, HQ + k, t0:t0 + n], start=True, stop=True)
                mm.then_inc(*b["hg_sc"].one())
            b["hg_q"].skip()
            pe.wait_ge(*b["hg_ready"].next())

        def evacuated(x):
            pe.wait_ge(*b[f"gdn_ev{x}"].next())

        def from_vector(x):
            pe.wait_ge(*b[f"gdn_v{x}"].next())

        def delta_rule(pair):
            n = pair[0][2]
            m, xs, whole = 4 * n, range(len(pair)), pair[0][0] < 2

            def heads(x, bank, lhs, rhs):
                passed(n == 64)
                W_ = SETS[x]["W"]
                for k in range(4):
                    sl = slice(k * n, (k + 1) * n)
                    mm = nc.tensor.matmul(SETS[x]["banks"][bank][0:n, sl], W_[lhs][0:n, sl], W_[rhs][0:n, sl], start=True,
                                          stop=True)
                mm.then_inc(*b[f"gdn_mm{x}"].one())

            def transposes(x, bank, src):
                passed(n == 64)
                for k in range(4):
                    sl = slice(k * n, (k + 1) * n)
                    mm = nc.tensor.transpose(SETS[x]["banks"][bank][0:n, sl], SETS[x]["W"][src][0:n, sl], c_["ident"][0:n, 0:n])
                mm.then_inc(*b[f"gdn_mm{x}"].one())

            X = 1 if whole else 0
            for x in xs:
                transposes(x, 0, X)
            for x in xs:
                evacuated(x)
                heads(x, 0, 2, X)
                heads(x, 1, X, 2)
            for x in xs:
                from_vector(x)
                evacuated(x)
                heads(x, 0, 5, 4)
            for x in xs:
                from_vector(x)
                heads(x, 1, 6, 1)
            for x in xs:
                evacuated(x)
                heads(x, 0, 4, 3)
            for x in xs:
                evacuated(x)
                if whole:
                    transposes(x, 1, 2)
            if whole:
                for m2 in (16, 32, 64, 128):
                    for x in xs:
                        from_vector(x)
                        evacuated(x)
                        heads(x, 0, 1, 2)
                    for x in xs:
                        evacuated(x)
                        heads(x, 1, 5, 6)
                    for x in xs:
                        from_vector(x)
                        if m2 < 128:
                            transposes(x, 0, 2)

        def new_values(x, t, n):
            W_, (A, B) = SETS[x]["W"], SETS[x]["banks"]
            _, _, _, kb, vb, _, nsk = SETS[x]["bufs"]
            if t:
                passed()
                for k in range(4):
                    mm = nc.tensor.matmul(A[:, k * n:(k + 1) * n], kb[0:n, k * P:(k + 1) * P],
                                          W_[2][0:n, k * n:(k + 1) * n], start=True, stop=True)
                mm.then_inc(*b[f"gdn_mm{x}"].one())
                evacuated(x)
            if t < 2:
                for k in range(4):
                    out = B[0:n, k * P:(k + 1) * P]
                    mm = nc.tensor.matmul(out, W_[2][0:n, k * n:(k + 1) * n], vb[0:n, k * P:(k + 1) * P], start=True,
                                          stop=t == 0)
                    if t:
                        mm = nc.tensor.matmul(out, nsk[:, k * n:(k + 1) * n], state[GDN][:, k, :], start=False, stop=True)
                mm.then_inc(*b[f"gdn_mm{x}"].one())
            else:
                passed()
                for k in range(4):
                    nc.tensor.matmul(B[:, k * n:(k + 1) * n], vb[0:n, k * P:(k + 1) * P],
                                     W_[2][0:n, k * n:(k + 1) * n], start=True, stop=False)
                    for s in range(NS):
                        at = k * n + C * s
                        mm = nc.tensor.matmul(B[:, at:at + C], st_s[:, s, k * P:(k + 1) * P], nsk[:, at:at + C],
                                              start=False, stop=s == NS - 1)
                mm.then_inc(*b[f"gdn_mm{x}"].one())
                evacuated(x)
                passed()
                for k in range(4):
                    mm = nc.tensor.transpose(A[0:n, k * P:(k + 1) * P], W_[6][:, k * n:(k + 1) * n], c_["ident"])
                mm.then_inc(*b[f"gdn_mm{x}"].one())
            evacuated(x)

        def outputs(kind, g, t, t0, n, x):
            _, vals, pm, qd, _ = buffers(kind, x)
            width = 64 if kind == "mb" else P

            def place(k):
                if kind == "mb":
                    return mix[64 * (k % 2):64 * (k % 2) + 64, 0, (k // 2) * n:(k // 2 + 1) * n]
                if kind == "ret":
                    return mix[:, k % 2, (k // 2) * n:(k // 2 + 1) * n]
                return mix[:, 0, k * n:(k + 1) * n]

            def state_of(k, s):
                at = k // 2 if kind == "ret" else k
                pr = {"mb": slice(64 * g, 64 * g + 64), "ret": slice(64 * (k % 2), 64 * (k % 2) + 64)}.get(
                          kind, slice(0, P))
                if s is None:
                    own = {"hg": HGRN, "mb": MB, "ret": RET, "gdn": GDN}[kind]
                    return state[own][pr, at, :], pr
                c0 = 256 if kind == "ret" else 0
                return st_s[pr, s, c0 + at * width:c0 + (at + 1) * width], pr

            def query(k, at, count):
                if kind == "hg":
                    return proj[:, HQ + k, t0 + at:t0 + at + count]
                return qd[state_of(k, None)[1], k * n + at:k * n + at + count]

            def inside(k, start):
                weights = hp[0:n, 512 * t + k * n:512 * t + (k + 1) * n] if kind == "hg" else pm[0:n, k * n:(k + 1) * n]
                return nc.tensor.matmul(place(k), vals[0:n, k * width:(k + 1) * width], weights,
                                        start=start, stop=t == 0)

            def before(k):
                if t == 1:
                    st, pr = state_of(k, None)
                    return nc.tensor.matmul(place(k), st, query(k, 0, n), start=False, stop=True)
                for s in range(NS):
                    st, pr = state_of(k, s)
                    mm = nc.tensor.matmul(place(k)[:, C * s:C * s + C], st, query(k, C * s, C),
                                          start=False, stop=s == NS - 1)
                return mm

            if t == 2 and kind in ("mb", "ret"):
                for k in range(4):
                    inside(k, True).then_inc(*b["o_part"].one())
                    pe.wait_ge(*b["o_part"].now())
                    passed()
                    mm = before(k)
            else:
                for k in range(4):
                    mm = inside(k, True)
                    if t:
                        mm = before(k)
            mm.then_inc(*b["o_done"].one())

        def states(kind, g, t, n, x):
            _, vals, _, _, kend = buffers(kind, x)
            width = 64 if kind == "mb" else P
            key = P if kind in ("hg", "gdn") else 64
            passed()
            for k in range(4):
                pr = {"mb": slice(64 * g, 64 * g + 64), "ret": slice(64 * (k % 2), 64 * (k % 2) + 64)}.get(
                          kind, slice(0, P))
                at = k // 2 if kind == "ret" else k
                keys = kend[0:n, k * key:(k + 1) * key]
                if t < 2:
                    mm = nc.tensor.matmul(mix[pr, 3, at * width:(at + 1) * width], keys, vals[0:n, k * width:(k + 1) * width],
                                          start=True, stop=True)
                    continue
                pe.wait_ge(*b["vm_ready"].next())
                if k == 1:
                    pe.wait_ge(*b["o_copied"].now())
                passed()
                bank = 2 if k % 2 == 0 else 0
                for half in range(NS * width // 512):
                    mm = nc.tensor.matmul(mix[pr, bank + half, :], keys, vm[k % 2][:, 512 * half:512 * half + 512],
                                          start=True, stop=True)
                mm.then_inc(*b["state_mm"].one())
            if t < 2:
                mm.then_inc(*b["state_mm"].one())

        def scalar_decay(l):
            for kind, g in GROUPS:
                col = {"hg": 0, "mb": 4 * g, "ret": RET, "gdn": GDN}[kind]
                b["dma_state"].skip({("mb", 0): 2, ("hg", 0): 1, ("gdn", 0): 1}.get((kind, g), 0))

                pr = slice(64 * g, 64 * g + 64)
                seen_at = {}
                for what, t in ORDERS[kind]:
                    if what == "invert":
                        delta_rule(PAIRS[t])
                        continue
                    (t0, n), x = TILES3[t], t % 2
                    if what == "prepare":
                        pe.wait_ge(*b["state_new"].now())
                        pe.wait_ge(*b["o_copied"].now())
                        for name in ("p_ready", "k_ready", "v_copied"):
                            pe.wait_ge(*b[name].now())
                        passed(t == 2)
                        if kind != "hg":
                            for k in range(4):
                                mm = nc.tensor.matmul(psum[0][:, k * n:(k + 1) * n],
                                                      la_tok[0:n, t, col + k:col + k + 1].to_broadcast([n, P]),
                                                      tri_of(t)[0:n, 0:n], start=True, stop=True)
                            mm.then_inc(*b["cum_bc"].one())
                            pe.wait_ge(*b["rotated"].now())
                            passed(t == 2)
                        if kind == "hg":
                            turns = [(bank, e, proj[:, at + e, t0:t0 + n]) for bank, at in ((psum[3], HI), (mix[:, 2], HF))
                                     for e in range(4)]
                        elif kind == "mb":
                            nc.tensor.matmul(psum[1][0:n, 0:n], xp[pr, 4, t0:t0 + n], xp[pr, 5, t0:t0 + n], start=True, stop=True)
                            turns = [(psum[3], e, xp[:, 2 * g + e, t0:t0 + n]) for e in range(2)]
                            turns.append((mix[:, 2], 0, xp[:, 4, t0:t0 + n]))
                        elif kind == "ret":
                            for k in range(4):
                                r = slice(64 * (k % 2), 64 * (k % 2) + 64)
                                nc.tensor.matmul(psum[1 + k % 2][0:n, (k // 2) * n:(k // 2 + 1) * n], proj[r, RK + k // 2, t0:t0 + n],
                                                 proj[r, RQ + k // 2, t0:t0 + n], start=True, stop=True)
                            turns = [(psum[3], e, proj[:, RV + e, t0:t0 + n]) for e in range(4)]
                            turns += [(mix[:, 2], e, proj[:, RK + e, t0:t0 + n]) for e in range(2)]
                        else:
                            for k in range(4):
                                for bank, other in ((1, 6), (2, 10)):
                                    nc.tensor.matmul(psum[bank][0:n, k * n:(k + 1) * n], xp[:, 10 + k, t0:t0 + n],
                                                     xp[:, other + k, t0:t0 + n], start=True, stop=True)
                            turns = [(psum[3], e, xp[:, 14 + e, t0:t0 + n]) for e in range(4)]
                            turns += [(mix[:, 2], e, xp[:, 10 + e, t0:t0 + n]) for e in range(4)]
                        for bank, e, src in turns:
                            mm = nc.tensor.transpose(bank[0:n, e * P:(e + 1) * P], src, c_["ident"])
                        mm.then_inc(*b["scores"].one())
                        if kind != "hg":
                            b["p_ready"].skip()
                        b["k_ready"].skip()
                        b["v_copied"].skip()
                        seen_at[t] = {name: b[name].n for name in ("p_ready", "k_ready", "v_copied")}
                        if kind == "gdn":
                            from_vector(x)
                            passed()
                        continue
                    if t == 2:
                        pe.wait_ge(*b["dma_state"].now())
                    pe.wait_ge(*b["state_new"].now())
                    if kind == "gdn":
                        new_values(x, t, n)
                    pe.wait_ge(*b["o_copied"].now())
                    for name, n_then in seen_at[t].items():
                        pe.wait_ge(b[name].sem, b[name].at() - (b[name].n - n_then))
                    if t and kind != "hg":
                        pe.wait_ge(*b["q_ready"].next())
                    passed(t == 2 or kind == "mb")
                    outputs(kind, g, t, t0, n, x)
                    b["o_copied"].skip(2 if kind == "ret" else 1)
                    states(kind, g, t, n, x)
                    b["state_new"].skip()
                if (kind, g) == ("mb", 0):
                    continue
                pe.wait_ge(*b["f_pre"].next())
                if kind == "mb":
                    pe.wait_ge(*b["f_sq"].next())
                    for k in range(4):
                        mm = nc.tensor.matmul(mix[:, 0, 0:T], ones, f_sq[:, k * T:(k + 1) * T], start=k == 0, stop=k == 3)
                    mm.then_inc(*b["f_sum"].one())
                else:
                    head_sums(f_sq)
                pe.wait_ge(*b["f_root"].next())
                passed()
                if kind == "hg":
                    unit_norms()
                    b["l2_done"].skip(2)
                    pe.wait_ge(*b["l2_done"].now())

        for name in START:
            nc.tensor.sem_inc(sems[name], unit_of(name))
        nc.tensor.sem_inc(sems["h_ready"], KD)
        nc.tensor.sem_inc(sems["tiles_done"], AHEAD)
        pe.wait_ge(b["dma_in"].sem, 32)
        with b.loop(DEPTH, "layer") as l:
            mlp(l, 0)
            feature_sum()
            wait_u()
            for tag in ("proj0", "conv0", "tail0"):
                products(tag, u, "u_ready")
            row_transposes()
            hgrn(l)
            scalar_decay(l)
            b["y_ready"].skip()
            sec = sections["merge0"]
            with b.passing(sec), b.loop(KD, sec.tag):
                pe.wait_ge(*b["y_ready"].now())
                for n, base in enumerate((Z, HG, RG, GZ)):
                    split_product(2 * n, sec, *u)
                    b[f"dma_w{sec.loads[2 * n][3]}"].skip()
                    r, q = sec.loads[2 * n + 1][3], sec.banks[2 * n + 1]
                    pe.wait_ge(*b[f"bank_free{q}"].now())
                    b[f"bank_free{q}"].skip()
                    pe.wait_ge(*b[f"dma_w{r}"].next())
                    for k in range(KB):
                        mm = nc.tensor.matmul(psum[q][:, 0:T], raw[r][:, k * P:(k + 1) * P],
                                              proj[:, base + k, :], start=k == 0, stop=k == KB - 1)
                    mm.then_inc(sems["tiles_done"], 1)
            b["merged"].skip(KD)
            products("out0", mrg, "merged")
            feature_sum(of_y=True)
            mlp(l, 1)


def constants():
    c = {}
    i, j = np.arange(P)[:, None], np.arange(P)[None, :]
    BIG = 1e30
    c["ones"], c["ident"] = np.ones((P, P)), np.eye(P)
    c["tri"] = (i <= j)
    c["neg"] = np.where(i <= j, 0, -BIG)
    c["pos"] = np.where(i > j, 0, BIG)
    seq = i // C == j // C
    half = lambda m: m[:, :64] * np.where(np.arange(P)[:, None] < 64, 1, 0)
    c["tri_s"], c["same_s"] = half((i <= j) & seq), half(seq)
    c["neg_s"] = np.where((i <= j) & seq, 0, -BIG)[:, :64]
    c["pos_s"] = np.where((i > j) & seq, 0, BIG)[:, :64]
    rot = np.zeros((P, P))
    for p in range(P):
        rot[p + 32 if p % 64 < 32 else p - 32, p] = -1 if p % 64 < 32 else 1
    c["rot"] = rot
    steps = np.arange(32, dtype=np.float32) * np.float32(1 / 31)
    inv = (1.0 / np.power(10000.0, steps.astype(np.float64))).astype(np.float32)
    pos = np.concatenate([np.arange(SEQ), np.tile(PAST_LEN + np.arange(DEC_SEQ), DEC_BATCH)]).astype(np.float32)
    ang = (pos[None, :] * np.tile(inv, 4)[:, None]).astype(np.float32).astype(np.float64)
    c["cos"], c["sin"] = np.cos(ang), np.sin(ang)
    c["b8"] = (i > j) & (i // 8 == j // 8)
    for m in (16, 32, 64, 128):
        c[f"b{m}"] = (i // m == j // m) & (i % m >= m // 2) & (j % m < m // 2)
    for m in (2, 4, 8, 16, 32, 64, 128):
        c[f"next{m}"] = (i // m == j // m) & (i % m < m // 2) & (j % m >= m // 2)
    c["lgam"] = np.broadcast_to(np.log((1.0 - np.exp2(-5.0 - np.arange(4))).astype(np.float32)), (P, 4))
    c["pick"] = (i // C == np.arange(8)[None, :])
    c["eps"], c["eps4"] = np.full((P, 1), EPS), np.full((P, 1), 4 * EPS)
    return np.concatenate([np.asarray(c[k], np.float32) for k in CONST], axis=1)


OUTS = {"x": (P, KD, T), "st_conv": (DEPTH, P, NCONV, NS + 1, 3), "mb_p": (DEPTH, P, 256), "ret_p": (DEPTH, P, 256),
        "gdn_p": (DEPTH, P, 512), "hg_p": (DEPTH, P, 512), "mb_s": (DEPTH, P, NS * 256), "ret_s": (DEPTH, P, NS * 256),
        "gdn_s": (DEPTH, P, NS * 512), "hg_s": (DEPTH, P, NS * 512)}


def results(r):
    tok = r["x"].transpose(1, 0, 2).reshape(D_MODEL, T).T
    cv = r["st_conv"].transpose(0, 3, 4, 2, 1).reshape(DEPTH, NS + 1, 3, NCONV * P)
    mb = lambda x, n: x.reshape(DEPTH, 2, 64, n, 4, 64).transpose(0, 3, 1, 4, 2, 5).reshape(DEPTH, n, 8, 64, 64)
    ret = lambda x, n: x.reshape(DEPTH, 2, 64, n, 2, P).transpose(0, 3, 4, 1, 2, 5).reshape(DEPTH, n, 4, 64, P)
    gd = lambda x, n: x.reshape(DEPTH, P, n, 4, P).transpose(0, 2, 3, 1, 4)
    got = (tok[:SEQ].reshape(1, SEQ, D_MODEL), tok[SEQ:].reshape(DEC_BATCH, DEC_SEQ, D_MODEL),
           mb(r["mb_p"], 1), cv[:, :1, :, :768], gd(r["hg_p"], 1), ret(r["ret_p"], 1), gd(r["gdn_p"], 1), cv[:, :1, :, 768:],
           mb(r["mb_s"], NS), cv[:, 1:, :, :768], gd(r["hg_s"], NS), ret(r["ret_s"], NS), gd(r["gdn_s"], NS), cv[:, 1:, :, 768:])
    return tuple(np.ascontiguousarray(x) for x in got)


def layouts(x):
    A = {k: np.asarray(v) for k, v in x.items()}
    out = {}
    tok = np.concatenate([A["x_prompt"].reshape(SEQ, D_MODEL), A["x_sample"].reshape(-1, D_MODEL)])
    out["x"] = tok.T.reshape(KD, P, T).transpose(1, 0, 2)
    out["w_up"] = A["ffn_w_in"].reshape(DEPTH, 2, KD, P, 2, KF, P).transpose(0, 1, 5, 4, 3, 2, 6).reshape(DEPTH, 2, KF, 2, P, KD * P)
    out["w_down"] = A["ffn_w_out"].reshape(DEPTH, 2, KF, P, KD, P).transpose(0, 1, 4, 3, 2, 5).reshape(DEPTH, 2, KD, P, KF * P)
    w = A["w_in"]
    s = np.cumsum([0, 512, 768, 8, 512, 512, 512, 512, 256, 256, 512, 512, 1536, 512, 4, 4, 4096])
    seg = [w[:, :, s[i]:s[i + 1]] for i in range(16)]
    z, xbc, dt, hq, hf, hi, hg, rq, rk, rv, rg, qkv, gz, ga, gb, gates = seg
    cols = np.concatenate([z, hq, hf, hi, hg, rq, rk, rv, rg, gz, xbc, qkv], axis=2)
    out["w_proj"] = cols.reshape(DEPTH, KD, P, NPLAIN + NCONV, P).transpose(0, 3, 2, 1, 4).reshape(DEPTH, NPLAIN + NCONV, P, KD * P)
    small = np.zeros((DEPTH, D_MODEL, ROWS), np.float32)
    small[:, :, 0:8], small[:, :, 32:36], small[:, :, 64:68] = dt, ga, gb
    out["w_rows"] = small.reshape(DEPTH, KD, P, ROWS).transpose(0, 2, 1, 3).reshape(DEPTH, P, KD * ROWS)
    out["w_gate"] = gates.reshape(DEPTH, KD, P, 4, KD, P).transpose(0, 4, 3, 2, 1, 5).reshape(DEPTH, KD, 4, P, KD * P)
    out["w_branch"] = A["w_branch"].reshape(DEPTH, 4, KB, P, KD, P).transpose(0, 4, 1, 3, 2, 5).reshape(DEPTH, KD, 4, P, KB * P)
    out["w_out"] = A["w_out"].reshape(DEPTH, KD, P, KD, P).transpose(0, 3, 2, 1, 4).reshape(DEPTH, KD, P, KD * P)
    v = np.zeros((DEPTH, P, NV), np.float32)

    def put(at, rows):
        v[:, :, at:at + rows.shape[1]] = rows.transpose(0, 2, 1)

    put(V_G, A["norm_g"].reshape(DEPTH, 48, P))
    cw = np.concatenate([A["mb_conv_w"], A["gdn_conv_w"]], axis=2).reshape(DEPTH, 4, NCONV, P)
    put(V_CW, cw.transpose(0, 2, 1, 3).reshape(DEPTH, 72, P))
    put(V_CB, A["mb_conv_b"].reshape(DEPTH, 6, P))
    put(V_D, np.repeat(A["mb_d"], 64, axis=1).reshape(DEPTH, 4, P))
    put(V_MN, A["mb_norm"].reshape(DEPTH, 4, P))
    put(V_LB, np.broadcast_to(A["hg_lb_logits"].reshape(1, 8, P), (DEPTH, 8, P)))
    put(V_HN, A["hg_norm"].reshape(DEPTH, 1, P))
    put(V_GN, A["gdn_norm"].reshape(DEPTH, 1, P))
    v[:, 0:8, V_RB], v[:, 32:36, V_RB] = A["mb_dt_bias"], A["gdn_dt_bias"]
    v[:, 0:8, V_RA], v[:, 32:36, V_RA] = A["mb_a_log"], A["gdn_a_log"]
    v[1:, :, V_ON] = 1.0
    out["vec"] = v
    out["const"] = constants()
    cv = np.concatenate([A["state_ssm_conv"], A["state_gdn_conv"]], axis=3)
    out["st_conv"] = cv.reshape(DEPTH, NS, 3, NCONV, P).transpose(0, 4, 3, 1, 2).reshape(DEPTH, P, NCONV * NS * 3)
    out["st_mb"] = A["state_ssm"].reshape(DEPTH, NS, 2, 4, 64, 64).transpose(0, 2, 4, 1, 3, 5).reshape(DEPTH, P, NS * 256)
    out["st_ret"] = A["state_ret"].reshape(DEPTH, NS, 2, 2, 64, P).transpose(0, 3, 4, 1, 2, 5).reshape(DEPTH, P, NS * 256)
    out["st_gdn"] = A["state_gdn"].transpose(0, 3, 1, 2, 4).reshape(DEPTH, P, NS * 512)
    out["st_hg"] = A["state_hgrn"].transpose(0, 3, 1, 2, 4).reshape(DEPTH, P, NS * 512)
    return {k: np.ascontiguousarray(v) for k, v in out.items()}


def kernel(**inputs):
    import concourse.bacc as _bacc
    from concourse import mybir as _mybir
    from concourse.bass_utils import run_bass_kernel_spmd as _run

    arrays = {f"in_{k}": v for k, v in layouts(inputs).items()}

    def program(per_body):
        nc = _bacc.Bacc("TRN2", target_bir_lowering=False, num_devices=1)
        a = {k[3:]: nc.dram_tensor(k, v.shape, _mybir.dt.from_np(v.dtype), kind="ExternalInput").ap()
             for k, v in arrays.items()}
        o = {k: nc.dram_tensor(f"out_{k}", shape, F32, kind="ExternalOutput").ap() for k, shape in OUTS.items()}
        found = {}
        build(nc, a, o, per_body, found)
        return nc, found

    nc, _ = program(program({})[1])
    r = _run(nc, [arrays], core_ids=[0])
    return results({k: r.results[0][f"out_{k}"] for k in OUTS})
```
